# Optimizing a Trainium2 kernel written in Bass

```python
import math
import jax
import jax.numpy as jnp
from jax import lax
import numpy as np

D_MODEL = 1024
BATCH = 1
SEQ = 1024
DEPTH = 2
DEC_BATCH = 8
DEC_SEQ = 1
PAST_LEN = 4096
PAGE_SIZE = 128

N_EVEN = (DEPTH + 1) // 2
N_ODD = DEPTH // 2

A_HEADS = 4
A_DK = 128
A_DV = 128
A_QK = A_HEADS * A_DK
A_WIDTH = A_HEADS * A_DV
A_CONV_CH = 2 * A_QK + A_WIDTH
CONV_W = 4
DELTA_CHUNK = 64

B_HEADS = 8
B_KV = 2
B_HPG = B_HEADS // B_KV
B_DH = 64
B_WIDTH = B_HEADS * B_DH
N_BRANCH = 3
B_KV_COLS = N_BRANCH * 2 * B_KV * B_DH
CMP_BLK = 32
SEL_BLK = 64
SEL_TOPK = 16
WINDOW = 512
SEL_QBLK = 64
WIN_QBLK = 128
B_SCALE = B_DH ** -0.5

EVEN_SIZES = (A_CONV_CH, A_HEADS, A_HEADS, A_WIDTH, B_WIDTH, B_KV_COLS, B_HEADS * N_BRANCH)
EVEN_IN = A_CONV_CH + 2 * A_HEADS + A_WIDTH + B_WIDTH + B_KV_COLS + B_HEADS * N_BRANCH

C_HEADS = 4
C_DK = 128
C_DV = 256
C_QK = C_HEADS * C_DK
C_WIDTH = C_HEADS * C_DV
C_LOWRANK = 16
GLA_TAU = 16.0
GLA_CHUNK = 16
ODD_SIZES = (C_QK, C_QK, C_WIDTH, C_LOWRANK, C_WIDTH)
ODD_IN = 2 * C_QK + 2 * C_WIDTH + C_LOWRANK

D_FF = -(-(8 * D_MODEL) // (3 * 256)) * 256

ALPHA = (2 * DEPTH) ** 0.25
BETA = (8 * DEPTH) ** -0.25
NEG = -1e30
FORCE = 1e9

kernel_name = 'hybrid_deltanet_nsa_gla_deepnorm_step'

f32 = jnp.float32

def split_cols(h, sizes):
    out, s = [], 0
    for n in sizes:
        out.append(h[..., s:s + n])
        s += n
    return out

def layer_norm(x, g, b, eps=1e-5):
    xf = x.astype(f32)
    mu = jnp.mean(xf, -1, keepdims=True)
    var = jnp.mean(jnp.square(xf - mu), -1, keepdims=True)
    return ((xf - mu) * lax.rsqrt(var + eps) * g.astype(f32) + b.astype(f32)).astype(x.dtype)

def rms_norm(x, g, eps=1e-6):
    xf = x.astype(f32)
    return xf * lax.rsqrt(jnp.mean(xf * xf, -1, keepdims=True) + eps) * g.astype(f32)

def l2_normalize(x, eps=1e-6):
    xf = x.astype(f32)
    return xf * lax.rsqrt(jnp.sum(xf * xf, -1, keepdims=True) + eps)

def masked_softmax(s, mask):
    p = jax.nn.softmax(jnp.where(mask, s, NEG), axis=-1)
    return jnp.where(mask, p, 0.0)

def causal_conv(x, buf, w):
    T = x.shape[1]
    xp = jnp.concatenate([buf, x], axis=1)
    y = xp[:, 0:T] * w[0]
    for j in range(1, CONV_W):
        y = y + xp[:, j:j + T] * w[j]
    return y, xp[:, -(CONV_W - 1):]

def to_chunks(a, C, pad):
    a = jnp.pad(a.astype(f32), [(0, 0), (0, pad)] + [(0, 0)] * (a.ndim - 2))
    B_, Tp = a.shape[:2]
    a = a.reshape((B_, Tp // C, C) + a.shape[2:])
    return jnp.moveaxis(a, 3, 1)

def from_chunks(o, T):
    N, B_, H, C, D = o.shape
    return jnp.transpose(o, (1, 0, 3, 2, 4)).reshape(B_, N * C, H, D)[:, :T]

def gated_delta_chunked(q, k, v, g, beta, S0):
    B_, T, H, _ = q.shape
    C = min(DELTA_CHUNK, T)
    pad = (-T) % C
    q, k, v, g, beta = [to_chunks(a, C, pad) for a in (q, k, v, g, beta)]
    q = q * (A_DK ** -0.5)
    gam = jnp.cumsum(g, axis=-1)
    causal = jnp.tril(jnp.ones((C, C), bool))
    strict = jnp.tril(jnp.ones((C, C), bool), -1)
    diff = gam[..., :, None] - gam[..., None, :]
    Ldec = jnp.where(causal, jnp.exp(jnp.where(causal, diff, 0.0)), 0.0)
    kb = k * beta[..., None]
    A = jnp.where(strict, jnp.einsum('bhncd,bhnsd->bhncs', kb, k) * Ldec, 0.0)
    eye = jnp.eye(C, dtype=f32)
    Tm = lax.linalg.triangular_solve(eye + A, jnp.broadcast_to(eye, A.shape), left_side=True, lower=True)
    u = jnp.einsum('bhncs,bhnse->bhnce', Tm, v * beta[..., None])
    w = jnp.einsum('bhncs,bhnsd->bhncd', Tm, kb * jnp.exp(gam)[..., None])
    qk = jnp.einsum('bhncd,bhnsd->bhncs', q, k) * Ldec
    qg = q * jnp.exp(gam)[..., None]
    kdec = k * jnp.exp(gam[..., -1:] - gam)[..., None]
    glast = jnp.exp(gam[..., -1])

    def step(S, xs):
        u_c, w_c, qk_c, qg_c, kd_c, gl_c = xs
        v_new = u_c - jnp.einsum('bhcd,bhde->bhce', w_c, S)
        o = jnp.einsum('bhcd,bhde->bhce', qg_c, S) + jnp.einsum('bhcs,bhse->bhce', qk_c, v_new)
        S = S * gl_c[..., None, None] + jnp.einsum('bhcd,bhce->bhde', kd_c, v_new)
        return S, o

    xs = tuple(jnp.moveaxis(a, 2, 0) for a in (u, w, qk, qg, kdec, glast))
    S, o = lax.scan(step, S0.astype(f32), xs)
    return from_chunks(o, T), S

def gla_chunked(q, k, v, log_a, S0):
    B_, T, H, _ = q.shape
    C = min(GLA_CHUNK, T)
    pad = (-T) % C
    q, k, v, la = [to_chunks(a, C, pad) for a in (q, k, v, log_a)]
    q = q * (C_DK ** -0.5)
    b = jnp.cumsum(la, axis=3)
    qt = q * jnp.exp(b)
    kt = k * jnp.exp(-b)
    causal = jnp.tril(jnp.ones((C, C), bool))
    att = jnp.where(causal, jnp.einsum('bhncd,bhnsd->bhncs', qt, kt), 0.0)
    intra = jnp.einsum('bhncs,bhnse->bhnce', att, v)
    kdec = k * jnp.exp(b[..., -1:, :] - b)
    glast = jnp.exp(b[..., -1, :])

    def step(S, xs):
        qt_c, kd_c, v_c, in_c, gl_c = xs
        o = jnp.einsum('bhcd,bhde->bhce', qt_c, S) + in_c
        S = S * gl_c[..., None] + jnp.einsum('bhcd,bhce->bhde', kd_c, v_c)
        return S, o

    xs = tuple(jnp.moveaxis(a, 2, 0) for a in (qt, kdec, v, intra, glast))
    S, o = lax.scan(step, S0.astype(f32), xs)
    return from_chunks(o, T), S

def nsa_compressed(q, qpos, kc, vc):
    B_, Tq = q.shape[:2]
    Tk = kc.shape[1]
    nc = Tk // CMP_BLK
    kcb = jnp.mean(kc[:, :nc * CMP_BLK].reshape(B_, nc, CMP_BLK, B_KV, B_DH), axis=2)
    vcb = jnp.mean(vc[:, :nc * CMP_BLK].reshape(B_, nc, CMP_BLK, B_KV, B_DH), axis=2)
    qg = q.reshape(B_, Tq, B_KV, B_HPG, B_DH)
    s = jnp.einsum('bqghd,bcgd->bghqc', qg, kcb) * B_SCALE
    mask = (jnp.arange(nc)[None, :] + 1) * CMP_BLK <= qpos[:, None] + 1
    p = masked_softmax(s, mask)
    o = jnp.einsum('bghqc,bcgd->bqghd', p, vcb).reshape(B_, Tq, B_HEADS, B_DH)
    return o, jnp.sum(p, axis=2)

def nsa_select_blocks(imp, qpos, Tk):
    B_, G, Tq, nc = imp.shape
    ns = -(-Tk // SEL_BLK)
    r = SEL_BLK // CMP_BLK
    imp = jnp.pad(imp, ((0, 0), (0, 0), (0, 0), (0, ns * r - nc)))
    imp = jnp.sum(imp.reshape(B_, G, Tq, ns, r), axis=-1)
    blk = jnp.arange(ns)[None, :]
    cur = (qpos // SEL_BLK)[:, None]
    valid = blk * SEL_BLK <= qpos[:, None]
    forced = (blk == 0) | (blk == cur) | (blk == cur - 1)
    score = jnp.where(forced, FORCE, jnp.where(valid, imp, NEG))
    _, idx = lax.top_k(score, min(SEL_TOPK, ns))
    return idx

def nsa_selected(q, qpos, ks, vs, idx):
    B_, Tk = ks.shape[:2]
    Tq = q.shape[1]
    ns = -(-Tk // SEL_BLK)
    padk = ns * SEL_BLK - Tk
    kb = jnp.pad(ks, ((0, 0), (0, padk), (0, 0), (0, 0))).reshape(B_, ns, SEL_BLK, B_KV, B_DH).transpose(0, 3, 1, 2, 4)
    vb = jnp.pad(vs, ((0, 0), (0, padk), (0, 0), (0, 0))).reshape(B_, ns, SEL_BLK, B_KV, B_DH).transpose(0, 3, 1, 2, 4)
    qb = SEL_QBLK if Tq % SEL_QBLK == 0 else Tq
    gather = jax.vmap(jax.vmap(lambda tbl, i: tbl[i]))

    def block(i):
        s0 = i * qb
        qi = lax.dynamic_slice_in_dim(q, s0, qb, 1).reshape(B_, qb, B_KV, B_HPG, B_DH)
        pi = lax.dynamic_slice_in_dim(qpos, s0, qb, 0)
        ii = lax.dynamic_slice_in_dim(idx, s0, qb, 2)
        kg = gather(kb, ii)
        vg = gather(vb, ii)
        nk = ii.shape[-1] * SEL_BLK
        s = jnp.einsum('bqghd,bgqksd->bghqks', qi, kg) * B_SCALE
        s = s.reshape(B_, B_KV, B_HPG, qb, nk)
        kpos = ii[..., None] * SEL_BLK + jnp.arange(SEL_BLK)
        mask = (kpos <= pi[None, None, :, None, None]).reshape(B_, B_KV, 1, qb, nk)
        p = masked_softmax(s, mask)
        o = jnp.einsum('bghqn,bgqnd->bqghd', p, vg.reshape(B_, B_KV, qb, nk, B_DH))
        return o.reshape(B_, qb, B_HEADS, B_DH)

    out = lax.map(block, jnp.arange(Tq // qb))
    return jnp.moveaxis(out, 0, 1).reshape(B_, Tq, B_HEADS, B_DH)

def window_attend(q, qpos, k, v, kpos):
    B_, Q = q.shape[:2]
    qg = q.reshape(B_, Q, B_KV, B_HPG, B_DH)
    s = jnp.einsum('bqghd,bkgd->bghqk', qg, k) * B_SCALE
    d = qpos[:, None] - kpos[None, :]
    mask = (d >= 0) & (d < WINDOW) & (kpos[None, :] >= 0)
    p = masked_softmax(s, mask)
    return jnp.einsum('bghqk,bkgd->bqghd', p, v).reshape(B_, Q, B_HEADS, B_DH)

def nsa_window_prompt(q, kw, vw):
    B_, T = q.shape[:2]
    qb = WIN_QBLK if T % WIN_QBLK == 0 else T
    span = WINDOW + qb
    kp = jnp.pad(kw, ((0, 0), (WINDOW, 0), (0, 0), (0, 0)))
    vp = jnp.pad(vw, ((0, 0), (WINDOW, 0), (0, 0), (0, 0)))

    def block(i):
        s0 = i * qb
        qi = lax.dynamic_slice_in_dim(q, s0, qb, 1)
        ki = lax.dynamic_slice_in_dim(kp, s0, span, 1)
        vi = lax.dynamic_slice_in_dim(vp, s0, span, 1)
        return window_attend(qi, s0 + jnp.arange(qb), ki, vi, s0 - WINDOW + jnp.arange(span))

    out = lax.map(block, jnp.arange(T // qb))
    return jnp.moveaxis(out, 0, 1).reshape(B_, T, B_HEADS, B_DH)

def nsa_mixer(q, kv_new, gates, hist, win_buf, pos0):
    B_, T = q.shape[:2]
    q = q.astype(f32)
    kv_new = kv_new.astype(f32)
    rows = kv_new[:, :, :2].reshape(B_, T, 4, B_KV, B_DH)
    full = rows if hist is None else jnp.concatenate([hist.astype(f32), rows], axis=1)
    Tk = full.shape[1]
    qpos = pos0 + jnp.arange(T)
    o_cmp, imp = nsa_compressed(q, qpos, full[:, :, 0], full[:, :, 1])
    idx = nsa_select_blocks(imp, qpos, Tk)
    o_sel = nsa_selected(q, qpos, full[:, :, 2], full[:, :, 3], idx)
    win_new = kv_new[:, :, 2]
    if win_buf is None:
        o_win = nsa_window_prompt(q, win_new[:, :, 0], win_new[:, :, 1])
        new_buf = win_new[:, -min(WINDOW, T):]
    else:
        wb = win_buf.shape[1]
        cat = jnp.concatenate([win_buf.astype(f32), win_new], axis=1)
        kpos = pos0 - wb + jnp.arange(wb + T)
        o_win = window_attend(q, qpos, cat[:, :, 0], cat[:, :, 1], kpos)
        new_buf = cat[:, -min(WINDOW, wb + T):]
    o = gates[..., 0:1] * o_cmp + gates[..., 1:2] * o_sel + gates[..., 2:3] * o_win
    return o, rows, new_buf

def even_mixer(x, w_in, conv_w, A_log, dt_bias, dn_g, w_out, conv_buf, S0, hist, win_buf, pos0):
    B_, T, _ = x.shape
    h = x @ w_in
    qkv_a, beta_a, a_a, gate_a, q_b, kv_b, g_b = split_cols(h, EVEN_SIZES)
    conv, new_conv = causal_conv(qkv_a, conv_buf.astype(x.dtype), conv_w)
    conv = jax.nn.silu(conv.astype(f32))
    qa, ka, va = split_cols(conv, (A_QK, A_QK, A_WIDTH))
    qa = l2_normalize(qa.reshape(B_, T, A_HEADS, A_DK))
    ka = l2_normalize(ka.reshape(B_, T, A_HEADS, A_DK))
    va = va.reshape(B_, T, A_HEADS, A_DV)
    beta = jax.nn.sigmoid(beta_a.astype(f32))
    g = -jnp.exp(A_log.astype(f32)) * jax.nn.softplus(a_a.astype(f32) + dt_bias.astype(f32))
    o_a, S_new = gated_delta_chunked(qa, ka, va, g, beta, S0)
    o_a = rms_norm(o_a, dn_g) * jax.nn.silu(gate_a.astype(f32).reshape(B_, T, A_HEADS, A_DV))
    o_b, rows, new_buf = nsa_mixer(q_b.reshape(B_, T, B_HEADS, B_DH),
                                   kv_b.reshape(B_, T, N_BRANCH, 2, B_KV, B_DH),
                                   jax.nn.sigmoid(g_b.astype(f32)).reshape(B_, T, B_HEADS, N_BRANCH),
                                   hist, win_buf, pos0)
    mixed = jnp.concatenate([o_a.reshape(B_, T, A_WIDTH), o_b.reshape(B_, T, B_WIDTH)], axis=-1).astype(x.dtype)
    dt = x.dtype
    return mixed @ w_out, rows.astype(dt), new_buf.astype(dt), new_conv.astype(dt), S_new.astype(dt)

def odd_mixer(x, w_in, w_g2, b_g2, gn_g, w_out, S0):
    B_, T, _ = x.shape
    h = (x @ w_in).astype(f32)
    q, k, v, g1, r = split_cols(h, ODD_SIZES)
    log_a = jax.nn.log_sigmoid(g1 @ w_g2.astype(f32) + b_g2.astype(f32)) / GLA_TAU
    o, S_new = gla_chunked(q.reshape(B_, T, C_HEADS, C_DK), k.reshape(B_, T, C_HEADS, C_DK),
                           v.reshape(B_, T, C_HEADS, C_DV), log_a.reshape(B_, T, C_HEADS, C_DK), S0)
    o = rms_norm(o, gn_g) * jax.nn.silu(r.reshape(B_, T, C_HEADS, C_DV))
    return o.reshape(B_, T, C_WIDTH).astype(x.dtype) @ w_out, S_new.astype(x.dtype)

def swiglu(x, wg, wu, wd):
    return (jax.nn.silu(x @ wg) * (x @ wu)) @ wd

def setup_inputs(seed: int = 0) -> dict:
    key = jax.random.key(seed)
    keys = iter(jax.random.split(key, 40))

    def nrm(shape, scale):
        return jax.random.normal(next(keys), shape, jnp.float32) * scale

    n_pages = PAST_LEN // PAGE_SIZE
    used = DEC_BATCH * n_pages
    n_pool = used + max(1, used // 4)
    page_table = jax.random.permutation(next(keys), n_pool)[:used].reshape(DEC_BATCH, n_pages).astype(jnp.int32)
    w_buf = min(WINDOW, PAST_LEN)
    dt = jnp.exp(jax.random.uniform(next(keys), (N_EVEN, A_HEADS), jnp.float32, math.log(1e-3), math.log(1e-1)))
    dt_bias = dt + jnp.log(-jnp.expm1(-dt))
    a_log = jnp.log(jax.random.uniform(next(keys), (N_EVEN, A_HEADS), jnp.float32, 1.0, 16.0))
    mix_even = A_WIDTH + B_WIDTH
    return {
        'x_prompt': nrm((BATCH, SEQ, D_MODEL), 1.0),
        'x_sample': nrm((DEC_BATCH, DEC_SEQ, D_MODEL), 1.0),
        'cache_nsa_kv': nrm((n_pool, N_EVEN, PAGE_SIZE, 4, B_KV, B_DH), 1.0),
        'state_nsa_win': nrm((N_EVEN, DEC_BATCH, w_buf, 2, B_KV, B_DH), 1.0),
        'state_delta_conv': nrm((N_EVEN, DEC_BATCH, CONV_W - 1, A_CONV_CH), 1.0),
        'state_delta_S': nrm((N_EVEN, DEC_BATCH, A_HEADS, A_DK, A_DV), 0.1),
        'state_gla_S': nrm((N_ODD, DEC_BATCH, C_HEADS, C_DK, C_DV), 1.0),
        'page_table': page_table,
        'w_in_even': nrm((N_EVEN, D_MODEL, EVEN_IN), D_MODEL ** -0.5),
        'conv_w_delta': nrm((N_EVEN, CONV_W, A_CONV_CH), CONV_W ** -0.5),
        'delta_A_log': a_log,
        'delta_dt_bias': dt_bias,
        'delta_norm_g': 1.0 + nrm((N_EVEN, A_DV), 0.02),
        'w_out_even': nrm((N_EVEN, mix_even, D_MODEL), BETA * mix_even ** -0.5),
        'w_in_odd': nrm((N_ODD, D_MODEL, ODD_IN), D_MODEL ** -0.5),
        'w_gla_gate2': nrm((N_ODD, C_LOWRANK, C_QK), C_LOWRANK ** -0.5),
        'b_gla_gate2': nrm((N_ODD, C_QK), 0.02),
        'gla_norm_g': 1.0 + nrm((N_ODD, C_DV), 0.02),
        'w_out_odd': nrm((N_ODD, C_WIDTH, D_MODEL), BETA * C_WIDTH ** -0.5),
        'w_ffn_gate': nrm((DEPTH, D_MODEL, D_FF), D_MODEL ** -0.5),
        'w_ffn_up': nrm((DEPTH, D_MODEL, D_FF), BETA * D_MODEL ** -0.5),
        'w_ffn_down': nrm((DEPTH, D_FF, D_MODEL), BETA * D_FF ** -0.5),
        'ln_g': 1.0 + nrm((DEPTH, 2, D_MODEL), 0.02),
        'ln_b': nrm((DEPTH, 2, D_MODEL), 0.02),
    }

def reference(x_prompt, x_sample, cache_nsa_kv, state_nsa_win, state_delta_conv, state_delta_S, state_gla_S,
              page_table, w_in_even, conv_w_delta, delta_A_log, delta_dt_bias, delta_norm_g, w_out_even,
              w_in_odd, w_gla_gate2, b_gla_gate2, gla_norm_g, w_out_odd, w_ffn_gate, w_ffn_up, w_ffn_down,
              ln_g, ln_b):
    past = page_table.shape[1] * PAGE_SIZE
    dec_b = x_sample.shape[0]
    bp = x_prompt.shape[0]
    xp, xs = x_prompt, x_sample
    p_rows, p_win, p_conv, p_dS, p_gS = [], [], [], [], []
    s_rows, s_win, s_conv, s_dS, s_gS = [], [], [], [], []
    for layer in range(DEPTH):
        li = layer // 2
        if layer % 2 == 0:
            wts = (w_in_even[li], conv_w_delta[li], delta_A_log[li], delta_dt_bias[li], delta_norm_g[li], w_out_even[li])
            conv0 = jnp.zeros((bp, CONV_W - 1, A_CONV_CH), xp.dtype)
            S0 = jnp.zeros((bp, A_HEADS, A_DK, A_DV), f32)
            yp, rows, win, conv, dS = even_mixer(xp, *wts, conv0, S0, None, None, 0)
            p_rows.append(rows); p_win.append(win); p_conv.append(conv); p_dS.append(dS)
            hist = cache_nsa_kv[page_table, li].reshape(dec_b, past, 4, B_KV, B_DH)
            ys, rows, win, conv, dS = even_mixer(xs, *wts, state_delta_conv[li], state_delta_S[li], hist,
                                                 state_nsa_win[li], past)
            s_rows.append(rows); s_win.append(win); s_conv.append(conv); s_dS.append(dS)
        else:
            wts = (w_in_odd[li], w_gla_gate2[li], b_gla_gate2[li], gla_norm_g[li], w_out_odd[li])
            yp, gS = odd_mixer(xp, *wts, jnp.zeros((bp, C_HEADS, C_DK, C_DV), f32))
            p_gS.append(gS)
            ys, gS = odd_mixer(xs, *wts, state_gla_S[li])
            s_gS.append(gS)
        xp = layer_norm(ALPHA * xp + yp, ln_g[layer, 0], ln_b[layer, 0])
        xs = layer_norm(ALPHA * xs + ys, ln_g[layer, 0], ln_b[layer, 0])
        xp = layer_norm(ALPHA * xp + swiglu(xp, w_ffn_gate[layer], w_ffn_up[layer], w_ffn_down[layer]), ln_g[layer, 1], ln_b[layer, 1])
        xs = layer_norm(ALPHA * xs + swiglu(xs, w_ffn_gate[layer], w_ffn_up[layer], w_ffn_down[layer]), ln_g[layer, 1], ln_b[layer, 1])
    return (xp, xs,
            jnp.stack(p_rows), jnp.stack(p_win), jnp.stack(p_conv), jnp.stack(p_dS), jnp.stack(p_gS),
            jnp.stack(s_rows), jnp.stack(s_win), jnp.stack(s_conv), jnp.stack(s_dS), jnp.stack(s_gS))


_drawn_inputs = setup_inputs


def setup_inputs(seed=0):
    import zlib

    import numpy as np

    out = dict(_drawn_inputs(seed))
    spreads = {}
    factors = {'cache_nsa_kv': 6.593, 'delta_norm_g': 8.0, 'b_gla_gate2': 6.221, 'gla_norm_g': 8.0}
    for name, (base, spread) in spreads.items():
        noise = np.random.default_rng([zlib.crc32(name.encode()), seed]).standard_normal(out[name].shape)
        drawn = base * np.exp(spread * noise) if base else spread * noise
        out[name] = jnp.asarray(drawn.astype(out[name].dtype))
    for name, factor in factors.items():
        out[name] = (out[name] * factor).astype(out[name].dtype)
    return out
```

```python
import math
from contextlib import ExitStack, contextmanager

import numpy as np

import concourse.bass as bass
from concourse import mybir
from concourse.alu_op_type import AluOpType as ALU

ACT = mybir.ActivationFunctionType
F32 = mybir.dt.float32
I32 = mybir.dt.int32
AX = mybir.AxisListType

P = 128
D = 1024
KD = D // P
T = 1024
TT = T // P
NS = 8
N = T + NS
CW = N // 3
NB = 3
FF = 2816
KF = FF // P
ALPHA = 4.0 ** 0.25
NEG = -1e30
HEADS = 4
GV = 256
PAGES = 32
PGRP = 4
NG = PAGES // PGRP

Q_A, K_A, V_A, GATE_A, Q_B, K_CMP, V_CMP, K_SEL, V_SEL, K_WIN, V_WIN, SMALL = 0, 4, 8, 12, 16, 20, 21, 22, 23, 24, 25, 26
R_BETA, R_G, R_NSA = 0, 32, 64
NSMALL = 96
OQ, OK, OV, OR_, OG1 = 0, 4, 8, 16, 24
LEVELS = 7


def constants():
    i = np.arange(P)
    ident = np.eye(P, dtype=np.float32)
    level = np.zeros((P, LEVELS, P), np.float32)
    for lv in range(LEVELS):
        s = 1 << lv
        row, col = i[None, :], i[:, None]
        level[:, lv] = (row // (2 * s) == col // (2 * s)) & (row // s % 2 == 1) & (col // s % 2 == 0)
    upper = (i[:, None] <= i[None, :]).astype(np.float32)
    causal = np.where(i[None, :] <= i[:, None], 0, NEG).astype(np.float32)
    oldest = np.where(i[None, :] > i[:, None], 0, NEG).astype(np.float32)
    qpos = (np.arange(TT) * P)[None, :, None] + i[:, None, None]
    ok = (np.arange(32)[None, None, :] + 1) * 32 <= qpos + 1
    cmp_add = np.where(ok, 0, NEG).astype(np.float32).reshape(P, -1)
    cmp_one = ok.astype(np.float32).reshape(P, -1)
    pool = np.where(i[:, None] // 32 == np.arange(4)[None, :], 1 / 32, 0).astype(np.float32)
    rowsel = np.zeros((NSMALL, 8, P), np.float32)
    for h in range(HEADS):
        rowsel[R_BETA + h, h] = 1
        rowsel[R_G + h, 4 + h] = 1
    sh = np.arange(64)
    group = ((sh[:, None] // 8 == sh[None, :] // 8) & (sh[:, None] % 8 // 4 == sh[None, :] % 8 // 4)).astype(np.float32)
    own = (np.arange(8)[:, None] == sh[None, :] // 8).astype(np.float32)
    headrow = (np.arange(8)[None, :] == sh[:, None] % 8).astype(np.float32)
    pick = np.repeat(np.eye(8, dtype=np.float32), P, axis=1)
    return {
        "c_ident": ident, "c_level": level.reshape(P, -1), "c_upper": upper, "c_causal": causal, "c_oldest": oldest,
        "c_cmp_add": cmp_add, "c_cmp_one": cmp_one, "c_pool": pool, "c_rowsel": rowsel.reshape(NSMALL, -1),
        "c_group": group, "c_own": own, "c_headrow": headrow, "c_pick": pick,
    }


class Res:
    pass


@contextmanager
def phase(nc):
    with nc.cleanup_on_exit():
        with ExitStack() as ctx:
            yield ctx
    nc.all_engine_barrier()


def load_phase(nc, r):
    with phase(nc) as ctx:
        stage = ctx.enter_context(nc.sbuf_tensor("x_stage", [P, 3, D], F32))
        const_in = nc.alloc_semaphore("const_in")
        x_in = [nc.alloc_semaphore(f"x_in{u}") for u in range(3)]
        x_turned = nc.alloc_semaphore("x_turned")
        x_kept_a = nc.alloc_semaphore("x_kept_a")
        x_kept_v = nc.alloc_semaphore("x_kept_v")
        ones_set = nc.alloc_semaphore("ones_set")
        block = ctx.enter_context(nc.Block())
        tiles = [(r.x_prompt[0, t * P:(t + 1) * P, :], P) for t in range(TT)] + [
            (r.x_sample.rearrange("b t d -> (b t) d"), NS)]
        n_const = len(r.const_loads)

        @block.sync
        def _(sp):
            for n, (src, rows) in enumerate(tiles):
                if n >= 3:
                    sp.wait_ge(x_turned, 2 * (n - 2))
                sp.dma_start(stage[0:rows, n % 3, :], src).then_inc(x_in[n % 3], 16)

        @block.scalar
        def _(act):
            for dst, src in r.const_loads:
                act.dma_start(dst, src).then_inc(const_in, 16)
            act.wait_ge(const_in, 16 * n_const)
            for n, (_, rows) in enumerate(tiles):
                b = n % 2 * 2
                act.wait_ge(x_turned, 2 * n + 1)
                act.copy(r.X[:, 0:4, n * P:n * P + rows],
                         r.ps[:, b, :].rearrange("p (k t) -> p k t", k=4)[:, :, 0:rows]).then_inc(x_kept_a, 1)

        @block.vector
        def _(v):
            v.memset(r.ones_d[:], 1.0 / D)
            v.memset(r.ones[:], 1.0)
            v.memset(r.bias[:, 0:1], 1e-5)
            v.memset(r.bias[:, 1:2], 1e-6).then_inc(ones_set, 1)
            for n, (_, rows) in enumerate(tiles):
                b = n % 2 * 2 + 1
                v.wait_ge(x_turned, 2 * n + 2)
                v.tensor_copy(r.X[:, 4:8, n * P:n * P + rows],
                              r.ps[:, b, :].rearrange("p (k t) -> p k t", k=4)[:, :, 0:rows]).then_inc(x_kept_v, 1)

        @block.tensor
        def _(pe):
            pe.wait_ge(const_in, 16 * n_const)
            for n, (_, rows) in enumerate(tiles):
                pe.wait_ge(x_in[n % 3], 16 * (n // 3 + 1))
                if n >= 2:
                    pe.wait_ge(x_kept_a, n - 1)
                    pe.wait_ge(x_kept_v, n - 1)
                for half in range(2):
                    for k in range(4):
                        mm = pe.transpose(r.ps[:, n % 2 * 2 + half, k * P:k * P + rows],
                                          stage[0:rows, n % 3, (4 * half + k) * P:(4 * half + k + 1) * P],
                                          r.ident[0:rows, 0:rows])
                    mm.then_inc(x_turned, 1)


def project_phase(nc, r, name, moving, kt, chunks, load, out, residual=False, small=None):
    total = chunks[-1][1]
    flat = out[:].rearrange("p k n -> p (k n)")
    with phase(nc) as ctx:
        w = ctx.enter_context(nc.sbuf_tensor(name + "_w", [P, 2, kt, P], F32))
        w_in = [nc.alloc_semaphore(name + f"_w_in{u}") for u in range(2)]
        w_clear = nc.alloc_semaphore(name + "_w_clear")
        w_small = nc.alloc_semaphore(name + "_w_small")
        product = nc.alloc_semaphore(name + "_product")
        bank_free = nc.alloc_semaphore(name + "_bank_free")
        block = ctx.enter_context(nc.Block())
        per = len(load(0, 0, 0))

        @block.sync
        def _(sp):
            for u in range(2):
                for dst, src in load(u, u, 0):
                    sp.dma_start(w[:, u][dst], src).then_inc(w_in[u], 16)
            for a, b, shift in chunks:
                a = max(a, 2)
                if shift is not None:
                    with sp.Fori(a // 2, b // 2) as i:
                        for u in range(2):
                            sp.wait_ge(product, i * 6 + (3 * u - 3))
                            for dst, src in load(i * 2 + u, u, shift):
                                sp.dma_start(w[:, u][dst], src).then_inc(w_in[u], 16)
                else:
                    for m in range(a, b):
                        sp.wait_ge(product, 3 * m - 3)
                        for dst, src in load(m, m % 2, shift):
                            sp.dma_start(w[:, m % 2][dst], src).then_inc(w_in[m % 2], 16)
            if small:
                sp.wait_ge(w_clear, 1)
                for dst, src in small[1]:
                    sp.dma_start(w[:, 0][dst], src).then_inc(w_small, 16)

        @block.tensor
        def _(pe):
            with pe.Fori(0, total // 2) as i:
                for u in range(2):
                    pe.wait_ge(w_in[u], i * (16 * per) + 16 * per)
                    for c in range(NB):
                        pe.wait_ge(bank_free, i * 6 + (3 * u + c + 1))
                        for k in range(kt):
                            mm = pe.matmul(r.ps[:, 3 * u + c, 0:CW], w[:, u, k, :], moving[:, k, c * CW:(c + 1) * CW],
                                           start=(k == 0), stop=(k == kt - 1))
                        mm.then_inc(product, 1)
            if small:
                pe.wait_ge(w_small, 16 * len(small[1]))
                for c in range(NB):
                    pe.wait_ge(bank_free, 3 * total + c + 1)
                    for k in range(kt):
                        mm = pe.matmul(r.ps[0:small[0], c, 0:CW], w[:, 0, k, 0:small[0]],
                                       moving[:, k, c * CW:(c + 1) * CW], start=(k == 0), stop=(k == kt - 1))
                    mm.then_inc(product, 1)

        @block.vector
        def _(v):
            v.sem_inc(bank_free, 6)
            with v.Fori(0, total // 2) as i:
                for u in range(2):
                    for c in range(NB):
                        v.wait_ge(product, i * 6 + (3 * u + c + 1))
                        dst = flat[:, bass.ds(i * (2 * N) + (u * N + c * CW), CW)]
                        src = r.ps[:, 3 * u + c, 0:CW]
                        if residual:
                            v.scalar_tensor_tensor(out=dst, in0=dst, scalar=ALPHA, in1=src, op0=ALU.mult,
                                                   op1=ALU.add).then_inc(bank_free, 1)
                        else:
                            v.tensor_scalar(dst, src, 1.0, None, ALU.mult).then_inc(bank_free, 1)
            if small:
                v.wait_ge(product, 3 * total)
                v.memset(w[:, 0, :, :], 0.0).then_inc(w_clear, 1)
                for c in range(NB):
                    v.wait_ge(product, 3 * total + c + 1)
                    v.tensor_copy(out[0:small[0], total, c * CW:(c + 1) * CW],
                                  r.ps[0:small[0], c, 0:CW]).then_inc(bank_free, 1)


def norm_phase(nc, r, layer, which):
    ln = layer * 2 + which
    with phase(nc) as ctx:
        total = ctx.enter_context(nc.sbuf_tensor(f"ln{ln}_total", [P, NB, CW], F32))
        square = ctx.enter_context(nc.sbuf_tensor(f"ln{ln}_square", [P, KD, CW], F32))
        spread = ctx.enter_context(nc.sbuf_tensor(f"ln{ln}_spread", [P, NB, CW], F32))
        rstd = ctx.enter_context(nc.sbuf_tensor(f"ln{ln}_rstd", [P, NB, CW], F32))
        summed, mean_ready, centred, squared, spread_ready, var_ready, rstd_ready, scaled, logged = [
            nc.alloc_semaphore(f"ln{ln}_" + s) for s in
            ("summed", "mean_ready", "centred", "squared", "spread_ready", "var_ready", "rstd_ready", "scaled",
             "logged")]
        block = ctx.enter_context(nc.Block())

        def cols(c):
            return slice(c * CW, (c + 1) * CW)

        @block.vector
        def _(v):
            for c in range(NB):
                v.tensor_reduce(total[:, c, :], r.X[:, :, cols(c)].rearrange("p k n -> p n k"), AX.X,
                                ALU.add).then_inc(summed, 1)
            for c in range(NB):
                v.wait_ge(mean_ready, c + 1)
                v.tensor_tensor(r.X[:, :, cols(c)], r.X[:, :, cols(c)],
                                r.ps[:, c, 0:CW].unsqueeze(1).to_broadcast([P, KD, CW]),
                                ALU.subtract).then_inc(centred, 1)
            for c in range(NB):
                v.wait_ge(squared, c + 1)
                v.tensor_reduce(spread[:, c, :], square[:].rearrange("p k n -> p n k"), AX.X,
                                ALU.add).then_inc(spread_ready, 1)
            for c in range(NB):
                v.wait_ge(rstd_ready, c + 1)
                v.tensor_tensor(r.X[:, :, cols(c)], r.X[:, :, cols(c)],
                                rstd[:, c, :].unsqueeze(1).to_broadcast([P, KD, CW]), ALU.mult).then_inc(scaled, 1)

        @block.tensor
        def _(pe):
            for c in range(NB):
                pe.wait_ge(summed, c + 1)
                pe.matmul(r.ps[:, c, 0:CW], r.ones_d[:], total[:, c, :], start=True, stop=True).then_inc(mean_ready, 1)
            for c in range(NB):
                pe.wait_ge(spread_ready, c + 1)
                pe.matmul(r.ps[:, 3 + c, 0:CW], r.ones_d[:], spread[:, c, :], start=True,
                          stop=True).then_inc(var_ready, 1)

        @block.scalar
        def _(act):
            act.preload_act_table_set("natural_log_exp_and_others")
            for c in range(NB):
                act.wait_ge(centred, c + 1)
                if c:
                    act.wait_ge(spread_ready, c)
                act.activation(square[:], r.X[:, :, cols(c)], ACT.Square).then_inc(squared, 1)
            for c in range(NB):
                act.wait_ge(var_ready, c + 1)
                act.activation(rstd[:, c, :], r.ps[:, 3 + c, 0:CW], ACT.Ln, bias=r.bias[:, 0:1]).then_inc(logged, 1)
                act.wait_ge(logged, c + 1)
                act.activation(rstd[:, c, :], rstd[:, c, :], ACT.Exp, scale=-0.5).then_inc(rstd_ready, 1)
            for c in range(NB):
                act.wait_ge(scaled, c + 1)
                for k in range(KD):
                    act.activation(r.X[:, k, cols(c)], r.X[:, k, cols(c)], ACT.Identity,
                                   bias=r.lnb[:, ln * KD + k:ln * KD + k + 1],
                                   scale=r.lng[:, ln * KD + k:ln * KD + k + 1])


def ffn_up_phase(nc, r, layer):
    flat = r.H[:].rearrange("p k n -> p (k n)")
    wg = r.w_ffn_gate[layer].rearrange("(k p) n -> p k n", p=P)
    wu = r.w_ffn_up[layer].rearrange("(k p) n -> p k n", p=P)
    with phase(nc) as ctx:
        w = ctx.enter_context(nc.sbuf_tensor(f"up{layer}_w", [P, 2, 2, KD, P], F32))
        lit = ctx.enter_context(nc.sbuf_tensor(f"up{layer}_silu", [P, 2, CW], F32))
        w_in = [nc.alloc_semaphore(f"up{layer}_w_in{u}") for u in range(2)]
        gated, upped, silu_ready, hidden = [nc.alloc_semaphore(f"up{layer}_" + s) for s in
                                            ("gated", "upped", "silu_ready", "hidden")]
        block = ctx.enter_context(nc.Block())

        @block.sync
        def _(sp):
            def fetch(m, u):
                sp.dma_start(w[:, u, 0], wg[:, :, bass.ds(m * P, P)]).then_inc(w_in[u], 16)
                sp.dma_start(w[:, u, 1], wu[:, :, bass.ds(m * P, P)]).then_inc(w_in[u], 16)

            fetch(0, 0)
            fetch(1, 1)
            with sp.Fori(1, KF // 2) as i:
                for u in range(2):
                    sp.wait_ge(upped, i * 6 + (3 * u - 3))
                    fetch(i * 2 + u, u)

        @block.tensor
        def _(pe):
            with pe.Fori(0, KF // 2) as i:
                for u in range(2):
                    pe.wait_ge(w_in[u], i * 32 + 32)
                    for c in range(NB):
                        pe.wait_ge(hidden, i * 6 + (3 * u + c + 1))
                        pair = (3 * u + c) % 3
                        for part, done in ((0, gated), (1, upped)):
                            for k in range(KD):
                                mm = pe.matmul(r.ps[:, 2 * pair + part, 0:CW], w[:, u, part, k, :],
                                               r.X[:, k, c * CW:(c + 1) * CW], start=(k == 0), stop=(k == KD - 1))
                            mm.then_inc(done, 1)

        @block.scalar
        def _(act):
            with act.Fori(0, KF // 2) as i:
                for g in range(6):
                    act.wait_ge(hidden, i * 6 + (g + 2))
                    act.wait_ge(gated, i * 6 + (g + 1))
                    act.activation(lit[:, g % 2, :], r.ps[:, 2 * (g % 3), 0:CW], ACT.Silu).then_inc(silu_ready, 1)

        @block.vector
        def _(v):
            v.sem_inc(hidden, 3)
            with v.Fori(0, KF // 2) as i:
                for g in range(6):
                    v.wait_ge(silu_ready, i * 6 + (g + 1))
                    v.wait_ge(upped, i * 6 + (g + 1))
                    v.tensor_tensor(flat[:, bass.ds(i * (2 * N) + (g // 3 * N + g % 3 * CW), CW)],
                                    lit[:, g % 2, :], r.ps[:, 2 * (g % 3) + 1, 0:CW], ALU.mult).then_inc(hidden, 1)


def even_rows_phase(nc, r):
    with phase(nc) as ctx:
        buf = ctx.enter_context(nc.sbuf_tensor("conv_buf", [24, 12 * P], F32))
        tail = ctx.enter_context(nc.sbuf_tensor("conv_tail", [11, 12 * P], F32))
        buf_in, turned, kept_a, kept_v, stored = [nc.alloc_semaphore("rows_" + s) for s in
                                                  ("buf_in", "turned", "kept_a", "kept_v", "stored")]
        block = ctx.enter_context(nc.Block())
        units = []
        for t in range(TT):
            units.append(([r.H[:, K_CMP + j, t * P:(t + 1) * P] for j in range(6)], P, P, r.rows[:, t, :]))
        units.append(([r.H[:, K_CMP + j, T:N] for j in range(6)], NS, P, r.srows[:, :]))
        for g in range(2):
            units.append(([r.H[:, 6 * g + j, T - 3:N] for j in range(6)], 11, P, tail[:, g * 6 * P:(g + 1) * 6 * P]))
        for g in range(2):
            units.append(([buf[:, (6 * g + j) * P:(6 * g + j + 1) * P] for j in range(6)], P, 24,
                          r.bufT[:, 6 * g:6 * g + 6, :].rearrange("p k n -> p (k n)")))

        @block.sync
        def _(sp):
            conv = r.state_delta_conv[0]
            n = 0
            sp.dma_start(buf[:], conv.rearrange("b j c -> (b j) c")).then_inc(buf_in, 16)
            sp.dma_start(r.o_conv_s[0][:, 0:2, :], conv[:, 1:3, :]).then_inc(stored, 16)
            sp.dma_start(r.o_win_s[0].rearrange("b w c g d -> b w (c g d)")[:, 0:511, :],
                         r.state_nsa_win[0].rearrange("b w c g d -> b w (c g d)")[:, 1:512, :]).then_inc(stored, 16)
            n += 2
            for t in range(TT):
                sp.wait_ge(kept_a, t + 1)
                sp.wait_ge(kept_v, t + 1)
                sp.dma_start(r.o_rows_p[0, 0, t * P:(t + 1) * P].rearrange("t c g d -> t (c g d)"),
                             r.rows[:, t, 0:512]).then_inc(stored, 16)
                n += 1
                if t >= 4:
                    sp.dma_start(r.o_win_p[0, 0, (t - 4) * P:(t - 3) * P].rearrange("t c g d -> t (c g d)"),
                                 r.rows[:, t, 512:768]).then_inc(stored, 16)
                    n += 1
            sp.wait_ge(kept_a, 9)
            sp.wait_ge(kept_v, 9)
            sp.dma_start(r.o_rows_s[0, :, 0].rearrange("b c g d -> b (c g d)"), r.srows[:, 0:512]).then_inc(stored, 16)
            sp.dma_start(r.o_win_s[0, :, 511].rearrange("b c g d -> b (c g d)"),
                         r.srows[:, 512:768]).then_inc(stored, 16)
            sp.wait_ge(kept_a, 11)
            sp.wait_ge(kept_v, 11)
            sp.dma_start(r.o_conv_p[0, 0], tail[0:3, :]).then_inc(stored, 16)
            sp.dma_start(r.o_conv_s[0, :, 2], tail[3:11, :]).then_inc(stored, 16)
            n += 4
            sp.wait_ge(stored, 16 * n)

        @block.tensor
        def _(pe):
            for n, (srcs, rows, cols, _) in enumerate(units):
                b = n % 3 * 2
                if n >= 3:
                    pe.wait_ge(kept_a, n - 2)
                    pe.wait_ge(kept_v, n - 2)
                if n == 11:
                    pe.wait_ge(buf_in, 16)
                for j in range(6):
                    k = 24 if n >= 11 else P
                    mm = pe.transpose(r.ps[0:rows, b + j // 4, j % 4 * cols:j % 4 * cols + cols], srcs[j],
                                      r.ident[0:k, 0:k])
                    if j in (3, 5):
                        mm.then_inc(turned, 1)

        @block.scalar
        def _(act):
            for n, (_, rows, cols, dst) in enumerate(units):
                act.wait_ge(turned, 2 * n + 1)
                act.copy(dst[0:rows, 0:4 * cols], r.ps[0:rows, n % 3 * 2, 0:4 * cols]).then_inc(kept_a, 1)

        @block.vector
        def _(v):
            for n, (_, rows, cols, dst) in enumerate(units):
                v.wait_ge(turned, 2 * n + 2)
                v.tensor_copy(dst[0:rows, 4 * cols:6 * cols], r.ps[0:rows, n % 3 * 2 + 1, 0:2 * cols]).then_inc(kept_v, 1)


def gates_phase(nc, r):
    S = r.H[:, SMALL, :]
    B, G, C = slice(R_BETA, R_BETA + 4), slice(R_G, R_G + 4), slice(R_NSA, R_NSA + 24)
    with phase(nc) as ctx:
        par = ctx.enter_context(nc.sbuf_tensor("g_par", [P, 4], F32))
        z = ctx.enter_context(nc.sbuf_tensor("g_z", [P, N], F32))
        az = ctx.enter_context(nc.sbuf_tensor("g_az", [P, N], F32))
        keep = ctx.enter_context(nc.sbuf_tensor("g_keep", [P, T], F32))
        par_in, a, v_, turned, kept = [nc.alloc_semaphore("g_" + s) for s in
                                       ("par_in", "act_step", "dve_step", "turned", "kept")]
        block = ctx.enter_context(nc.Block())

        @block.sync
        def _(sp):
            sp.dma_start(par[G, 0:1], r.dt_bias).then_inc(par_in, 16)
            sp.dma_start(par[G, 1:2], r.A_log).then_inc(par_in, 16)

        @block.vector
        def _(v):
            v.memset(keep[:], 1.0).then_inc(v_, 1)
            v.wait_ge(v_, 1)
            v.memset(keep[:].rearrange("p (c t) -> p c t", t=P)[:, :, 0:1], 0.0)
            v.wait_ge(par_in, 32)
            v.tensor_scalar(z[G, :], S[G, :], par[G, 0:1], None, ALU.add).then_inc(v_, 1)
            v.wait_ge(v_, 2)
            v.scalar_tensor_tensor(out=az[G, :], in0=z[G, :], scalar=-1.0, in1=z[G, :], op0=ALU.mult,
                                   op1=ALU.max).then_inc(v_, 1)
            v.wait_ge(a, 2)
            v.tensor_scalar(z[B, :], z[B, :], 1.0, None, ALU.add)
            v.tensor_scalar(z[C, :], z[C, :], 1.0, None, ALU.add).then_inc(v_, 1)
            v.wait_ge(v_, 4)
            v.reciprocal(S[B, :], z[B, :])
            v.reciprocal(S[C, :], z[C, :])
            v.wait_ge(a, 5)
            v.scalar_tensor_tensor(out=z[G, :], in0=z[G, :], scalar=0.0, in1=az[G, :], op0=ALU.max,
                                   op1=ALU.add).then_inc(v_, 1)
            v.wait_ge(v_, 5)
            v.tensor_scalar(z[G, :], z[G, :], par[G, 2:3], -1.0, ALU.mult, ALU.mult).then_inc(v_, 1)
            v.wait_ge(v_, 6)
            v.tensor_tensor_scan(S[G, 0:T], keep[G, :], z[G, 0:T], 0.0, ALU.mult, ALU.add)
            v.tensor_copy(S[G, T:N], z[G, T:N]).then_inc(v_, 1)
            for n in range(9):
                rows = P if n < 8 else NS
                v.wait_ge(turned, n + 1)
                v.tensor_copy(r.tok[0:rows, n, :], r.ps[0:rows, n % 8, 0:NSMALL]).then_inc(kept, 1)

        @block.scalar
        def _(act):
            act.preload_act_table_set("natural_log_exp_and_others")
            act.activation(z[B, :], S[B, :], ACT.Exp, scale=-1.0).then_inc(a, 1)
            act.activation(z[C, :], S[C, :], ACT.Exp, scale=-1.0).then_inc(a, 1)
            act.wait_ge(par_in, 32)
            act.activation(par[G, 2:3], par[G, 1:2], ACT.Exp).then_inc(a, 1)
            act.wait_ge(v_, 3)
            act.activation(az[G, :], az[G, :], ACT.Exp, scale=-1.0).then_inc(a, 1)
            act.wait_ge(a, 4)
            act.activation(az[G, :], az[G, :], ACT.Ln, bias=1.0).then_inc(a, 1)

        @block.tensor
        def _(pe):
            pe.wait_ge(v_, 7)
            for n in range(9):
                rows = P if n < 8 else NS
                if n == 8:
                    pe.wait_ge(kept, 1)
                pe.transpose(r.ps[0:rows, n % 8, 0:NSMALL], S[0:NSMALL, n * P:n * P + rows],
                             r.ident[0:NSMALL, 0:NSMALL]).then_inc(turned, 1)


def store_phase(nc, r):
    with phase(nc) as ctx:
        stage = ctx.enter_context(nc.sbuf_tensor("y_stage", [P, 2, D], F32))
        turned, kept_a, kept_v = [nc.alloc_semaphore("y_" + s) for s in ("turned", "kept_a", "kept_v")]
        stored = [nc.alloc_semaphore(f"y_stored{u}") for u in range(2)]
        block = ctx.enter_context(nc.Block())
        tiles = [(r.o_y_p[0, t * P:(t + 1) * P, :], P) for t in range(TT)] + [
            (r.o_y_s.rearrange("b t d -> (b t) d"), NS)]

        @block.sync
        def _(sp):
            for n, (dst, rows) in enumerate(tiles):
                sp.wait_ge(kept_a, n + 1)
                sp.wait_ge(kept_v, n + 1)
                sp.dma_start(dst, stage[0:rows, n % 2, :]).then_inc(stored[n % 2], 16)
            sp.wait_ge(stored[0], 16 * 5)
            sp.wait_ge(stored[1], 16 * 4)

        @block.tensor
        def _(pe):
            for n, (_, rows) in enumerate(tiles):
                if n >= 2:
                    pe.wait_ge(kept_a, n - 1)
                    pe.wait_ge(kept_v, n - 1)
                for half in range(2):
                    for k in range(4):
                        mm = pe.transpose(r.ps[0:rows, n % 2 * 2 + half, k * P:(k + 1) * P],
                                          r.X[:, 4 * half + k, n * P:n * P + rows], r.ident[:])
                    mm.then_inc(turned, 1)

        @block.scalar
        def _(act):
            for n, (_, rows) in enumerate(tiles):
                act.wait_ge(turned, 2 * n + 1)
                if n >= 2:
                    act.wait_ge(stored[n % 2], 16 * (n // 2))
                act.copy(stage[0:rows, n % 2, 0:512], r.ps[0:rows, n % 2 * 2, :]).then_inc(kept_a, 1)

        @block.vector
        def _(v):
            for n, (_, rows) in enumerate(tiles):
                v.wait_ge(turned, 2 * n + 2)
                if n >= 2:
                    v.wait_ge(stored[n % 2], 16 * (n // 2))
                v.tensor_copy(stage[0:rows, n % 2, 512:1024], r.ps[0:rows, n % 2 * 2 + 1, :]).then_inc(kept_v, 1)

def nsa_prompt_phase(nc, r):
    flat = r.H[:].rearrange("p k n -> p (k n)")
    UNITS = [(t, g) for t in range(TT) for g in range(2)]
    NU = len(UNITS)

    def blocks(t):
        lo = max(0, t - 4)
        return [("cmp", 0)] + [("sel", b) for b in range(t + 1)] + [("win", b) for b in range(lo, t + 1)]

    def groups(t):
        bl = blocks(t)
        return [bl[0:1]] + [bl[s:s + 4] for s in range(1, len(bl), 4)]

    first = [0]
    for t, g in UNITS:
        first.append(first[-1] + len(groups(t)))
    GT = first[-1]
    with phase(nc) as ctx:
        def sb(name, shape):
            return ctx.enter_context(nc.sbuf_tensor("np_" + name, shape, F32))

        causal, oldest = sb("causal", [P, P]), sb("oldest", [P, P])
        cmp_add, cmp_one = sb("cmp_add", [P, TT, 32]), sb("cmp_one", [P, TT, 32])
        kcb, vcbT, vcb = sb("kcb", [P, 32]), sb("vcbT", [P, 32]), sb("vcb", [32, P])
        QS = sb("q", [P, 2, P])
        gates = sb("gates", [P, 2, 2, 3])
        Psel, Pwin, Pcmp = sb("psel", [P, 2, T]), sb("pwin", [P, 2, 640]), sb("pcmp", [P, 2, 32])
        PT = sb("pt", [P, 14, P])
        top, ntop, den, coef = sb("top", [P, 2, 3]), sb("ntop", [P, 2, 3]), sb("den", [P, 2, 3]), sb("coef", [P, 2, 3])
        (tables_in, means_ready, vcb_turned, vcb_kept, q_ready, scored, masked, topped, negated, exped, inverted,
         weighed, scaled, turned, kept, o_ready, o_kept) = [
            nc.alloc_semaphore("np_" + s) for s in
            ("tables_in", "means_ready", "vcb_turned", "vcb_kept", "q_ready", "scored", "masked", "topped", "negated",
             "exped", "inverted", "weighed", "scaled", "turned", "kept", "o_ready", "o_kept")]
        block = ctx.enter_context(nc.Block())
        s_sel = r.ps[:, 0:2, :].rearrange("p b n -> p (b n)")
        s_win = r.ps[:, 2:4, :].rearrange("p b n -> p (b n)")
        gate_view = r.tok[:, :, R_NSA:R_NSA + 24].rearrange("p t (g h b) -> p t g h b", g=2, h=4)

        @block.sync
        def _(sp):
            for dst, src in ((causal[:], r.c_causal), (oldest[:], r.c_oldest),
                             (cmp_add[:].rearrange("p t c -> p (t c)"), r.c_cmp_add),
                             (cmp_one[:].rearrange("p t c -> p (t c)"), r.c_cmp_one)):
                sp.dma_start(dst, src).then_inc(tables_in, 16)

        @block.tensor
        def _(pe):
            pe.wait_ge(means_ready, 2)
            pe.transpose(r.ps[0:32, 6, 0:P], vcbT[:], r.ident[:]).then_inc(vcb_turned, 1)
            pe.wait_ge(vcb_kept, 1)

            def scores(i, j):
                t, g = UNITS[j]
                rows = slice(64 * g, 64 * g + 64)
                lo, hi = max(0, t - 4) * P, (t + 1) * P
                pe.wait_ge(q_ready, i * TT + (t + 1))
                pe.wait_ge(exped, i * NU + (j + 1))
                for s in range(0, hi, 512):
                    e = min(hi, s + 512)
                    pe.matmul(s_sel[:, s:e], QS[rows, t % 2, :], r.H[rows, K_SEL, s:e], start=True, stop=True)
                for s in range(0, hi - lo, 512):
                    e = min(hi - lo, s + 512)
                    pe.matmul(s_win[:, s:e], QS[rows, t % 2, :], r.H[rows, K_WIN, lo + s:lo + e], start=True,
                              stop=True)
                pe.matmul(s_win[:, 640:672], QS[rows, t % 2, :], kcb[rows, :], start=True,
                          stop=True).then_inc(scored, 1)

            def turn(i, j):
                t, g = UNITS[j]
                pe.wait_ge(scaled, i * NU + (j + 1))
                lo = max(0, t - 4)
                for n, grp in enumerate(groups(t)):
                    gg = first[j] + n
                    pe.wait_ge(kept, i * GT + (max(gg - 1, 0) + 1))
                    for q, (kind, b) in enumerate(grp):
                        if kind == "cmp":
                            mm = pe.transpose(r.ps[0:32, 4 + gg % 2, 0:P], Pcmp[:, j % 2, :], r.ident[:])
                        else:
                            src = Psel[:, j % 2, b * P:(b + 1) * P] if kind == "sel" else \
                                Pwin[:, j % 2, (b - lo) * P:(b - lo + 1) * P]
                            mm = pe.transpose(r.ps[:, 4 + gg % 2, q * P:(q + 1) * P], src, r.ident[:])
                    mm.then_inc(turned, 1)

            def values(i, j):
                t, g = UNITS[j]
                bl = blocks(t)
                pe.wait_ge(kept, i * GT + (first[j + 1] + 1))
                pe.wait_ge(o_kept, i * NU + (max(j - 1, 0) + 1))
                for n, (kind, b) in enumerate(bl):
                    if kind == "cmp":
                        lhs, rhs = vcb[:], PT[0:32, 0, :]
                    else:
                        lhs = r.rows[:, b, 384:512] if kind == "sel" else r.rows[:, b, 640:768]
                        rhs = PT[:, n, :]
                    mm = pe.matmul(r.ps[:, 6 + j % 2, 0:P], lhs, rhs, start=(n == 0), stop=(n == len(bl) - 1))
                mm.then_inc(o_ready, 1)

            pe.sem_inc(scored, 1)
            pe.sem_inc(turned, 1)
            pe.sem_inc(o_ready, 1)
            with pe.Fori(0, 4) as i:
                scores(i, 0)
                for j in range(NU):
                    if j + 1 < NU:
                        scores(i, j + 1)
                    turn(i, j)
                    values(i, j)

        @block.scalar
        def _(act):
            act.sem_inc(exped, 1)
            act.sem_inc(kept, 1)
            with act.Fori(0, 4) as i:
                for j, (t, g) in enumerate(UNITS):
                    s = j % 2
                    lo, hi = max(0, t - 4) * P, (t + 1) * P
                    act.wait_ge(turned, i * GT + ((first[j - 1] if j else 0) + 1))
                    act.wait_ge(negated, i * NU + (j + 1))
                    act.activation(Pcmp[:, s, :], s_win[:, 640:672], ACT.Exp, bias=ntop[:, s, 0:1], scale=0.125,
                                   accum_out=den[:, s, 0:1])
                    act.activation(Psel[:, s, 0:hi], s_sel[:, 0:hi], ACT.Exp, bias=ntop[:, s, 1:2], scale=0.125,
                                   accum_out=den[:, s, 1:2])
                    act.activation(Pwin[:, s, 0:hi - lo], s_win[:, 0:hi - lo], ACT.Exp, bias=ntop[:, s, 2:3],
                                   scale=0.125, accum_out=den[:, s, 2:3]).then_inc(exped, 1)
                    at = 0
                    for n, grp in enumerate(groups(t)):
                        gg = first[j] + n
                        if n == 0:
                            act.wait_ge(o_ready, i * NU + (j + 1))
                        act.wait_ge(turned, i * GT + (gg + 2))
                        if n == 0:
                            act.copy(PT[0:32, 0, :], r.ps[0:32, 4 + gg % 2, 0:P]).then_inc(kept, 1)
                        else:
                            act.copy(PT[:, at:at + len(grp), :].rearrange("p b n -> p (b n)"),
                                     r.ps[:, 4 + gg % 2, 0:len(grp) * P]).then_inc(kept, 1)
                        at += len(grp)

        @block.vector
        def _(v):
            v.tensor_reduce(kcb[:], r.H[:, K_CMP, 0:T].rearrange("p (c j) -> p c j", j=32), AX.X, ALU.add)
            v.tensor_reduce(vcbT[:], r.H[:, V_CMP, 0:T].rearrange("p (c j) -> p c j", j=32), AX.X,
                            ALU.add).then_inc(means_ready, 1)
            v.wait_ge(means_ready, 1)
            v.tensor_scalar(kcb[:], kcb[:], 1 / 32, None, ALU.mult)
            v.tensor_scalar(vcbT[:], vcbT[:], 1 / 32, None, ALU.mult).then_inc(means_ready, 1)
            v.wait_ge(vcb_turned, 1)
            v.tensor_copy(vcb[:], r.ps[0:32, 6, 0:P]).then_inc(vcb_kept, 1)
            v.wait_ge(tables_in, 64)
            v.sem_inc(o_kept, 1)

            def fetch(i, t):
                v.wait_ge(scored, i * NU + (max(2 * t - 2, 0) + 1))
                v.tensor_copy(gates[:, t % 2, :, :], gate_view[:, t, :, bass.ds(i, 1), :].squeeze(2))
                v.tensor_copy(QS[:, t % 2, :], flat[:, bass.ds(i * N + (Q_B * N + t * P), P)]).then_inc(q_ready, 1)

            def maxima(i, j):
                t, g = UNITS[j]
                s = j % 2
                hi = (t + 1) * P
                w = hi - max(0, t - 4) * P
                v.wait_ge(scored, i * NU + (j + 2))
                v.tensor_tensor(s_sel[:, hi - P:hi], s_sel[:, hi - P:hi], causal[:], ALU.add)
                v.tensor_tensor(s_win[:, w - P:w], s_win[:, w - P:w], causal[:], ALU.add)
                if t >= 4:
                    v.tensor_tensor(s_win[:, 0:P], s_win[:, 0:P], oldest[:], ALU.add)
                v.tensor_tensor(s_win[:, 640:672], s_win[:, 640:672], cmp_add[:, t, :], ALU.add).then_inc(masked, 1)
                v.wait_ge(masked, i * NU + (j + 1))
                v.tensor_reduce(top[:, s, 0:1], s_win[:, 640:672], AX.X, ALU.max)
                v.tensor_reduce(top[:, s, 1:2], s_sel[:, 0:hi], AX.X, ALU.max)
                v.tensor_reduce(top[:, s, 2:3], s_win[:, 0:w], AX.X, ALU.max).then_inc(topped, 1)
                v.wait_ge(topped, i * NU + (j + 1))
                v.tensor_scalar(ntop[:, s, :], top[:, s, :], -0.125, None, ALU.mult).then_inc(negated, 1)

            def weigh(i, j):
                t, g = UNITS[j]
                s = j % 2
                hi = (t + 1) * P
                w = hi - max(0, t - 4) * P
                v.wait_ge(exped, i * NU + (j + 2))
                v.reciprocal(coef[:, s, :], den[:, s, :]).then_inc(inverted, 1)
                v.wait_ge(inverted, i * NU + (j + 1))
                v.tensor_tensor(coef[:, s, :], coef[:, s, :], gates[:, t % 2, g, :], ALU.mult).then_inc(weighed, 1)
                v.wait_ge(weighed, i * NU + (j + 1))
                v.scalar_tensor_tensor(out=Pcmp[:, s, :], in0=Pcmp[:, s, :], scalar=coef[:, s, 0:1],
                                       in1=cmp_one[:, t, :], op0=ALU.mult, op1=ALU.mult)
                v.tensor_scalar(Psel[:, s, 0:hi], Psel[:, s, 0:hi], coef[:, s, 1:2], None, ALU.mult)
                v.tensor_scalar(Pwin[:, s, 0:w], Pwin[:, s, 0:w], coef[:, s, 2:3], None, ALU.mult).then_inc(scaled, 1)

            with v.Fori(0, 4) as i:
                fetch(i, 0)
                maxima(i, 0)
                for j, (t, g) in enumerate(UNITS):
                    weigh(i, j)
                    if g == 0 and t + 1 < TT:
                        fetch(i, t + 1)
                    if j + 1 < NU:
                        maxima(i, j + 1)
                    v.wait_ge(o_ready, i * NU + (j + 2))
                    v.tensor_scalar(flat[64 * g:64 * g + 64, bass.ds(i * N + (Q_B * N + t * P), P)],
                                    r.ps[64 * g:64 * g + 64, 6 + j % 2, 0:P], 1.0, None,
                                    ALU.mult).then_inc(o_kept, 1)


def conv_phase(nc, r):
    flat = r.H[:].rearrange("p k n -> p (k n)")
    buf = r.bufT[:].rearrange("p k (s j) -> p k s j", j=3)
    with phase(nc) as ctx:
        cw = ctx.enter_context(nc.sbuf_tensor("conv_w", [P, 48], F32))
        acc = ctx.enter_context(nc.sbuf_tensor("conv_acc", [P, 2, N], F32))
        w_in, tapped, acc_free = [nc.alloc_semaphore("conv_" + s) for s in ("w_in", "tapped", "acc_free")]
        block = ctx.enter_context(nc.Block())

        @block.sync
        def _(sp):
            sp.dma_start(cw[:], r.conv_w).then_inc(w_in, 16)

        @block.vector
        def _(v):
            v.wait_ge(w_in, 16)
            v.sem_inc(acc_free, 2)
            with v.Fori(0, 6) as i:
                for u in range(2):
                    v.wait_ge(acc_free, i * 2 + (u + 1))
                    v.tensor_scalar(acc[:, u, :], flat[:, bass.ds(i * (2 * N) + u * N, N)],
                                    cw[:, bass.ds(i * 2 + (36 + u), 1)], None, ALU.mult).then_inc(tapped, 1)
                    for j in (2, 1, 0):
                        w = cw[:, bass.ds(i * 2 + (12 * j + u), 1)]
                        back = 3 - j
                        v.wait_ge(tapped, i * 8 + (4 * u + back))
                        v.scalar_tensor_tensor(out=acc[:, u, T:N], in0=buf[:, bass.ds(i * 2 + u, 1), :, j].squeeze(1),
                                               scalar=w, in1=acc[:, u, T:N], op0=ALU.mult, op1=ALU.add)
                        v.scalar_tensor_tensor(out=acc[:, u, back:T],
                                               in0=flat[:, bass.ds(i * (2 * N) + u * N, T - back)],
                                               scalar=w, in1=acc[:, u, back:T], op0=ALU.mult,
                                               op1=ALU.add).then_inc(tapped, 1)

        @block.scalar
        def _(act):
            act.activation(r.H[:, GATE_A:GATE_A + 4, :], r.H[:, GATE_A:GATE_A + 4, :], ACT.Silu)
            with act.Fori(0, 6) as i:
                for u in range(2):
                    act.wait_ge(tapped, i * 8 + (4 * u + 4))
                    act.wait_ge(w_in, 16)
                    act.activation(flat[:, bass.ds(i * (2 * N) + u * N, N)], acc[:, u, :],
                                   ACT.Silu).then_inc(acc_free, 1)


def delta_prompt_phase(nc, r):
    H4 = range(HEADS)
    with phase(nc) as ctx:
        def sb(name, shape):
            return ctx.enter_context(nc.sbuf_tensor("dp_" + name, shape, F32))

        level, upper, rowsel = sb("level", [P, LEVELS, P]), sb("upper", [P, P]), sb("rowsel", [NSMALL, 8, P])
        ng = sb("ng", [P, 1])
        SQ, RN = sb("sq", [P, 8, P]), sb("rn", [P, 8, P])
        QT, KT, VT, GB, DL, EG, QG, AT, QK = [sb(n, [P, 4, P]) for n in
                                              ("qt", "kt", "vt", "gb", "dl", "eg", "qg", "at", "qk")]
        AM = sb("am", [P, 2, 4, P])
        Dm, DT, PS, KBG, KD, VB, S, RO = [sb(n, [P, 4, P]) for n in ("d", "dt", "p", "kbg", "kd", "vb", "s", "ro")]
        U, WT = SQ[:, 0:4, :], SQ[:, 4:8, :]
        VN, OS = RN[:, 0:4, :], RN[:, 4:8, :]
        tk, e4, bg = sb("tk", [P, 12]), sb("e4", [P, 8]), sb("bg", [P, 4])
        names = ("tables_in", "chunk_done", "squared", "sums_ready", "logged", "rn_ready", "gb_ready", "v_copied",
                 "decay_in", "decay_ready", "qk_ready", "turned", "kk_ready", "lt_masked", "at_half", "at_ready",
                 "bg_ready", "kbg_ready", "kdv_ready", "am_ready", "p_ready", "p_kept", "d_ready", "updated",
                 "uw_ready", "wt_kept", "u_kept", "ws_ready", "vn_ready", "o_ready", "ds_ready", "o_squared",
                 "o_summed", "o_logged", "ro_ready", "o_scaled", "s_ready", "stored")
        (tables_in, chunk_done, squared, sums_ready, logged, rn_ready, gb_ready, v_copied, decay_in, decay_ready,
         qk_ready, turned, kk_ready, lt_masked, at_half, at_ready, bg_ready, kbg_ready, kdv_ready, am_ready, p_ready,
         p_kept, d_ready, updated, uw_ready, wt_kept, u_kept, ws_ready, vn_ready, o_ready, ds_ready, o_squared,
         o_summed, o_logged, ro_ready, o_scaled, s_ready, stored) = [
            nc.alloc_semaphore("dp_" + s) for s in names]
        block = ctx.enter_context(nc.Block())

        def bank(b):
            return r.ps[:, b, :].rearrange("p (h n) -> p h n", h=4)

        @block.sync
        def _(sp):
            for dst, src in ((level[:].rearrange("p l n -> p (l n)"), r.c_level), (upper[:], r.c_upper),
                             (rowsel[:].rearrange("p l n -> p (l n)"), r.c_rowsel), (ng[:], r.delta_ng)):
                sp.dma_start(dst, src).then_inc(tables_in, 16)
            sp.wait_ge(s_ready, TT + 1)
            sp.dma_start(r.o_dS_p[0, 0].rearrange("h d e -> d h e"), S[:]).then_inc(stored, 16)
            sp.wait_ge(stored, 16)

        @block.scalar
        def _(act):
            act.preload_act_table_set("natural_log_exp_and_others")
            with act.Fori(0, TT) as c:
                cols = bass.ds(c * P, P)
                act.wait_ge(chunk_done, c + 1)
                act.wait_ge(tables_in, 64)
                act.activation(SQ[:], r.H[:, Q_A:Q_A + 8, cols], ACT.Square).then_inc(squared, 1)
                act.copy(VT[:], r.H[:, V_A:V_A + 4, cols]).then_inc(v_copied, 1)
                act.wait_ge(sums_ready, c + 1)
                act.activation(RN[:].rearrange("p k n -> p (k n)"), r.ps[:, 0:2, :].rearrange("p b n -> p (b n)"),
                               ACT.Ln, bias=r.bias[:, 1:2]).then_inc(logged, 1)
                act.wait_ge(logged, c + 1)
                act.activation(RN[:], RN[:], ACT.Exp, scale=-0.5).then_inc(rn_ready, 1)
                act.wait_ge(decay_in, c + 1)
                act.activation(DL[:], DL[:], ACT.Exp)
                act.activation(EG[:], GB[:], ACT.Exp)
                act.activation(e4[:], tk[:, 4:12], ACT.Exp).then_inc(decay_ready, 1)
                act.wait_ge(decay_ready, c + 1)
                act.wait_ge(turned, c + 1)
                for h in H4:
                    act.activation(KD[:, h, :], bank(4)[:, h, :], ACT.Copy, scale=e4[:, 4 + h:5 + h])
                for h in H4:
                    mm = act.activation(VB[:, h, :], bank(5)[:, h, :], ACT.Copy, scale=tk[:, h:h + 1])
                mm.then_inc(kdv_ready, 1)
                for lv in range(LEVELS):
                    act.wait_ge(p_ready, c * LEVELS + (lv + 1))
                    act.copy(PS[:], bank(6)).then_inc(p_kept, 1)
                act.wait_ge(uw_ready, c + 1)
                act.copy(WT, bank(1)).then_inc(wt_kept, 1)
                act.wait_ge(o_ready, c + 1)
                act.activation(OS, bank(5), ACT.Square).then_inc(o_squared, 1)
                act.wait_ge(o_summed, c + 1)
                act.activation(RO[:], bank(7), ACT.Ln, bias=r.bias[:, 1:2], scale=1 / 128).then_inc(o_logged, 1)
                act.wait_ge(o_logged, c + 1)
                act.activation(RO[:], RO[:], ACT.Exp, scale=-0.5).then_inc(ro_ready, 1)

        @block.tensor
        def _(pe):
            pe.wait_ge(tables_in, 64)
            with pe.Fori(0, TT) as c:
                cols = bass.ds(c * P, P)
                pe.wait_ge(squared, c + 1)
                pe.matmul(r.ps[:, 0, :], r.ones[:], SQ[:, 0:4, :], start=True, stop=True)
                pe.matmul(r.ps[:, 1, :], r.ones[:], SQ[:, 4:8, :], start=True, stop=True)
                for j in range(8):
                    mm = pe.matmul(bank(2 + j // 4)[:, j % 4, :], rowsel[:, j, :], r.H[0:NSMALL, SMALL, cols],
                                   start=True, stop=True)
                mm.then_inc(sums_ready, 1)
                pe.wait_ge(v_copied, c + 1)
                for h in H4:
                    pe.transpose(bank(5)[:, h, :], VT[:, h, :], r.ident[:])
                pe.wait_ge(qk_ready, c + 1)
                for h in H4:
                    mm = pe.transpose(bank(4)[:, h, :], KT[:, h, :], r.ident[:])
                mm.then_inc(turned, 1)
                for h in H4:
                    pe.matmul(bank(0)[:, h, :], KT[:, h, :], KT[:, h, :], start=True, stop=True)
                for h in H4:
                    mm = pe.matmul(bank(1)[:, h, :], KT[:, h, :], QT[:, h, :], start=True, stop=True)
                mm.then_inc(kk_ready, 1)
                for lv in range(LEVELS):
                    pe.wait_ge(am_ready, c * LEVELS + (lv + 1))
                    pe.wait_ge(updated, c * (LEVELS + 1) + (lv + 1))
                    for h in H4:
                        mm = pe.matmul(bank(6)[:, h, :], AM[:, lv % 2, h, :], Dm[:, h, :], start=True, stop=True)
                    mm.then_inc(p_ready, 1)
                    pe.wait_ge(p_kept, c * LEVELS + (lv + 1))
                    if lv < LEVELS - 1:
                        for h in H4:
                            pe.matmul(bank(7)[:, h, :], DT[:, h, :], PS[:, h, :], start=True, stop=True)
                    for h in H4:
                        mm = pe.matmul(bank(3)[:, h, :], PS[:, h, :], DT[:, h, :], start=True, stop=True)
                    mm.then_inc(d_ready, 1)
                pe.wait_ge(updated, c * (LEVELS + 1) + (LEVELS + 1))
                pe.wait_ge(kdv_ready, c + 1)
                pe.wait_ge(kbg_ready, c + 1)
                for h in H4:
                    pe.matmul(bank(0)[:, h, :], DT[:, h, :], VB[:, h, :], start=True, stop=True)
                for h in H4:
                    mm = pe.matmul(bank(1)[:, h, :], KBG[:, h, :], DT[:, h, :], start=True, stop=True)
                mm.then_inc(uw_ready, 1)
                pe.wait_ge(wt_kept, c + 1)
                pe.wait_ge(s_ready, c + 1)
                for h in H4:
                    mm = pe.matmul(bank(4)[:, h, :], WT[:, h, :], S[:, h, :], start=True, stop=True)
                mm.then_inc(ws_ready, 1)
                pe.wait_ge(vn_ready, c + 1)
                for h in H4:
                    pe.matmul(bank(5)[:, h, :], S[:, h, :], QG[:, h, :], start=True, stop=False)
                    mm = pe.matmul(bank(5)[:, h, :], VN[:, h, :], QK[:, h, :], start=False, stop=True)
                mm.then_inc(o_ready, 1)
                for h in H4:
                    mm = pe.matmul(bank(6)[:, h, :], KD[:, h, :], VN[:, h, :], start=True, stop=True)
                mm.then_inc(ds_ready, 1)
                pe.wait_ge(o_squared, c + 1)
                pe.matmul(r.ps[:, 7, :], r.ones[:], OS, start=True, stop=True).then_inc(o_summed, 1)

        def update(v, c, lv):
            v.wait_ge(d_ready, c * LEVELS + (lv + 1))
            if lv < LEVELS - 1:
                v.tensor_tensor(Dm[:], Dm[:], bank(7), ALU.subtract)
            v.tensor_tensor(DT[:], DT[:], bank(3), ALU.subtract).then_inc(updated, 1)

        @block.vector
        def _(v):
            v.wait_ge(tables_in, 64)
            v.memset(S[:], 0.0).then_inc(s_ready, 1)
            v.sem_inc(chunk_done, 1)
            ident4 = r.ident[:].unsqueeze(1).to_broadcast([P, 4, P])
            upper4 = upper[:].unsqueeze(1).to_broadcast([P, 4, P])
            with v.Fori(0, TT) as c:
                cols = bass.ds(c * P, P)
                v.wait_ge(chunk_done, c + 1)
                v.tensor_copy(tk[:, 0:4], r.tok[:, bass.ds(c, 1), R_BETA:R_BETA + 4].squeeze(1))
                v.tensor_copy(tk[:, 4:8], r.tok[:, bass.ds(c, 1), R_G:R_G + 4].squeeze(1))
                v.tensor_copy(Dm[:], ident4)
                v.tensor_copy(DT[:], ident4).then_inc(updated, 1)
                v.wait_ge(updated, c * (LEVELS + 1) + 1)
                v.wait_ge(sums_ready, c + 1)
                v.tensor_copy(GB[:], bank(3)).then_inc(gb_ready, 1)
                v.wait_ge(gb_ready, c + 1)
                for h in H4:
                    v.tensor_scalar(DL[:, h, :], GB[:, h, :], tk[:, 4 + h:5 + h], 0.0, ALU.subtract, ALU.min)
                v.tensor_tensor(tk[:, 8:12], GB[:, :, P - 1], tk[:, 4:8], ALU.subtract).then_inc(decay_in, 1)
                v.wait_ge(rn_ready, c + 1)
                v.scalar_tensor_tensor(out=QT[:], in0=r.H[:, Q_A:Q_A + 4, cols], scalar=128 ** -0.5, in1=RN[:, 0:4, :],
                                       op0=ALU.mult, op1=ALU.mult)
                v.tensor_tensor(KT[:], r.H[:, K_A:K_A + 4, cols], RN[:, 4:8, :], ALU.mult).then_inc(qk_ready, 1)
                v.wait_ge(decay_ready, c + 1)
                v.tensor_tensor(DL[:], DL[:], upper4, ALU.mult).then_inc(lt_masked, 1)
                v.tensor_tensor(bg[:], tk[:, 0:4], e4[:, 0:4], ALU.mult).then_inc(bg_ready, 1)
                v.wait_ge(lt_masked, c + 1)
                v.wait_ge(kk_ready, c + 1)
                v.tensor_tensor(AT[:], bank(0), DL[:], ALU.mult).then_inc(at_half, 1)
                v.wait_ge(at_half, c + 1)
                v.tensor_tensor(AT[:], AT[:], bank(2), ALU.mult).then_inc(at_ready, 1)
                v.wait_ge(at_ready, c + 1)
                for lv in range(LEVELS):
                    if lv >= 2:
                        v.wait_ge(p_ready, c * LEVELS + (lv - 1))
                    v.tensor_tensor(AM[:, lv % 2], AT[:], level[:, lv, :].unsqueeze(1).to_broadcast([P, 4, P]),
                                    ALU.mult).then_inc(am_ready, 1)
                    if lv == 0:
                        v.tensor_tensor(QK[:], bank(1), DL[:], ALU.mult)
                        v.wait_ge(qk_ready, c + 1)
                        v.tensor_tensor(QG[:], QT[:], EG[:], ALU.mult)
                    if lv == 1:
                        v.wait_ge(bg_ready, c + 1)
                        v.wait_ge(turned, c + 1)
                        v.wait_ge(kdv_ready, c + 1)
                        for h in H4:
                            mm = v.tensor_scalar(KBG[:, h, :], bank(4)[:, h, :], bg[:, h:h + 1], None, ALU.mult)
                        mm.then_inc(kbg_ready, 1)
                    if lv:
                        update(v, c, lv - 1)
                update(v, c, LEVELS - 1)
                v.wait_ge(uw_ready, c + 1)
                v.tensor_copy(U, bank(0)).then_inc(u_kept, 1)
                v.wait_ge(u_kept, c + 1)
                v.wait_ge(ws_ready, c + 1)
                v.tensor_tensor(VN, U, bank(4), ALU.subtract).then_inc(vn_ready, 1)
                v.wait_ge(ds_ready, c + 1)
                for h in H4:
                    mm = v.scalar_tensor_tensor(out=S[:, h, :], in0=S[:, h, :], scalar=EG[:, h, P - 1:P],
                                                in1=bank(6)[:, h, :], op0=ALU.mult, op1=ALU.add)
                mm.then_inc(s_ready, 1)
                v.wait_ge(ro_ready, c + 1)
                v.scalar_tensor_tensor(out=RO[:], in0=bank(5), scalar=ng[:, 0:1], in1=RO[:], op0=ALU.mult,
                                       op1=ALU.mult).then_inc(o_scaled, 1)
                v.wait_ge(o_scaled, c + 1)
                v.tensor_tensor(r.H[:, GATE_A:GATE_A + 4, cols], RO[:], r.H[:, GATE_A:GATE_A + 4, cols],
                                ALU.mult).then_inc(chunk_done, 1)


def gla_gate_phase(nc, r):
    with phase(nc) as ctx:
        g2 = ctx.enter_context(nc.sbuf_tensor("gg_w", [16, 512], F32))
        b2 = ctx.enter_context(nc.sbuf_tensor("gg_b", [P, 4], F32))
        az = ctx.enter_context(nc.sbuf_tensor("gg_az", [P, 2, N], F32))
        w_in, product, biased, absed, exped, logged, lowered, done = [
            nc.alloc_semaphore("gg_" + s) for s in
            ("w_in", "product", "biased", "absed", "exped", "logged", "lowered", "done")]
        block = ctx.enter_context(nc.Block())

        @block.sync
        def _(sp):
            sp.dma_start(g2[:], r.w_g2).then_inc(w_in, 16)
            sp.dma_start(b2[:], r.b_g2).then_inc(w_in, 16)

        @block.tensor
        def _(pe):
            pe.wait_ge(w_in, 32)
            for m in range(4):
                if m >= 2:
                    pe.wait_ge(biased, m - 1)
                for c in range(NB):
                    mm = pe.matmul(r.ps[:, m % 2 * 3 + c, 0:CW], g2[:, m * P:(m + 1) * P],
                                   r.H[0:16, OG1, c * CW:(c + 1) * CW], start=True, stop=True)
                mm.then_inc(product, 1)

        @block.vector
        def _(v):
            def log_sigmoid(m):
                v.wait_ge(logged, m + 1)
                v.scalar_tensor_tensor(out=r.LA[:, m, :], in0=r.LA[:, m, :], scalar=0.0, in1=az[:, m % 2, :],
                                       op0=ALU.min, op1=ALU.subtract).then_inc(lowered, 1)
                v.wait_ge(lowered, m + 1)
                v.tensor_scalar(r.LA[:, m, :], r.LA[:, m, :], 1 / 16, None, ALU.mult).then_inc(done, 1)

            v.wait_ge(w_in, 32)
            for m in range(4):
                v.wait_ge(product, m + 1)
                for c in range(NB):
                    mm = v.tensor_scalar(r.LA[:, m, c * CW:(c + 1) * CW], r.ps[:, m % 2 * 3 + c, 0:CW], b2[:, m:m + 1],
                                         None, ALU.add)
                mm.then_inc(biased, 1)
                if m >= 2:
                    log_sigmoid(m - 2)
                v.wait_ge(biased, m + 1)
                v.scalar_tensor_tensor(out=az[:, m % 2, :], in0=r.LA[:, m, :], scalar=-1.0, in1=r.LA[:, m, :],
                                       op0=ALU.mult, op1=ALU.max).then_inc(absed, 1)
            log_sigmoid(2)
            log_sigmoid(3)

        @block.scalar
        def _(act):
            act.preload_act_table_set("natural_log_exp_and_others")
            for m in range(4):
                act.wait_ge(absed, m + 1)
                act.activation(az[:, m % 2, :], az[:, m % 2, :], ACT.Exp, scale=-1.0).then_inc(exped, 1)
                act.wait_ge(exped, m + 1)
                act.activation(az[:, m % 2, :], az[:, m % 2, :], ACT.Ln, bias=1.0).then_inc(logged, 1)
            act.activation(r.H[:, OR_:OR_ + 8, :], r.H[:, OR_:OR_ + 8, :], ACT.Silu)


def gla_prompt_phase(nc, r):
    H4 = range(HEADS)
    with phase(nc) as ctx:
        def sb(name, shape):
            return ctx.enter_context(nc.sbuf_tensor("gp_" + name, shape, F32))

        upper, keep16, one = sb("upper", [P, P]), sb("keep16", [P, P]), sb("one", [P, P])
        gn = sb("gn", [P, 2])
        VT, VK, OS = sb("vt", [P, 8, P]), sb("vk", [P, 8, P]), sb("os", [P, 8, P])
        B, BL, QL, QB, KD, KT, ATT, RO = [sb(n, [P, 4, P]) for n in ("b", "bl", "ql", "qb", "kd", "kt", "att", "ro")]
        BR = sb("br", [P, 4, 8])
        GL = sb("gl", [P, 4])
        EX = sb("ex", [P, 2, 8, P])
        S = sb("s", [P, 4, GV])
        names = ("tables_in", "chunk_done", "v_copied", "v_turned", "v_kept", "scanned", "ref_ready", "q_exped",
                 "kd_exped", "kd_ready", "kd_turned", "kd_kept", "q_ready", "ex_ready", "kx_ready", "att_ready",
                 "att_kept", "o_ready", "ds_ready", "s_ready", "o_squared", "o_summed", "o_logged", "ro_ready",
                 "o_scaled", "stored", "zeroed")
        (tables_in, chunk_done, v_copied, v_turned, v_kept, scanned, ref_ready, q_exped, kd_exped, kd_ready, kd_turned,
         kd_kept, q_ready, ex_ready, kx_ready, att_ready, att_kept, o_ready, ds_ready, s_ready, o_squared, o_summed,
         o_logged, ro_ready, o_scaled, stored, zeroed) = [nc.alloc_semaphore("gp_" + s) for s in names]
        block = ctx.enter_context(nc.Block())

        def bank(b):
            return r.ps[:, b, :].rearrange("p (h n) -> p h n", h=4)

        def pair(b):
            return r.ps[:, b:b + 2, :].rearrange("p b (h n) -> p (b h) n", h=4)

        @block.sync
        def _(sp):
            sp.dma_start(upper[:], r.c_upper).then_inc(tables_in, 16)
            sp.dma_start(gn[:], r.gla_ng).then_inc(tables_in, 16)
            sp.wait_ge(s_ready, TT + 1)
            sp.dma_start(r.o_gS_p[0, 0].rearrange("h d e -> d h e"), S[:]).then_inc(stored, 16)
            sp.wait_ge(stored, 16)

        @block.scalar
        def _(act):
            act.preload_act_table_set("natural_log_exp_and_others")
            act.wait_ge(zeroed, 1)
            with act.Fori(0, TT) as c:
                cols = bass.ds(c * P, P)
                act.wait_ge(chunk_done, c + 1)
                act.wait_ge(tables_in, 32)
                act.copy(VT[:], r.H[:, OV:OV + 8, cols]).then_inc(v_copied, 1)
                act.wait_ge(ref_ready, c + 1)
                act.activation(QL[:], BL[:], ACT.Exp)
                act.activation(QB[:], B[:], ACT.Exp).then_inc(q_exped, 1)
                act.activation(GL[:], B[:, :, P - 1], ACT.Exp)
                for h in H4:
                    mm = act.activation(KD[:, h, :], B[:, h, :], ACT.Exp, bias=B[:, h, P - 1:P], scale=-1.0)
                mm.then_inc(kd_exped, 1)
                act.wait_ge(v_turned, c + 1)
                act.copy(VK[:], pair(0)).then_inc(v_kept, 1)
                for h in H4:
                    if h >= 2:
                        act.wait_ge(att_ready, c * 4 + (h - 1))
                    for b in range(8):
                        mm = act.activation(EX[:, h % 2, b, 0:16 * (b + 1)], B[:, h, 0:16 * (b + 1)], ACT.Exp,
                                            bias=BR[:, h, b:b + 1], scale=-1.0)
                    mm.then_inc(ex_ready, 1)
                    if h == 1:
                        act.wait_ge(kd_turned, c + 1)
                        act.copy(KT[:], bank(2)).then_inc(kd_kept, 1)
                act.wait_ge(o_ready, c + 1)
                act.activation(OS[:], pair(4), ACT.Square).then_inc(o_squared, 1)
                act.wait_ge(o_summed, c + 1)
                act.activation(RO[:], bank(0), ACT.Ln, bias=r.bias[:, 1:2], scale=1 / GV).then_inc(o_logged, 1)
                act.wait_ge(o_logged, c + 1)
                act.activation(RO[:], RO[:], ACT.Exp, scale=-0.5).then_inc(ro_ready, 1)

        @block.tensor
        def _(pe):
            pe.wait_ge(tables_in, 32)
            with pe.Fori(0, TT) as c:
                pe.wait_ge(v_copied, c + 1)
                for j in range(8):
                    mm = pe.transpose(pair(0)[:, j, :], VT[:, j, :], r.ident[:])
                mm.then_inc(v_turned, 1)
                pe.wait_ge(kd_ready, c + 1)
                for h in H4:
                    mm = pe.transpose(bank(2)[:, h, :], KD[:, h, :], r.ident[:])
                mm.then_inc(kd_turned, 1)
                pe.wait_ge(q_ready, c + 1)
                for h in H4:
                    pe.wait_ge(kx_ready, c * 4 + (h + 1))
                    for b in range(8):
                        mm = pe.matmul(bank(3)[:, h, 16 * b:16 * b + 16], EX[:, h % 2, b, :],
                                       QL[:, h, 16 * b:16 * b + 16], start=True, stop=True)
                    mm.then_inc(att_ready, 1)
                pe.wait_ge(att_kept, c + 1)
                pe.wait_ge(s_ready, c + 1)
                pe.wait_ge(v_kept, c + 1)
                for h in H4:
                    for e in range(2):
                        pe.matmul(pair(4)[:, 2 * h + e, :], S[:, h, e * P:(e + 1) * P], QB[:, h, :], start=True,
                                  stop=False)
                        mm = pe.matmul(pair(4)[:, 2 * h + e, :], VK[:, 2 * h + e, :], ATT[:, h, :], start=False,
                                       stop=True)
                mm.then_inc(o_ready, 1)
                pe.wait_ge(kd_kept, c + 1)
                for h in H4:
                    mm = pe.matmul(pair(6)[:, 2 * h:2 * h + 2, :], KT[:, h, :], VK[:, 2 * h:2 * h + 2, :], start=True,
                                   stop=True)
                mm.then_inc(ds_ready, 1)
                pe.wait_ge(o_squared, c + 1)
                sq = OS[:].rearrange("p (h e) n -> p h e n", e=2)
                pe.matmul(r.ps[:, 0, :], r.ones[:], sq[:, :, 0, :], start=True, stop=False)
                pe.matmul(r.ps[:, 0, :], r.ones[:], sq[:, :, 1, :], start=False, stop=True).then_inc(o_summed, 1)

        @block.vector
        def _(v):
            v.memset(S[:], 0.0).then_inc(s_ready, 1)
            v.memset(EX[:], 0.0)
            v.memset(one[:], 1.0)
            v.memset(keep16[:], 1.0).then_inc(zeroed, 1)
            v.wait_ge(zeroed, 1)
            v.memset(keep16[:].rearrange("p (b t) -> p b t", t=16)[:, :, 0:1], 0.0).then_inc(zeroed, 1)
            v.wait_ge(zeroed, 2)
            v.wait_ge(tables_in, 32)
            v.sem_inc(chunk_done, 1)
            with v.Fori(0, TT) as c:
                cols = bass.ds(c * P, P)
                v.wait_ge(chunk_done, c + 1)
                for h in H4:
                    la = r.LA[:, h, cols]
                    v.tensor_tensor_scan(B[:, h, :], one[:], la, 0.0, ALU.mult, ALU.add)
                    mm = v.tensor_tensor_scan(BL[:, h, :], keep16[:], la, 0.0, ALU.mult, ALU.add)
                mm.then_inc(scanned, 1)
                v.wait_ge(scanned, c + 1)
                v.tensor_tensor(BR[:], B[:].rearrange("p h (b t) -> p h b t", t=16)[:, :, :, 0],
                                BL[:].rearrange("p h (b t) -> p h b t", t=16)[:, :, :, 0],
                                ALU.subtract).then_inc(ref_ready, 1)
                q, k = r.H[:, OQ:OQ + 4, cols], r.H[:, OK:OK + 4, cols]
                v.wait_ge(q_exped, c + 1)
                v.scalar_tensor_tensor(out=QL[:], in0=q, scalar=128 ** -0.5, in1=QL[:], op0=ALU.mult, op1=ALU.mult)
                v.scalar_tensor_tensor(out=QB[:], in0=q, scalar=128 ** -0.5, in1=QB[:], op0=ALU.mult,
                                       op1=ALU.mult).then_inc(q_ready, 1)
                v.wait_ge(kd_exped, c + 1)
                v.tensor_tensor(KD[:], k, KD[:], ALU.mult).then_inc(kd_ready, 1)
                for h in H4:
                    v.wait_ge(ex_ready, c * 4 + (h + 1))
                    v.tensor_tensor(EX[:, h % 2], EX[:, h % 2],
                                    r.H[:, OK + h, cols].unsqueeze(1).to_broadcast([P, 8, P]),
                                    ALU.mult).then_inc(kx_ready, 1)
                v.wait_ge(att_ready, c * 4 + 4)
                v.tensor_tensor(ATT[:], bank(3), upper[:].unsqueeze(1).to_broadcast([P, 4, P]),
                                ALU.mult).then_inc(att_kept, 1)
                v.wait_ge(ds_ready, c + 1)
                for h in H4:
                    mm = v.scalar_tensor_tensor(out=S[:, h, :], in0=S[:, h, :], scalar=GL[:, h:h + 1],
                                                in1=pair(6)[:, 2 * h:2 * h + 2, :].rearrange("p e n -> p (e n)"),
                                                op0=ALU.mult, op1=ALU.add)
                mm.then_inc(s_ready, 1)
                v.wait_ge(ro_ready, c + 1)
                out = OS[:].rearrange("p (h e) n -> p h e n", e=2)
                got = pair(4).rearrange("p (h e) n -> p h e n", e=2)
                for e in range(2):
                    mm = v.scalar_tensor_tensor(out=out[:, :, e, :], in0=got[:, :, e, :], scalar=gn[:, e:e + 1],
                                                in1=RO[:], op0=ALU.mult, op1=ALU.mult)
                mm.then_inc(o_scaled, 1)
                v.wait_ge(o_scaled, c + 1)
                v.tensor_tensor(r.H[:, OR_:OR_ + 8, cols], OS[:], r.H[:, OR_:OR_ + 8, cols],
                                ALU.mult).then_inc(chunk_done, 1)


def sample_state_phase(nc, r, delta):
    E = 1 if delta else 2
    tag = "ds_" if delta else "gs_"
    Qc, Kc, Vc, Oc = (Q_A, K_A, V_A, GATE_A) if delta else (OQ, OK, OV, OR_)
    state_in = r.state_delta_S[0] if delta else r.state_gla_S[0]
    state_out = r.o_dS_s[0] if delta else r.o_gS_s[0]
    q, k = r.H[:, Qc:Qc + 4, T:N], r.H[:, Kc:Kc + 4, T:N]
    val, gate = r.H[:, Vc:Vc + 4 * E, T:N], r.H[:, Oc:Oc + 4 * E, T:N]
    with phase(nc) as ctx:
        def sb(name, shape):
            return ctx.enter_context(nc.sbuf_tensor(tag + name, shape, F32))

        S = sb("s", [P, NS, 4, E * P])
        tmp = r.H[:, Kc:Kc + 2, 0:4 * E * P].rearrange("p u (h e) -> p u h e", h=4)
        pick, ng = sb("pick", [NS, NS, P]), sb("ng", [P, E])
        qn, kn, dec, kw, prod, qk = [sb(n, [P, 4, NS]) for n in ("qn", "kn", "dec", "kw", "prod", "qk")]
        sq, rn = sb("sq", [P, 8, NS]), sb("rn", [P, 8, NS])
        vn, o, os_ = sb("vn", [P, 4 * E, NS]), sb("o", [P, 4 * E, NS]), sb("os", [P, 4 * E, NS])
        vrow = r.H[0:NS, Kc + 2, 0:4 * E * P]
        ro = sb("ro", [P, 4, NS])
        rowsel = sb("rowsel", [NSMALL, 8, P]) if delta else None
        bb = sb("bb", [P, 8, NS])
        s_in = [nc.alloc_semaphore(tag + f"s_in{i}") for i in range(NS)]
        tables_in, act_step, dve_step, pe_step, spread, outer, moved, stored = [
            nc.alloc_semaphore(tag + s) for s in
            ("tables_in", "act_step", "dve_step", "pe_step", "spread", "outer", "moved", "stored")]
        block = ctx.enter_context(nc.Block())
        nt = 3 if delta else 2

        def small(b, n):
            return r.ps[:, b, 0:n * NS].rearrange("p (h s) -> p h s", s=NS)

        @block.sync
        def _(sp):
            sp.dma_start(pick[:].rearrange("p s n -> p (s n)"), r.c_pick).then_inc(tables_in, 16)
            sp.dma_start(ng[:], r.delta_ng if delta else r.gla_ng).then_inc(tables_in, 16)
            if delta:
                sp.dma_start(rowsel[:].rearrange("p l n -> p (l n)"), r.c_rowsel).then_inc(tables_in, 16)
            for s in range(NS):
                sp.dma_start(S[:, s], state_in[s].rearrange("h d e -> d h e")).then_inc(s_in[s], 16)
            for s in range(NS):
                sp.wait_ge(moved, s + 1)
                sp.dma_start(state_out[s].rearrange("h d e -> d h e"), S[:, s]).then_inc(stored, 16)
            sp.wait_ge(stored, 16 * NS)

        @block.scalar
        def _(act):
            act.preload_act_table_set("natural_log_exp_and_others")
            act.wait_ge(tables_in, 16 * nt)
            if delta:
                act.activation(sq[:], r.H[:, Qc:Qc + 8, T:N], ACT.Square).then_inc(act_step, 1)
                act.wait_ge(pe_step, 1)
                act.activation(rn[:], small(0, 8), ACT.Ln, bias=r.bias[:, 1:2]).then_inc(act_step, 1)
                act.wait_ge(act_step, 2)
                act.activation(rn[:], rn[:], ACT.Exp, scale=-0.5)
                act.activation(dec[:], small(1, 8)[:, 4:8, :], ACT.Exp)
                act.copy(bb[:], small(1, 8)).then_inc(act_step, 1)
            else:
                act.activation(dec[:], r.LA[:, :, T:N], ACT.Exp).then_inc(act_step, 1)
                act.sem_inc(act_step, 2)
            act.wait_ge(pe_step, 4)
            for j in range(E):
                mm = act.copy(vrow[:, j * 512:(j + 1) * 512], r.ps[0:NS, 4 + j, :])
            mm.then_inc(act_step, 1)
            for s in range(NS):
                act.wait_ge(spread, s + 1)
                if s >= 2:
                    act.wait_ge(moved, s - 1)
                for h in range(4):
                    src = r.ps[:, s % 2 * 2:s % 2 * 2 + E, :].rearrange("p b n -> p (b n)")[:, h * E * P:(h + 1) * E * P]
                    mm = act.activation(tmp[:, s % 2, h, :], src, ACT.Copy, scale=kn[:, h, s:s + 1])
                mm.then_inc(outer, 1)
            act.wait_ge(dve_step, 6)
            act.activation(os_[:], o[:], ACT.Square).then_inc(act_step, 1)
            act.wait_ge(pe_step, 5)
            act.activation(ro[:], small(7, 4), ACT.Ln, bias=r.bias[:, 1:2], scale=1 / (E * P)).then_inc(act_step, 1)
            act.wait_ge(act_step, 6)
            act.activation(ro[:], ro[:], ACT.Exp, scale=-0.5).then_inc(act_step, 1)

        @block.vector
        def _(v):
            v.wait_ge(tables_in, 16 * nt)
            v.wait_ge(act_step, 3)
            if delta:
                v.scalar_tensor_tensor(out=qn[:], in0=q, scalar=128 ** -0.5, in1=rn[:, 0:4, :], op0=ALU.mult,
                                       op1=ALU.mult)
                v.tensor_tensor(kn[:], k, rn[:, 4:8, :], ALU.mult).then_inc(dve_step, 1)
                v.wait_ge(dve_step, 1)
                v.tensor_tensor(prod[:], qn[:], kn[:], ALU.mult)
                v.tensor_tensor(kw[:], kn[:], dec[:], ALU.mult).then_inc(dve_step, 1)
                v.wait_ge(dve_step, 2)
                v.tensor_tensor(kw[:], kw[:], bb[:, 0:4, :], ALU.mult)
                v.tensor_tensor(qn[:], qn[:], dec[:], ALU.mult)
                v.tensor_tensor(vn[:], val, bb[:, 0:4, :], ALU.mult).then_inc(dve_step, 1)
            else:
                v.tensor_copy(kn[:], k)
                v.tensor_scalar(qn[:], q, 128 ** -0.5, None, ALU.mult).then_inc(dve_step, 1)
                v.wait_ge(dve_step, 1)
                v.tensor_tensor(prod[:], qn[:], k, ALU.mult).then_inc(dve_step, 1)
                v.wait_ge(dve_step, 2)
                v.tensor_tensor(qn[:], qn[:], dec[:], ALU.mult)
                v.tensor_copy(vn[:], val).then_inc(dve_step, 1)
            v.wait_ge(pe_step, 2)
            mm = v.tensor_copy(qk[:], small(6, 4))
            if delta:
                mm = v.tensor_tensor(vn[:], vn[:], small(2, 4), ALU.subtract)
            mm.then_inc(dve_step, 1)
            v.wait_ge(dve_step, 4)
            v.wait_ge(pe_step, 3)
            v.tensor_tensor(o[:].rearrange("p (h e) s -> p h e s", e=E), vn[:].rearrange("p (h e) s -> p h e s", e=E),
                            qk[:].unsqueeze(2).to_broadcast([P, 4, E, NS]), ALU.mult).then_inc(dve_step, 1)
            v.wait_ge(dve_step, 5)
            v.tensor_tensor(o[:], o[:], small(3, 4 * E), ALU.add).then_inc(dve_step, 1)
            for s in range(NS):
                v.wait_ge(outer, s + 1)
                for h in range(4):
                    mm = v.scalar_tensor_tensor(out=S[:, s, h, :], in0=S[:, s, h, :], scalar=dec[:, h, s:s + 1],
                                                in1=tmp[:, s % 2, h, :], op0=ALU.mult, op1=ALU.add)
                mm.then_inc(moved, 1)
            v.wait_ge(act_step, 7)
            ov = o[:].rearrange("p (h e) s -> p h e s", e=E)
            for e in range(E):
                mm = v.scalar_tensor_tensor(out=ov[:, :, e, :], in0=ov[:, :, e, :], scalar=ng[:, e:e + 1], in1=ro[:],
                                            op0=ALU.mult, op1=ALU.mult)
            mm.then_inc(dve_step, 1)
            v.wait_ge(dve_step, 7)
            v.tensor_tensor(gate, gate, o[:], ALU.mult)

        @block.tensor
        def _(pe):
            pe.wait_ge(tables_in, 16 * nt)
            if delta:
                pe.wait_ge(act_step, 1)
                pe.matmul(r.ps[:, 0, 0:8 * NS], r.ones[:], sq[:], start=True, stop=True)
                for j in range(8):
                    mm = pe.matmul(small(1, 8)[:, j, :], rowsel[:, j, :], r.H[0:NSMALL, SMALL, T:N], start=True,
                                   stop=True)
                mm.then_inc(pe_step, 1)
            else:
                pe.sem_inc(pe_step, 1)
            pe.wait_ge(dve_step, 3)
            pe.matmul(r.ps[:, 6, 0:4 * NS], r.ones[:], prod[:], start=True, stop=True)
            for s in range(NS):
                pe.wait_ge(s_in[s], 16)
                if delta:
                    for h in range(4):
                        pe.matmul(small(2, 4)[:, h, s:s + 1], S[:, s, h, :], kw[:, h, s:s + 1], start=True, stop=True)
            pe.matmul(r.ps[:, 7, 0:4 * NS], r.ones[:], prod[:], start=True, stop=True).then_inc(pe_step, 1)
            for s in range(NS):
                for h in range(4):
                    for e in range(E):
                        mm = pe.matmul(small(3, 4 * E)[:, h * E + e, s:s + 1], S[:, s, h, e * P:(e + 1) * P],
                                       qn[:, h, s:s + 1], start=True, stop=True)
            mm.then_inc(pe_step, 1)
            pe.wait_ge(dve_step, 4)
            for j in range(4 * E):
                mm = pe.transpose(r.ps[0:NS, 4 + j // 4, j % 4 * P:(j % 4 + 1) * P], vn[:, j, :], r.ident[:])
            mm.then_inc(pe_step, 1)
            pe.wait_ge(act_step, 4)
            pe.wait_ge(dve_step, 6)
            for s in range(NS):
                if s >= 2:
                    pe.wait_ge(outer, s - 1)
                for j in range(E):
                    mm = pe.matmul(r.ps[:, s % 2 * 2 + j, :], pick[:, s, :], vrow[:, j * 512:(j + 1) * 512],
                                   start=True, stop=True)
                mm.then_inc(spread, 1)
            pe.wait_ge(act_step, 5)
            if delta:
                pe.matmul(r.ps[:, 7, 0:4 * NS], r.ones[:], os_[:], start=True, stop=True).then_inc(pe_step, 1)
            else:
                ov = os_[:].rearrange("p (h e) s -> p h e s", e=2)
                pe.matmul(r.ps[:, 7, 0:4 * NS], r.ones[:], ov[:, :, 0, :], start=True, stop=False)
                pe.matmul(r.ps[:, 7, 0:4 * NS], r.ones[:], ov[:, :, 1, :], start=False,
                          stop=True).then_inc(pe_step, 1)


def nsa_sample_phase(nc, r):
    flat = r.H[:].rearrange("p k n -> p (k n)")
    R = 64
    cache = r.cache.rearrange("n e t c g d -> (n e) t (c g d)")
    n_pool = r.cache.shape[0]
    win = r.state_nsa_win[0].rearrange("b (j p) c g d -> b p j c (g d)", p=P)
    at = [0]

    def room(rows, n):
        at[0] += n
        assert at[0] <= 12 * N
        return flat[0:rows, at[0] - n:at[0]]

    PAST = PAGES * P
    SC, SW = room(R, PAST + 1), room(R, 513)
    PT = room(P, 37 * R).rearrange("p (n q) -> p n q", q=R)
    KC, VCT, VC = [room(P, NS * P).rearrange("p (s n) -> p s n", s=NS) for _ in range(3)]
    KT = room(P, 1024).rearrange("p (u n) -> p u n", u=2)
    Q = room(P, NS * R)
    Qs = Q.rearrange("p (s q) -> p s q", s=NS)
    with phase(nc) as ctx:
        def sb(name, shape, dt=F32):
            return ctx.enter_context(nc.sbuf_tensor("ns_" + name, shape, dt))

        KP, VP = sb("kp", [P, 4, PGRP, 384]), sb("vp", [P, NG + 1, PGRP, P])
        pages = sb("pages", [1, NS * PAGES], I32)
        pool, group, own, headrow = sb("pool", [P, 4]), sb("group", [R, R]), sb("own", [NS, R]), sb("headrow", [R, 8])
        PC, G24, gates = sb("pc", [R, P]), sb("g24", [R, 8, 3]), sb("gates", [R, 3])
        pick, top8, mask = sb("pick", [R, 72]), sb("top8", [R, 8]), sb("mask", [R, 64])
        top, ntop, den, coef = sb("top", [R, 3]), sb("ntop", [R, 3]), sb("den", [R, 3]), sb("coef", [R, 3])
        pn, diag = sb("pn", [NS, 2, R]), sb("diag", [R, 2, R])
        O = sb("o", [P, R])
        pages_in, tables_in, page_ok, q_ready, k_turned, kt_kept, kt_used, pooled, pool_kept, sc_kept, stored = [
            nc.alloc_semaphore("ns_" + s) for s in
            ("pages_in", "tables_in", "page_ok", "q_ready", "k_turned", "kt_kept", "kt_used", "pooled", "pool_kept",
             "sc_kept", "stored")]
        kp_in = [nc.alloc_semaphore(f"ns_kp_in{u}") for u in range(4)]
        vp_in = [nc.alloc_semaphore(f"ns_vp_in{u}") for u in range(NG + 1)]
        kp_in2 = [nc.alloc_semaphore(f"ns_kp_in2_{u}") for u in range(4)]
        vp_in2 = [nc.alloc_semaphore(f"ns_vp_in2_{u}") for u in range(NG)]
        pe_step, dve_step, act_step, pt_turned, pt_kept, vp_used, o_ready = [
            nc.alloc_semaphore("ns_" + s) for s in
            ("pe_step", "dve_step", "act_step", "pt_turned", "pt_kept", "vp_used", "o_ready")]
        block = ctx.enter_context(nc.Block())
        kp_past = NG * 2 * 32

        def fetch(eng, mine, kp_in, vp_in):
            eng.wait_ge(pages_in, 16)

            def page(index):
                return eng.value_load(pages[0:1, bass.ds(index, 1)], min_val=0, max_val=n_pool - 1)

            with eng.Fori(0, NG) as c:
                for s in range(NS):
                    eng.wait_ge(k_turned, c * NS + (s + 1))
                    for j in mine:
                        eng.dma_start(KP[:, s % 4, j, :],
                                      cache[bass.ds(page(c * PGRP + (s * PAGES + j)), 1), :, 0:384].squeeze(0)
                                      ).then_inc(kp_in[s % 4], 16)
            if 0 in mine:
                for s in range(NS):
                    eng.wait_ge(k_turned, NG * NS + s + 1)
                    eng.dma_start(KP[:, s % 4, :, 256:384], win[s, :, :, 0, :]).then_inc(kp_in[s % 4], 16)
            with eng.Fori(0, NS) as s:
                for g in range(NG):
                    eng.wait_ge(vp_used, s * (NG + 1) + (g + 1))
                    for j in mine:
                        eng.dma_start(VP[:, g, j, :],
                                      cache[bass.ds(page(s * PAGES + (g * PGRP + j)), 1), :, 384:512].squeeze(0)
                                      ).then_inc(vp_in[g], 16)
                if 0 in mine:
                    eng.wait_ge(vp_used, s * (NG + 1) + (NG + 1))
                    eng.dma_start(VP[:, NG, :, :], win[bass.ds(s, 1), :, :, 1, :].squeeze(0)).then_inc(vp_in[NG], 16)

        @block.sync
        def _(sp):
            sp.dma_start(pages[:], r.page_table.rearrange("(a b) n -> a (b n)", a=1)).then_inc(pages_in, 16)
            for dst, src in ((pool[:], r.c_pool), (group[:], r.c_group), (own[:], r.c_own), (headrow[:], r.c_headrow)):
                sp.dma_start(dst, src).then_inc(tables_in, 16)
            fetch(sp, (0, 1), kp_in, vp_in)

        @block.gpsimd
        def _(pool_):
            fetch(pool_, (2, 3), kp_in2, vp_in2)

        @block.tensor
        def _(pe):
            pe.wait_ge(tables_in, 64)
            pe.wait_ge(q_ready, 1)
            pe.sem_inc(k_turned, 4)
            pe.sem_inc(kt_used, 2)
            pe.sem_inc(vp_used, NG + 1)

            def turn(c, s, past):
                pe.wait_ge(kp_in[s % 4], c * 64 + (s // 4 + 1) * 32 if past else kp_past + (s // 4 + 1) * 16)
                if past:
                    pe.wait_ge(kp_in2[s % 4], c * 64 + (s // 4 + 1) * 32)
                    pe.wait_ge(pool_kept, c * NS + (s + 1))
                    for part in range(2):
                        for j in range(PGRP):
                            mm = pe.matmul(r.ps[:, 4 + s % 2, 16 * part + 4 * j:16 * part + 4 * j + 4],
                                           KP[:, s % 4, j, part * P:(part + 1) * P], pool[:], start=True, stop=True)
                    mm.then_inc(pooled, 1)
                pe.wait_ge(kt_kept, c * NS + (s + 1))
                for j in range(PGRP):
                    mm = pe.transpose(r.ps[:, s % 2, j * P:(j + 1) * P], KP[:, s % 4, j, 256:384], r.ident[:])
                mm.then_inc(k_turned, 1)

            def scores(c, s):
                pe.wait_ge(kt_kept, c * NS + (s + 3))
                if s == 0:
                    pe.wait_ge(sc_kept, c + 1)
                pe.matmul(r.ps[0:R, 2, :], Qs[:, s, :], KT[:, s % 2, :], start=(s == 0),
                          stop=(s == NS - 1)).then_inc(kt_used, 1)

            def sweep(c, past):
                turn(c, 0, past)
                for s in range(NS):
                    if s + 1 < NS:
                        turn(c, s + 1, past)
                    scores(c, s)

            with pe.Fori(0, NG) as c:
                sweep(c, True)
            sweep(NG, False)
            pe.wait_ge(pool_kept, NG * NS + 2)
            for s in range(NS):
                pe.matmul(r.ps[0:R, 3, 0:1], Qs[:, s, :], r.H[:, K_SEL, T + s:T + s + 1], start=(s == 0),
                          stop=(s == NS - 1))
            for s in range(NS):
                pe.matmul(r.ps[0:R, 3, 1:2], Qs[:, s, :], r.H[:, K_WIN, T + s:T + s + 1], start=(s == 0),
                          stop=(s == NS - 1))
            for s in range(NS):
                pe.matmul(r.ps[0:R, 3, P:2 * P], Qs[:, s, :], KC[:, s, :], start=(s == 0), stop=(s == NS - 1))
            pe.matmul(r.ps[0:R, 3, 32:56], own[:], r.tok[0:NS, 8, R_NSA:R_NSA + 24], start=True,
                      stop=True).then_inc(pe_step, 1)
            for s in range(NS):
                mm = pe.transpose(r.ps[:, s // 4, s % 4 * P:(s % 4 + 1) * P], VCT[:, s, :], r.ident[:])
            mm.then_inc(pe_step, 1)
            pe.wait_ge(dve_step, 4)
            pe.matmul(r.ps[0:R, 4, 0:P], group[:], PC[:], start=True, stop=True).then_inc(pe_step, 1)
            pe.wait_ge(dve_step, 15)
            for j in range(2):
                mm = pe.matmul(r.ps[0:NS, 4, 256 + R * j:256 + R * (j + 1)], r.ones[0:R, 0:NS], diag[:, j, :],
                               start=True, stop=True)
            mm.then_inc(pe_step, 1)
            pe.wait_ge(act_step, 3)
            for b in range(5):
                if b >= 2:
                    pe.wait_ge(pt_kept, b - 1)
                for n in range(8 * b, min(8 * b + 8, 37)):
                    src = SC[:, n * P:(n + 1) * P] if n < 32 else SW[:, (n - 32) * P:(n - 31) * P] if n < 36 else PC[:]
                    mm = pe.transpose(r.ps[:, b % 2, n % 8 * R:(n % 8 + 1) * R], src, r.ident[0:R, 0:R])
                mm.then_inc(pt_turned, 1)
            pe.wait_ge(pt_kept, 5)
            for s in range(NS):
                pe.matmul(r.ps[:, 7, s * 8:s * 8 + 8], VC[:, s, :], PT[:, 36, s * 8:s * 8 + 8], start=True, stop=True)
            pe.wait_ge(dve_step, 16)
            pe.matmul(r.ps[:, 5, 0:R], r.srows[0:NS, 384:512], pn[:, 0, :], start=True, stop=False)
            pe.matmul(r.ps[:, 5, 0:R], r.srows[0:NS, 640:768], pn[:, 1, :], start=False, stop=True)
            with pe.Fori(0, NS) as s:
                for g in range(NG + 1):
                    pe.wait_ge(vp_in[g], s * 32 + 32 if g < NG else s * 16 + 16)
                    if g < NG:
                        pe.wait_ge(vp_in2[g], s * 32 + 32)
                    for j in range(PGRP):
                        mm = pe.matmul(r.ps[:, 6, bass.ds(s * 8, 8)], VP[:, g, j, :],
                                       PT[:, 4 * g + j, bass.ds(s * 8, 8)], start=(g == 0 and j == 0),
                                       stop=(g == NG and j == PGRP - 1))
                    mm.then_inc(vp_used, 1)

        @block.scalar
        def _(act):
            act.sem_inc(kt_kept, 2)
            with act.Fori(0, NG) as c:
                for s in range(NS):
                    act.wait_ge(k_turned, c * NS + (s + 5))
                    act.wait_ge(kt_used, c * NS + (s + 1))
                    act.copy(KT[:, s % 2, :], r.ps[:, s % 2, :]).then_inc(kt_kept, 1)
            for s in range(NS):
                act.wait_ge(k_turned, NG * NS + (s + 5))
                act.wait_ge(kt_used, NG * NS + (s + 1))
                act.copy(KT[:, s % 2, :], r.ps[:, s % 2, :]).then_inc(kt_kept, 1)
            act.wait_ge(dve_step, 2)
            act.activation(PC[:], r.ps[0:R, 3, P:2 * P], ACT.Exp, bias=ntop[:, 0:1], scale=0.125,
                           accum_out=den[:, 0:1]).then_inc(act_step, 1)
            act.wait_ge(pe_step, 2)
            act.copy(VC[:, 0:4, :].rearrange("p s n -> p (s n)"), r.ps[:, 0, :])
            act.copy(VC[:, 4:8, :].rearrange("p s n -> p (s n)"), r.ps[:, 1, :]).then_inc(act_step, 1)
            act.wait_ge(dve_step, 12)
            act.activation(SC[:], SC[:], ACT.Exp, bias=ntop[:, 1:2], scale=0.125, accum_out=den[:, 1:2])
            act.activation(SW[:], SW[:], ACT.Exp, bias=ntop[:, 2:3], scale=0.125,
                           accum_out=den[:, 2:3]).then_inc(act_step, 1)
            for b in range(5):
                n = min(8, 37 - 8 * b)
                act.wait_ge(pt_turned, b + 1)
                act.copy(PT[:, 8 * b:8 * b + n, :].rearrange("p n q -> p (n q)"),
                         r.ps[:, b % 2, 0:n * R]).then_inc(pt_kept, 1)

        @block.vector
        def _(v):
            v.sem_inc(pool_kept, 2)
            v.sem_inc(sc_kept, 1)
            v.memset(Q, 0.0).then_inc(dve_step, 1)
            v.wait_ge(dve_step, 1)
            for i in range(4):
                for g in range(2):
                    h = i + 4 * g
                    mm = v.tensor_copy(Q[64 * g:64 * g + 64, h:h + 72 * (NS - 1) + 1:72],
                                       r.H[64 * g:64 * g + 64, Q_B + i, T:N])
            mm.then_inc(q_ready, 1)
            with v.Fori(0, NG) as c:
                for s in range(NS):
                    v.wait_ge(pooled, c * NS + (s + 1))
                    v.tensor_copy(KC[:, s, bass.ds(c * 16, 16)], r.ps[:, 4 + s % 2, 0:16])
                    v.tensor_copy(VCT[:, s, bass.ds(c * 16, 16)], r.ps[:, 4 + s % 2, 16:32]).then_inc(pool_kept, 1)
                v.wait_ge(kt_used, c * NS + (NS + 2))
                v.tensor_copy(SC[:, bass.ds(c * 512, 512)], r.ps[0:R, 2, :]).then_inc(sc_kept, 1)
            v.wait_ge(kt_used, NG * NS + (NS + 2))
            v.tensor_copy(SW[:, 0:512], r.ps[0:R, 2, :]).then_inc(sc_kept, 1)
            v.wait_ge(pe_step, 1)
            v.wait_ge(sc_kept, NG + 2)
            v.memset(SW[:, 0:1], NEG)
            v.tensor_copy(SC[:, PAST:PAST + 1], r.ps[0:R, 3, 0:1])
            v.tensor_copy(SW[:, 512:513], r.ps[0:R, 3, 1:2])
            v.tensor_tensor(G24[:], r.ps[0:R, 3, 32:56].rearrange("p (h b) -> p h b", b=3),
                            headrow[:].unsqueeze(2).to_broadcast([R, 8, 3]), ALU.mult)
            v.tensor_reduce(top[:, 0:1], r.ps[0:R, 3, P:2 * P], AX.X, ALU.max).then_inc(sc_kept, 1)
            v.wait_ge(sc_kept, NG + 3)
            v.tensor_reduce(gates[:], G24[:].rearrange("p h b -> p b h"), AX.X, ALU.add)
            v.tensor_reduce(top[:, 2:3], SW[:], AX.X, ALU.max)
            v.tensor_scalar(ntop[:, 0:1], top[:, 0:1], -0.125, None, ALU.mult).then_inc(dve_step, 1)
            v.wait_ge(act_step, 1)
            v.reciprocal(coef[:, 0:1], den[:, 0:1]).then_inc(dve_step, 1)
            v.wait_ge(dve_step, 3)
            v.tensor_scalar(PC[:], PC[:], coef[:, 0:1], None, ALU.mult).then_inc(dve_step, 1)
            v.memset(pick[:], NEG).then_inc(dve_step, 1)
            v.wait_ge(dve_step, 5)
            v.wait_ge(pe_step, 3)
            v.tensor_scalar(PC[:], PC[:], gates[:, 0:1], None, ALU.mult)
            v.tensor_reduce(pick[:, 0:64], r.ps[0:R, 4, 0:P].rearrange("p (b c) -> p b c", c=2), AX.X,
                            ALU.add).then_inc(dve_step, 1)
            v.wait_ge(dve_step, 6)
            v.memset(pick[:, 0:1], 1e9)
            v.memset(pick[:, 63:65], 1e9).then_inc(dve_step, 1)
            v.wait_ge(dve_step, 7)
            for n in range(2):
                v.max(top8[:], pick[:]).then_inc(dve_step, 1)
                v.wait_ge(dve_step, 8 + 2 * n)
                v.match_replace(pick[:], top8[:], pick[:], -3e38).then_inc(dve_step, 1)
                v.wait_ge(dve_step, 9 + 2 * n)
            v.tensor_scalar(mask[:], pick[:, 0:64], -2e38, NEG, ALU.is_gt, ALU.mult).then_inc(sc_kept, 1)
            v.wait_ge(sc_kept, NG + 4)
            sv = SC[:, 0:PAST].rearrange("p (b n) -> p b n", n=64)
            v.tensor_tensor(sv, sv, mask[:].unsqueeze(2).to_broadcast([R, 64, 64]), ALU.add).then_inc(sc_kept, 1)
            v.wait_ge(sc_kept, NG + 5)
            v.tensor_reduce(top[:, 1:2], SC[:], AX.X, ALU.max).then_inc(sc_kept, 1)
            v.wait_ge(sc_kept, NG + 6)
            v.tensor_scalar(ntop[:, 1:3], top[:, 1:3], -0.125, None, ALU.mult).then_inc(dve_step, 1)
            v.wait_ge(act_step, 3)
            v.reciprocal(coef[:, 1:3], den[:, 1:3]).then_inc(dve_step, 1)
            v.wait_ge(dve_step, 13)
            v.tensor_tensor(coef[:, 1:3], coef[:, 1:3], gates[:, 1:3], ALU.mult).then_inc(dve_step, 1)
            v.wait_ge(dve_step, 14)
            v.tensor_scalar(SC[:], SC[:], coef[:, 1:2], None, ALU.mult)
            v.tensor_scalar(SW[:], SW[:], coef[:, 2:3], None, ALU.mult).then_inc(sc_kept, 1)
            v.wait_ge(sc_kept, NG + 7)
            v.tensor_scalar(diag[:, 0, :], r.ident[0:R, 0:R], SC[:, PAST:PAST + 1], None, ALU.mult)
            v.tensor_scalar(diag[:, 1, :], r.ident[0:R, 0:R], SW[:, 512:513], None,
                            ALU.mult).then_inc(dve_step, 1)
            v.wait_ge(pe_step, 4)
            v.tensor_tensor(pn[:], r.ps[0:NS, 4, 256:256 + 2 * R].rearrange("p (j q) -> p j q", j=2),
                            own[:].unsqueeze(1).to_broadcast([NS, 2, R]), ALU.mult).then_inc(dve_step, 1)
            v.wait_ge(vp_used, (NG + 1) * (NS + 1))
            v.tensor_copy(O[:], r.ps[:, 6, 0:R]).then_inc(dve_step, 1)
            v.wait_ge(dve_step, 17)
            v.tensor_tensor(O[:], O[:], r.ps[:, 7, 0:R], ALU.add).then_inc(dve_step, 1)
            v.wait_ge(dve_step, 18)
            v.tensor_tensor(O[:], O[:], r.ps[:, 5, 0:R], ALU.add).then_inc(dve_step, 1)
            v.wait_ge(dve_step, 19)
            for g in range(2):
                v.tensor_copy(r.H[64 * g:64 * g + 64, Q_B:Q_B + 4, T:N],
                              O[64 * g:64 * g + 64, :].rearrange("p (s h) -> p h s", h=8)[:, 4 * g:4 * g + 4, :])



def build(nc, a, outs):
    r = Res()
    (r.o_y_p, r.o_y_s, r.o_rows_p, r.o_win_p, r.o_conv_p, r.o_dS_p, r.o_gS_p, r.o_rows_s, r.o_win_s, r.o_conv_s,
     r.o_dS_s, r.o_gS_s) = outs
    r.x_prompt, r.x_sample = a["x_prompt"], a["x_sample"]
    r.cache, r.state_nsa_win, r.state_delta_conv = a["cache_nsa_kv"], a["state_nsa_win"], a["state_delta_conv"]
    r.state_delta_S, r.state_gla_S, r.page_table = a["state_delta_S"], a["state_gla_S"], a["page_table"]
    r.dt_bias, r.A_log = a["delta_dt_bias"], a["delta_A_log"]
    r.conv_w, r.delta_ng = a["conv_w_delta"], a["delta_norm_g"]
    r.c_causal, r.c_oldest, r.c_cmp_add, r.c_cmp_one = a["c_causal"], a["c_oldest"], a["c_cmp_add"], a["c_cmp_one"]
    r.c_level, r.c_upper, r.c_rowsel = a["c_level"], a["c_upper"], a["c_rowsel"]
    r.c_pick, r.gla_ng, r.b_g2, r.w_g2 = a["c_pick"], a["gla_norm_g"], a["b_gla_gate2"], a["w_gla_gate2"][0]
    r.c_pool, r.c_group, r.c_own, r.c_headrow = a["c_pool"], a["c_group"], a["c_own"], a["c_headrow"]
    r.w_ffn_gate, r.w_ffn_up = a["w_ffn_gate"], a["w_ffn_up"]
    with ExitStack() as ctx:
        def sb(name, shape, dt=F32):
            return ctx.enter_context(nc.sbuf_tensor(name, shape, dt))

        r.X = sb("X", [P, KD, N])
        r.ps = ctx.enter_context(nc.psum_tensor("ps", [P, 8, 512], F32))
        r.ident = sb("ident", [P, P])
        r.ones, r.ones_d = sb("ones", [P, P]), sb("ones_d", [P, P])
        r.bias = sb("bias", [P, 2])
        r.lng, r.lnb = sb("lng", [P, 4 * KD]), sb("lnb", [P, 4 * KD])
        r.const_loads = [(r.ident[:], a["c_ident"]),
                         (r.lng[:], a["ln_g"]),
                         (r.lnb[:], a["ln_b"])]
        load_phase(nc, r)
        r.H = sb("H", [P, 27, N])

        def view(w):
            return w.rearrange("(k p) n -> p k n", p=P)

        def whole(w):
            half = w.shape[1] // 2
            return lambda m, u, shift: [
                ((slice(None), slice(s, s + half), slice(None)), w[:, s:s + half, bass.ds(m * P + shift, P)])
                for s in (0, half)]

        w_even = view(a["w_in_even"][0])

        def load_even(m, u, shift):
            if shift is None:
                c0 = 2056 + 64 * (m - 16)
                return [((slice(None), slice(None), slice(64 * g, 64 * g + 64)),
                         w_even[:, :, c0 + 256 * g:c0 + 256 * g + 64]) for g in range(2)]
            return whole(w_even)(m, u, shift)

        even_chunks = [(0, 12, 0), (12, 16, 8), (16, 20, None), (20, 26, 8)]
        every = slice(None)
        even_small = (NSMALL, [((every, every, slice(R_BETA, R_BETA + 4)), w_even[:, :, 1536:1540]),
                               ((every, every, slice(R_G, R_G + 4)), w_even[:, :, 1540:1544]),
                               ((every, every, slice(R_NSA, R_NSA + 24)), w_even[:, :, 3336:3360])])
        project_phase(nc, r, "in_even", r.X, KD, even_chunks, load_even, r.H, small=even_small)
        with ExitStack() as even:
            r.tok = even.enter_context(nc.sbuf_tensor("tok", [P, 9, NSMALL], F32))
            r.bufT = even.enter_context(nc.sbuf_tensor("bufT", [P, 12, 24], F32))
            r.srows = even.enter_context(nc.sbuf_tensor("srows", [NS, 768], F32))
            with nc.sbuf_tensor("rows", [P, TT, 768], F32) as rows:
                r.rows = rows
                even_rows_phase(nc, r)
                gates_phase(nc, r)
                nsa_prompt_phase(nc, r)
            conv_phase(nc, r)
            delta_prompt_phase(nc, r)
            sample_state_phase(nc, r, True)
            nsa_sample_phase(nc, r)
        w_out = view(a["w_out_even"][0])

        def load_out_even(m, u, shift):
            cols = bass.ds(m * P, P)
            tail = a["w_out_even"][0, 512:1024].rearrange("(g i p) n -> g p i n", g=2, p=64)
            return [((every, slice(0, 4), every), w_out[:, 0:4, cols]),
                    ((slice(0, 64), slice(4, 8), every), tail[0][:, :, cols]),
                    ((slice(64, 128), slice(4, 8), every), tail[1][:, :, cols])]

        project_phase(nc, r, "out_even", r.H[:, GATE_A:GATE_A + 8, :], KD, [(0, 8, 0)], load_out_even, r.X,
                      residual=True)
        norm_phase(nc, r, 0, 0)
        ffn_up_phase(nc, r, 0)
        project_phase(nc, r, "down0", r.H, KF, [(0, 8, 0)], whole(view(a["w_ffn_down"][0])), r.X, residual=True)
        norm_phase(nc, r, 0, 1)
        w_odd = view(a["w_in_odd"][0])
        project_phase(nc, r, "in_odd", r.X, KD, [(0, 16, 0), (16, 24, 16)], whole(w_odd), r.H,
                      small=(32, [((every, every, slice(0, 16)), w_odd[:, :, 2048:2064])]))
        with nc.sbuf_tensor("LA", [P, 4, N], F32) as log_decay:
            r.LA = log_decay
            gla_gate_phase(nc, r)
            gla_prompt_phase(nc, r)
            sample_state_phase(nc, r, False)
        project_phase(nc, r, "out_odd", r.H[:, OR_:OR_ + 8, :], KD, [(0, 8, 0)], whole(view(a["w_out_odd"][0])), r.X,
                      residual=True)
        norm_phase(nc, r, 1, 0)
        ffn_up_phase(nc, r, 1)
        project_phase(nc, r, "down1", r.H, KF, [(0, 8, 0)], whole(view(a["w_ffn_down"][1])), r.X, residual=True)
        norm_phase(nc, r, 1, 1)
        store_phase(nc, r)


_INS = ["x_prompt", "x_sample", "cache_nsa_kv", "state_nsa_win", "state_delta_conv", "state_delta_S", "state_gla_S",
        "page_table", "w_in_even", "conv_w_delta", "delta_A_log", "delta_dt_bias", "delta_norm_g", "w_out_even",
        "w_in_odd", "w_gla_gate2", "b_gla_gate2", "gla_norm_g", "w_out_odd", "w_ffn_gate", "w_ffn_up", "w_ffn_down",
        "ln_g", "ln_b"]
_OUTS = [(1, T, D), (NS, 1, D), (1, 1, T, 4, 2, 64), (1, 1, 512, 2, 2, 64), (1, 1, 3, 1536), (1, 1, 4, 128, 128),
         (1, 1, 4, 128, 256), (1, NS, 1, 4, 2, 64), (1, NS, 512, 2, 2, 64), (1, NS, 3, 1536), (1, NS, 4, 128, 128),
         (1, NS, 4, 128, 256)]


def per_partition(v):
    v = np.asarray(v)
    return v.reshape(-1, P).T


def kernel(**inputs):
    import concourse.bacc as bacc
    from concourse.bass_utils import run_bass_kernel_spmd

    nc = bacc.Bacc("TRN2", target_bir_lowering=False, num_devices=1)
    arrays, aps = {}, {}
    for name in ("ln_g", "ln_b", "conv_w_delta", "delta_norm_g", "gla_norm_g", "b_gla_gate2"):
        inputs[name] = per_partition(inputs[name])
    for name in ("delta_A_log", "delta_dt_bias"):
        inputs[name] = np.asarray(inputs[name]).T
    for name, arr in [(n, inputs[n]) for n in _INS] + list(constants().items()):
        arr = np.ascontiguousarray(arr)
        arrays["in_" + name] = arr
        aps[name] = nc.dram_tensor("in_" + name, arr.shape, mybir.dt.from_np(arr.dtype), kind="ExternalInput").ap()
    outs = [nc.dram_tensor(f"out_{i}", shape, F32, kind="ExternalOutput").ap() for i, shape in enumerate(_OUTS)]
    build(nc, aps, outs)
    result = run_bass_kernel_spmd(nc, [arrays], core_ids=[0])
    return tuple(result.results[0][f"out_{i}"] for i in range(len(_OUTS)))
```

```python
import math
from contextlib import ExitStack, contextmanager

import numpy as np

import concourse.bass as bass
from concourse import mybir
from concourse.alu_op_type import AluOpType as ALU

ACT = mybir.ActivationFunctionType
F32 = mybir.dt.float32
I32 = mybir.dt.int32
F32R = mybir.dt.float32r
AX = mybir.AxisListType

P = 128
D = 1024
KD = D // P
T = 1024
TT = T // P
NS = 8
N = T + NS
CW = N // 3
NB = 3
FF = 2816
KF = FF // P
ALPHA = 4.0 ** 0.25
NEG = -1e30
HEADS = 4
GV = 256
PAGES = 32
PGRP = 4
NG = PAGES // PGRP

Q_A, K_A, V_A, GATE_A, Q_B, K_CMP, V_CMP, K_SEL, V_SEL, K_WIN, V_WIN, SMALL = 0, 4, 8, 12, 16, 20, 21, 22, 23, 24, 25, 26
R_BETA, R_G, R_NSA = 0, 32, 64
NSMALL = 96
OQ, OK, OV, OR_, OG1 = 0, 4, 8, 16, 24
LEVELS = 7


def constants():
    i = np.arange(P)
    ident = np.eye(P, dtype=np.float32)
    level = np.zeros((P, LEVELS, P), np.float32)
    for lv in range(LEVELS):
        s = 1 << lv
        row, col = i[None, :], i[:, None]
        level[:, lv] = (row // (2 * s) == col // (2 * s)) & (row // s % 2 == 1) & (col // s % 2 == 0)
    upper = (i[:, None] <= i[None, :]).astype(np.float32)
    causal = np.where(i[None, :] <= i[:, None], 0, NEG).astype(np.float32)
    oldest = np.where(i[None, :] > i[:, None], 0, NEG).astype(np.float32)
    qpos = (np.arange(TT) * P)[None, :, None] + i[:, None, None]
    ok = (np.arange(32)[None, None, :] + 1) * 32 <= qpos + 1
    cmp_add = np.where(ok, 0, NEG).astype(np.float32).reshape(P, -1)
    cmp_one = ok.astype(np.float32).reshape(P, -1)
    pool = np.where(i[:, None] // 32 == np.arange(4)[None, :], 1 / 32, 0).astype(np.float32)
    rowsel = np.zeros((NSMALL, 8, P), np.float32)
    for h in range(HEADS):
        rowsel[R_BETA + h, h] = 1
        rowsel[R_G + h, 4 + h] = 1
    sh = np.arange(64)
    group = ((sh[:, None] // 8 == sh[None, :] // 8) & (sh[:, None] % 8 // 4 == sh[None, :] % 8 // 4)).astype(np.float32)
    own = (np.arange(8)[:, None] == sh[None, :] // 8).astype(np.float32)
    headrow = (np.arange(8)[None, :] == sh[:, None] % 8).astype(np.float32)
    pick = np.repeat(np.eye(8, dtype=np.float32), P, axis=1)
    return {
        "c_ident": ident, "c_level": level.reshape(P, -1), "c_upper": upper, "c_causal": causal, "c_oldest": oldest,
        "c_cmp_add": cmp_add, "c_cmp_one": cmp_one, "c_pool": pool, "c_rowsel": rowsel.reshape(NSMALL, -1),
        "c_group": group, "c_own": own, "c_headrow": headrow, "c_pick": pick,
    }


class Res:
    pass


@contextmanager
def phase(nc):
    with nc.cleanup_on_exit():
        with ExitStack() as ctx:
            yield ctx
    nc.all_engine_barrier()


@contextmanager
def twin(nc, name, shape, part=None):
    offset = -(-nc.sbuf_base // 32) * 32
    rounded = list(shape)
    if part:
        offset += part[0] * N * 4
        rounded[1] = part[1] - part[0]
    with nc.sbuf_tensor(name, shape, F32) as tile:
        yield tile, nc.alloc_sbuf_tensor_at(name + "_rounded", rounded, F32R, offset=offset)


def load_phase(nc, r):
    with phase(nc) as ctx:
        stage = ctx.enter_context(nc.sbuf_tensor("x_stage", [P, 3, D], F32))
        const_in = nc.alloc_semaphore("const_in")
        x_in = [nc.alloc_semaphore(f"x_in{u}") for u in range(3)]
        x_turned = nc.alloc_semaphore("x_turned")
        x_rounded = nc.alloc_semaphore("x_rounded")
        x_kept = nc.alloc_semaphore("x_kept")
        ones_set = nc.alloc_semaphore("ones_set")
        block = ctx.enter_context(nc.Block())
        tiles = [(r.x_prompt[0, t * P:(t + 1) * P, :], P) for t in range(TT)] + [
            (r.x_sample.rearrange("b t d -> (b t) d"), NS)]
        n_const = len(r.const_loads)

        @block.sync
        def _(sp):
            for n, (src, rows) in enumerate(tiles):
                if n >= 3:
                    sp.wait_ge(x_turned, 2 * (n - 2))
                sp.dma_start(stage[0:rows, n % 3, :], src).then_inc(x_in[n % 3], 16)

        @block.scalar
        def _(act):
            for dst, src in r.const_loads:
                act.dma_start(dst, src).then_inc(const_in, 16)
            act.wait_ge(const_in, 16 * n_const)
            for n, (_, rows) in enumerate(tiles):
                act.wait_ge(x_turned, 2 * n + 2)
                for half in range(2):
                    act.copy(r.Xh[:, 4 * half:4 * half + 4, n * P:n * P + rows],
                             r.ps[:, n % 2 * 2 + half, :].rearrange("p (k t) -> p k t", k=4)[:, :, 0:rows]
                             ).then_inc(x_rounded, 1)

        @block.vector
        def _(v):
            v.memset(r.ones_d[:], 1.0 / D)
            v.memset(r.ones[:], 1.0)
            v.memset(r.bias[:, 0:1], 1e-5)
            v.memset(r.bias[:, 1:2], 1e-6).then_inc(ones_set, 1)
            for n, (_, rows) in enumerate(tiles):
                for half in range(2):
                    v.wait_ge(x_rounded, 2 * n + 1 + half)
                    v.tensor_tensor(r.Xl[:, 4 * half:4 * half + 4, n * P:n * P + rows],
                                    r.ps[:, n % 2 * 2 + half, :].rearrange("p (k t) -> p k t", k=4)[:, :, 0:rows],
                                    r.Xh[:, 4 * half:4 * half + 4, n * P:n * P + rows].bitcast(F32),
                                    ALU.subtract).then_inc(x_kept, 1)

        @block.tensor
        def _(pe):
            pe.wait_ge(const_in, 16 * n_const)
            for n, (_, rows) in enumerate(tiles):
                pe.wait_ge(x_in[n % 3], 16 * (n // 3 + 1))
                if n >= 2:
                    pe.wait_ge(x_kept, 2 * (n - 1))
                for half in range(2):
                    for k in range(4):
                        mm = pe.transpose(r.ps[:, n % 2 * 2 + half, k * P:k * P + rows],
                                          stage[0:rows, n % 3, (4 * half + k) * P:(4 * half + k + 1) * P],
                                          r.ident[0:rows, 0:rows])
                    mm.then_inc(x_turned, 1)


def residual_phase(nc, r, name, moving, moving_lo, parts, load, reload=False):
    kn = moving.shape[1] // parts
    flat = r.X[:].rearrange("p k n -> p (k n)")
    with phase(nc) as ctx:
        raw, lo = ctx.enter_context(twin(nc, name + "_w", [P, 2, kn, P]))
        hi = ctx.enter_context(nc.sbuf_tensor(name + "_w_hi", [P, 2, kn, P], F32R))
        moving_hi = ctx.enter_context(nc.sbuf_tensor(name + "_m_hi", [P, kn, N], F32R))
        w_in = [nc.alloc_semaphore(name + f"_w_in{u}") for u in range(2)]
        w_split, m_rounded, m_split, product, bank_free, x_in = [nc.alloc_semaphore(name + s) for s in (
            "_w_split", "_m_rounded", "_m_split", "_product", "_bank_free", "_x_in")]
        block = ctx.enter_context(nc.Block())
        per = len(load(0, 0))
        all_banks = NB * KD

        @block.sync
        def _(sp):
            for u in range(2):
                for dst, src in load(0, u):
                    sp.dma_start(raw[:, u][dst], src).then_inc(w_in[u], 16)
            if reload:
                sp.dma_start(r.X[:], r.x_spilled).then_inc(x_in, 16)
            for part in range(parts):
                with sp.Fori(0 if part else 1, KD // 2) as i:
                    for u in range(2):
                        sp.wait_ge(product, i * 6 + (part * all_banks + 3 * u - 3))
                        for dst, src in load(part, i * 2 + u):
                            sp.dma_start(raw[:, u][dst], src).then_inc(w_in[u], 16)

        @block.gpsimd
        def _(pool):
            split_weights(pool, r, w_in, w_split, raw, hi, lo, KD * parts, per)

        @block.tensor
        def _(pe):
            def three(part, u, c, k):
                dst, cols = r.ps[:, 3 * u + c, 0:CW], slice(c * CW, (c + 1) * CW)
                pe.matmul(dst, hi[:, u, k, :], moving_hi[:, k, cols], start=(k == 0), stop=False)
                pe.matmul(dst, hi[:, u, k, :], moving_lo[:, part * kn + k, cols], start=False, stop=False)
                return pe.matmul(dst, lo[:, u, k, :], moving_hi[:, k, cols], start=False, stop=(k == kn - 1))

            def chunk(part, u, split, free):
                pe.wait_ge(w_split, split)
                for c in range(NB):
                    pe.wait_ge(bank_free, free + (c + 1))
                    for k in range(kn):
                        mm = three(part, u, c, k)
                    mm.then_inc(product, 1)

            for part in range(parts):
                pe.wait_ge(w_split, 2 * KD * part + 2)
                pe.wait_ge(bank_free, all_banks * part + 3)
                for k in range(kn):
                    pe.wait_ge(m_split, kn * part + k + 1)
                    for c in range(NB):
                        mm = three(part, 0, c, k)
                        if k == kn - 1:
                            mm.then_inc(product, 1)
                chunk(part, 1, 2 * KD * part + 4, all_banks * part + 3)
                with pe.Fori(1, KD // 2) as i:
                    for u in range(2):
                        chunk(part, u, i * 4 + (2 * KD * part + 2 * u + 2), i * 6 + (all_banks * part + 3 * u))

        @block.scalar
        def _(act):
            for part in range(parts):
                if part:
                    act.wait_ge(product, all_banks * part)
                for k in range(kn):
                    act.copy(moving_hi[:, k, :], moving[:, part * kn + k, :]).then_inc(m_rounded, 1)

        @block.vector
        def _(v):
            v.sem_inc(bank_free, 6)
            for part in range(parts):
                for k in range(kn):
                    v.wait_ge(m_rounded, part * kn + k + 1)
                    v.tensor_tensor(moving_lo[:, part * kn + k, :], moving[:, part * kn + k, :],
                                    moving_hi[:, k, :].bitcast(F32), ALU.subtract).then_inc(m_split, 1)
                if reload:
                    v.wait_ge(x_in, 16)
                with v.Fori(0, KD // 2) as i:
                    for u in range(2):
                        for c in range(NB):
                            v.wait_ge(product, i * 6 + (all_banks * part + 3 * u + c + 1))
                            dst = flat[:, bass.ds(i * (2 * N) + (u * N + c * CW), CW)]
                            v.scalar_tensor_tensor(out=dst, in0=dst, scalar=1.0 if part else ALPHA,
                                                   in1=r.ps[:, 3 * u + c, 0:CW], op0=ALU.mult,
                                                   op1=ALU.add).then_inc(bank_free, 1)


def split_weights(pool, r, w_in, w_split, raw, hi, lo, steps, per):
    ones = r.ones[:].unsqueeze(1).to_broadcast([P, raw.shape[2], P])
    with pool.Fori(0, steps // 2) as i:
        for u in range(2):
            pool.wait_ge(w_in[u], i * (16 * per) + 16 * per)
            pool.tensor_tensor(hi[:, u], raw[:, u], ones, ALU.mult).then_inc(w_split, 1)
            pool.wait_ge(w_split, i * 4 + (2 * u + 1))
            pool.tensor_tensor(lo[:, u], raw[:, u], hi[:, u].bitcast(F32), ALU.subtract).then_inc(w_split, 1)


def project_split_phase(nc, r, name, chunks, load, out, small):
    total = chunks[-1][1]
    flat = out[:].rearrange("p k n -> p (k n)")
    with phase(nc) as ctx:
        raw, lo = ctx.enter_context(twin(nc, name + "_w", [P, 2, KD, P]))
        hi = ctx.enter_context(nc.sbuf_tensor(name + "_w_hi", [P, 2, KD, P], F32R))
        w_in = [nc.alloc_semaphore(name + f"_w_in{u}") for u in range(2)]
        w_split, w_clear, w_small, product, bank_free = [nc.alloc_semaphore(name + s) for s in (
            "_w_split", "_w_clear", "_w_small", "_product", "_bank_free")]
        block = ctx.enter_context(nc.Block())
        per = len(load(0, 0, 0))

        @block.sync
        def _(sp):
            for u in range(2):
                for dst, src in load(u, u, 0):
                    sp.dma_start(raw[:, u][dst], src).then_inc(w_in[u], 16)
            for a, b, shift in chunks:
                a = max(a, 2)
                if shift is not None:
                    with sp.Fori(a // 2, b // 2) as i:
                        for u in range(2):
                            sp.wait_ge(product, i * 6 + (3 * u - 3))
                            for dst, src in load(i * 2 + u, u, shift):
                                sp.dma_start(raw[:, u][dst], src).then_inc(w_in[u], 16)
                else:
                    for m in range(a, b):
                        sp.wait_ge(product, 3 * m - 3)
                        for dst, src in load(m, m % 2, shift):
                            sp.dma_start(raw[:, m % 2][dst], src).then_inc(w_in[m % 2], 16)
            sp.wait_ge(w_clear, 1)
            for dst, src in small:
                sp.dma_start(raw[:, 0][dst], src).then_inc(w_small, 16)

        @block.gpsimd
        def _(pool):
            split_weights(pool, r, w_in, w_split, raw, hi, lo, total, per)
            pool.wait_ge(product, 3 * total - 3)
            pool.memset(raw[:, 0, :, :], 0.0).then_inc(w_clear, 1)
            pool.wait_ge(w_small, 16 * len(small))
            pool.tensor_copy(hi[:, 0], raw[:, 0]).then_inc(w_split, 1)
            pool.wait_ge(w_split, 2 * total + 1)
            pool.tensor_tensor(lo[:, 0], raw[:, 0], hi[:, 0].bitcast(F32), ALU.subtract).then_inc(w_split, 1)

        @block.tensor
        def _(pe):
            def products(u, rows, c):
                for k in range(KD):
                    cols = slice(c * CW, (c + 1) * CW)
                    dst = r.ps[0:rows, 3 * u + c, 0:CW]
                    pe.matmul(dst, hi[:, u, k, 0:rows], r.Xh[:, k, cols], start=(k == 0), stop=False)
                    pe.matmul(dst, hi[:, u, k, 0:rows], r.Xl[:, k, cols], start=False, stop=False)
                    mm = pe.matmul(dst, lo[:, u, k, 0:rows], r.Xh[:, k, cols], start=False, stop=(k == KD - 1))
                mm.then_inc(product, 1)

            with pe.Fori(0, total // 2) as i:
                for u in range(2):
                    pe.wait_ge(w_split, i * 4 + (2 * u + 2))
                    for c in range(NB):
                        pe.wait_ge(bank_free, i * 6 + (3 * u + c + 1))
                        products(u, P, c)
            pe.wait_ge(w_split, 2 * total + 2)
            for c in range(NB):
                pe.wait_ge(bank_free, 3 * total + c + 1)
                products(0, NSMALL, c)

        @block.vector
        def _(v):
            v.sem_inc(bank_free, 6)
            with v.Fori(0, total // 2) as i:
                for u in range(2):
                    for c in range(NB):
                        v.wait_ge(product, i * 6 + (3 * u + c + 1))
                        v.tensor_scalar(flat[:, bass.ds(i * (2 * N) + (u * N + c * CW), CW)],
                                        r.ps[:, 3 * u + c, 0:CW], 1.0, None, ALU.mult).then_inc(bank_free, 1)
            for c in range(NB):
                v.wait_ge(product, 3 * total + c + 1)
                v.tensor_copy(out[0:NSMALL, total, c * CW:(c + 1) * CW],
                              r.ps[0:NSMALL, c, 0:CW]).then_inc(bank_free, 1)
            v.tensor_tensor(r.X[:], r.Xh[:].bitcast(F32), r.Xl[:].bitcast(F32), ALU.add)


def norm_phase(nc, r, layer, which, split):
    ln = layer * 2 + which
    with phase(nc) as ctx:
        total = ctx.enter_context(nc.sbuf_tensor(f"ln{ln}_total", [P, NB, CW], F32))
        square = ctx.enter_context(nc.sbuf_tensor(f"ln{ln}_square", [P, KD, CW], F32))
        spread = ctx.enter_context(nc.sbuf_tensor(f"ln{ln}_spread", [P, NB, CW], F32))
        rstd = ctx.enter_context(nc.sbuf_tensor(f"ln{ln}_rstd", [P, NB, CW], F32))
        summed, mean_ready, centred, squared, spread_ready, var_ready, rstd_ready, scaled, logged, whole, rounded = [
            nc.alloc_semaphore(f"ln{ln}_" + s) for s in
            ("summed", "mean_ready", "centred", "squared", "spread_ready", "var_ready", "rstd_ready", "scaled",
             "logged", "whole", "rounded")]
        block = ctx.enter_context(nc.Block())

        def cols(c):
            return slice(c * CW, (c + 1) * CW)

        @block.vector
        def _(v):
            for c in range(NB):
                v.tensor_reduce(total[:, c, :], r.X[:, :, cols(c)].rearrange("p k n -> p n k"), AX.X,
                                ALU.add).then_inc(summed, 1)
            for c in range(NB):
                v.wait_ge(mean_ready, c + 1)
                v.tensor_tensor(r.X[:, :, cols(c)], r.X[:, :, cols(c)],
                                r.ps[:, c, 0:CW].unsqueeze(1).to_broadcast([P, KD, CW]),
                                ALU.subtract).then_inc(centred, 1)
            for c in range(NB):
                v.wait_ge(squared, c + 1)
                v.tensor_reduce(spread[:, c, :], square[:].rearrange("p k n -> p n k"), AX.X,
                                ALU.add).then_inc(spread_ready, 1)
            for c in range(NB):
                v.wait_ge(rstd_ready, c + 1)
                v.tensor_tensor(r.X[:, :, cols(c)], r.X[:, :, cols(c)],
                                rstd[:, c, :].unsqueeze(1).to_broadcast([P, KD, CW]), ALU.mult).then_inc(scaled, 1)
                if split:
                    v.wait_ge(whole, c + 1)
                    v.wait_ge(rounded, c + 1)
                    v.tensor_tensor(r.Xl[:, :, cols(c)], square[:], r.Xh[:, :, cols(c)].bitcast(F32),
                                    ALU.subtract).then_inc(centred, 1)

        @block.tensor
        def _(pe):
            for c in range(NB):
                pe.wait_ge(summed, c + 1)
                pe.matmul(r.ps[:, c, 0:CW], r.ones_d[:], total[:, c, :], start=True, stop=True).then_inc(mean_ready, 1)
            for c in range(NB):
                pe.wait_ge(spread_ready, c + 1)
                pe.matmul(r.ps[:, 3 + c, 0:CW], r.ones_d[:], spread[:, c, :], start=True,
                          stop=True).then_inc(var_ready, 1)

        @block.scalar
        def _(act):
            act.preload_act_table_set("natural_log_exp_and_others")
            for c in range(NB):
                act.wait_ge(centred, c + 1)
                if c:
                    act.wait_ge(spread_ready, c)
                act.activation(square[:], r.X[:, :, cols(c)], ACT.Square).then_inc(squared, 1)
            for c in range(NB):
                act.wait_ge(var_ready, c + 1)
                act.activation(rstd[:, c, :], r.ps[:, 3 + c, 0:CW], ACT.Ln, bias=r.bias[:, 0:1]).then_inc(logged, 1)
                act.wait_ge(logged, c + 1)
                act.activation(rstd[:, c, :], rstd[:, c, :], ACT.Exp, scale=-0.5).then_inc(rstd_ready, 1)
            for c in range(NB):
                act.wait_ge(scaled, c + 1)
                if split and c:
                    act.wait_ge(centred, NB + c)
                for k in range(KD):
                    dst = square[:, k, :] if split else r.X[:, k, cols(c)]
                    mm = act.activation(dst, r.X[:, k, cols(c)], ACT.Identity,
                                        bias=r.lnb[:, ln * KD + k:ln * KD + k + 1],
                                        scale=r.lng[:, ln * KD + k:ln * KD + k + 1])
                if split:
                    mm.then_inc(whole, 1)
                    act.wait_ge(whole, c + 1)
                    act.copy(r.Xh[:, :, cols(c)], square[:]).then_inc(rounded, 1)


def ffn_up_phase(nc, r, layer):
    flat = r.F[:].rearrange("p k n -> p (k n)")
    wg = r.w_ffn_gate[layer].rearrange("(k p) n -> p k n", p=P)
    wu = r.w_ffn_up[layer].rearrange("(k p) n -> p k n", p=P)
    with phase(nc) as ctx:
        raw, lo = ctx.enter_context(twin(nc, f"up{layer}_w", [P, 2, 2, KD, P]))
        hi = ctx.enter_context(nc.sbuf_tensor(f"up{layer}_w_hi", [P, 2, 2, KD, P], F32R))
        w_split = nc.alloc_semaphore(f"up{layer}_w_split")
        lit = ctx.enter_context(nc.sbuf_tensor(f"up{layer}_silu", [P, 2, CW], F32))
        w_in = [nc.alloc_semaphore(f"up{layer}_w_in{u}") for u in range(2)]
        gated, upped, silu_ready, hidden = [nc.alloc_semaphore(f"up{layer}_" + s) for s in
                                            ("gated", "upped", "silu_ready", "hidden")]
        block = ctx.enter_context(nc.Block())

        @block.sync
        def _(sp):
            def fetch(m, u):
                sp.dma_start(raw[:, u, 0], wg[:, :, bass.ds(m * P, P)]).then_inc(w_in[u], 16)
                sp.dma_start(raw[:, u, 1], wu[:, :, bass.ds(m * P, P)]).then_inc(w_in[u], 16)

            fetch(0, 0)
            fetch(1, 1)
            with sp.Fori(1, KF // 2) as i:
                for u in range(2):
                    sp.wait_ge(upped, i * 6 + (3 * u - 3))
                    fetch(i * 2 + u, u)

        @block.gpsimd
        def _(pool):
            raw_, hi_, lo_ = (x[:].rearrange("p u a k m -> p u (a k) m") for x in (raw, hi, lo))
            split_weights(pool, r, w_in, w_split, raw_, hi_, lo_, KF, 2)

        @block.tensor
        def _(pe):
            with pe.Fori(0, KF // 2) as i:
                for u in range(2):
                    pe.wait_ge(w_split, i * 4 + (2 * u + 2))
                    for c in range(NB):
                        pe.wait_ge(hidden, i * 6 + (3 * u + c + 1))
                        pair = (3 * u + c) % 3
                        for part, done in ((0, gated), (1, upped)):
                            dst = r.ps[:, 2 * pair + part, 0:CW]
                            for k in range(KD):
                                xh, xl = r.Xh[:, k, c * CW:(c + 1) * CW], r.Xl[:, k, c * CW:(c + 1) * CW]
                                pe.matmul(dst, hi[:, u, part, k, :], xh, start=(k == 0), stop=False)
                                pe.matmul(dst, hi[:, u, part, k, :], xl, start=False, stop=False)
                                mm = pe.matmul(dst, lo[:, u, part, k, :], xh, start=False, stop=(k == KD - 1))
                            mm.then_inc(done, 1)

        @block.scalar
        def _(act):
            with act.Fori(0, KF // 2) as i:
                for g in range(6):
                    act.wait_ge(hidden, i * 6 + (g + 2))
                    act.wait_ge(gated, i * 6 + (g + 1))
                    act.activation(lit[:, g % 2, :], r.ps[:, 2 * (g % 3), 0:CW], ACT.Silu).then_inc(silu_ready, 1)

        @block.vector
        def _(v):
            v.sem_inc(hidden, 3)
            with v.Fori(0, KF // 2) as i:
                for g in range(6):
                    v.wait_ge(silu_ready, i * 6 + (g + 1))
                    v.wait_ge(upped, i * 6 + (g + 1))
                    v.tensor_tensor(flat[:, bass.ds(i * (2 * N) + (g // 3 * N + g % 3 * CW), CW)],
                                    lit[:, g % 2, :], r.ps[:, 2 * (g % 3) + 1, 0:CW], ALU.mult).then_inc(hidden, 1)
            v.tensor_tensor(r.X[:], r.Xh[:].bitcast(F32), r.Xl[:].bitcast(F32), ALU.add)


def even_rows_phase(nc, r):
    with phase(nc) as ctx:
        buf = ctx.enter_context(nc.sbuf_tensor("conv_buf", [24, 12 * P], F32))
        tail = ctx.enter_context(nc.sbuf_tensor("conv_tail", [11, 12 * P], F32))
        buf_in, turned, kept_a, kept_v, stored = [nc.alloc_semaphore("rows_" + s) for s in
                                                  ("buf_in", "turned", "kept_a", "kept_v", "stored")]
        block = ctx.enter_context(nc.Block())
        units = []
        for t in range(TT):
            units.append(([r.H[:, K_CMP + j, t * P:(t + 1) * P] for j in range(6)], P, P, r.rows[:, t, :]))
        units.append(([r.H[:, K_CMP + j, T:N] for j in range(6)], NS, P, r.srows[:, :]))
        for g in range(2):
            units.append(([r.H[:, 6 * g + j, T - 3:N] for j in range(6)], 11, P, tail[:, g * 6 * P:(g + 1) * 6 * P]))
        for g in range(2):
            units.append(([buf[:, (6 * g + j) * P:(6 * g + j + 1) * P] for j in range(6)], P, 24,
                          r.bufT[:, 6 * g:6 * g + 6, :].rearrange("p k n -> p (k n)")))

        @block.sync
        def _(sp):
            conv = r.state_delta_conv[0]
            n = 0
            sp.dma_start(buf[:], conv.rearrange("b j c -> (b j) c")).then_inc(buf_in, 16)
            sp.dma_start(r.o_conv_s[0][:, 0:2, :], conv[:, 1:3, :]).then_inc(stored, 16)
            sp.dma_start(r.o_win_s[0].rearrange("b w c g d -> b w (c g d)")[:, 0:511, :],
                         r.state_nsa_win[0].rearrange("b w c g d -> b w (c g d)")[:, 1:512, :]).then_inc(stored, 16)
            n += 2
            for t in range(TT):
                sp.wait_ge(kept_a, t + 1)
                sp.wait_ge(kept_v, t + 1)
                sp.dma_start(r.o_rows_p[0, 0, t * P:(t + 1) * P].rearrange("t c g d -> t (c g d)"),
                             r.rows[:, t, 0:512]).then_inc(stored, 16)
                n += 1
                if t >= 4:
                    sp.dma_start(r.o_win_p[0, 0, (t - 4) * P:(t - 3) * P].rearrange("t c g d -> t (c g d)"),
                                 r.rows[:, t, 512:768]).then_inc(stored, 16)
                    n += 1
            sp.wait_ge(kept_a, 9)
            sp.wait_ge(kept_v, 9)
            sp.dma_start(r.o_rows_s[0, :, 0].rearrange("b c g d -> b (c g d)"), r.srows[:, 0:512]).then_inc(stored, 16)
            sp.dma_start(r.o_win_s[0, :, 511].rearrange("b c g d -> b (c g d)"),
                         r.srows[:, 512:768]).then_inc(stored, 16)
            sp.wait_ge(kept_a, 11)
            sp.wait_ge(kept_v, 11)
            sp.dma_start(r.o_conv_p[0, 0], tail[0:3, :]).then_inc(stored, 16)
            sp.dma_start(r.o_conv_s[0, :, 2], tail[3:11, :]).then_inc(stored, 16)
            n += 4
            sp.wait_ge(stored, 16 * n)

        @block.tensor
        def _(pe):
            for n, (srcs, rows, cols, _) in enumerate(units):
                b = n % 3 * 2
                if n >= 3:
                    pe.wait_ge(kept_a, n - 2)
                    pe.wait_ge(kept_v, n - 2)
                if n == 11:
                    pe.wait_ge(buf_in, 16)
                for j in range(6):
                    k = 24 if n >= 11 else P
                    mm = pe.transpose(r.ps[0:rows, b + j // 4, j % 4 * cols:j % 4 * cols + cols], srcs[j],
                                      r.ident[0:k, 0:k])
                    if j in (3, 5):
                        mm.then_inc(turned, 1)

        @block.scalar
        def _(act):
            for n, (_, rows, cols, dst) in enumerate(units):
                act.wait_ge(turned, 2 * n + 1)
                act.copy(dst[0:rows, 0:4 * cols], r.ps[0:rows, n % 3 * 2, 0:4 * cols]).then_inc(kept_a, 1)

        @block.vector
        def _(v):
            for n, (_, rows, cols, dst) in enumerate(units):
                v.wait_ge(turned, 2 * n + 2)
                v.tensor_copy(dst[0:rows, 4 * cols:6 * cols], r.ps[0:rows, n % 3 * 2 + 1, 0:2 * cols]).then_inc(kept_v, 1)


def gates_phase(nc, r):
    S = r.H[:, SMALL, :]
    B, G, C = slice(R_BETA, R_BETA + 4), slice(R_G, R_G + 4), slice(R_NSA, R_NSA + 24)
    with phase(nc) as ctx:
        par = ctx.enter_context(nc.sbuf_tensor("g_par", [P, 4], F32))
        z = ctx.enter_context(nc.sbuf_tensor("g_z", [P, N], F32))
        az = ctx.enter_context(nc.sbuf_tensor("g_az", [P, N], F32))
        keep = ctx.enter_context(nc.sbuf_tensor("g_keep", [P, T], F32))
        par_in, a, v_, turned, kept = [nc.alloc_semaphore("g_" + s) for s in
                                       ("par_in", "act_step", "dve_step", "turned", "kept")]
        block = ctx.enter_context(nc.Block())

        @block.sync
        def _(sp):
            sp.dma_start(par[G, 0:1], r.dt_bias).then_inc(par_in, 16)
            sp.dma_start(par[G, 1:2], r.A_log).then_inc(par_in, 16)

        @block.vector
        def _(v):
            v.memset(keep[:], 1.0).then_inc(v_, 1)
            v.wait_ge(v_, 1)
            v.memset(keep[:].rearrange("p (c t) -> p c t", t=P)[:, :, 0:1], 0.0)
            v.wait_ge(par_in, 32)
            v.tensor_scalar(z[G, :], S[G, :], par[G, 0:1], None, ALU.add).then_inc(v_, 1)
            v.wait_ge(v_, 2)
            v.scalar_tensor_tensor(out=az[G, :], in0=z[G, :], scalar=-1.0, in1=z[G, :], op0=ALU.mult,
                                   op1=ALU.max).then_inc(v_, 1)
            v.wait_ge(a, 2)
            v.tensor_scalar(z[B, :], z[B, :], 1.0, None, ALU.add)
            v.tensor_scalar(z[C, :], z[C, :], 1.0, None, ALU.add).then_inc(v_, 1)
            v.wait_ge(v_, 4)
            v.reciprocal(S[B, :], z[B, :])
            v.reciprocal(S[C, :], z[C, :])
            v.wait_ge(a, 5)
            v.scalar_tensor_tensor(out=z[G, :], in0=z[G, :], scalar=0.0, in1=az[G, :], op0=ALU.max,
                                   op1=ALU.add).then_inc(v_, 1)
            v.wait_ge(v_, 5)
            v.tensor_scalar(z[G, :], z[G, :], par[G, 2:3], -1.0, ALU.mult, ALU.mult).then_inc(v_, 1)
            v.wait_ge(v_, 6)
            v.tensor_tensor_scan(S[G, 0:T], keep[G, :], z[G, 0:T], 0.0, ALU.mult, ALU.add)
            v.tensor_copy(S[G, T:N], z[G, T:N]).then_inc(v_, 1)
            for n in range(9):
                rows = P if n < 8 else NS
                v.wait_ge(turned, n + 1)
                v.tensor_copy(r.tok[0:rows, n, :], r.ps[0:rows, n % 8, 0:NSMALL]).then_inc(kept, 1)

        @block.scalar
        def _(act):
            act.preload_act_table_set("natural_log_exp_and_others")
            act.activation(z[B, :], S[B, :], ACT.Exp, scale=-1.0).then_inc(a, 1)
            act.activation(z[C, :], S[C, :], ACT.Exp, scale=-1.0).then_inc(a, 1)
            act.wait_ge(par_in, 32)
            act.activation(par[G, 2:3], par[G, 1:2], ACT.Exp).then_inc(a, 1)
            act.wait_ge(v_, 3)
            act.activation(az[G, :], az[G, :], ACT.Exp, scale=-1.0).then_inc(a, 1)
            act.wait_ge(a, 4)
            act.activation(az[G, :], az[G, :], ACT.Ln, bias=1.0).then_inc(a, 1)

        @block.tensor
        def _(pe):
            pe.wait_ge(v_, 7)
            for n in range(9):
                rows = P if n < 8 else NS
                if n == 8:
                    pe.wait_ge(kept, 1)
                pe.transpose(r.ps[0:rows, n % 8, 0:NSMALL], S[0:NSMALL, n * P:n * P + rows],
                             r.ident[0:NSMALL, 0:NSMALL]).then_inc(turned, 1)


def store_phase(nc, r):
    with phase(nc) as ctx:
        stage = ctx.enter_context(nc.sbuf_tensor("y_stage", [P, 2, D], F32))
        turned, kept_a, kept_v = [nc.alloc_semaphore("y_" + s) for s in ("turned", "kept_a", "kept_v")]
        stored = [nc.alloc_semaphore(f"y_stored{u}") for u in range(2)]
        block = ctx.enter_context(nc.Block())
        tiles = [(r.o_y_p[0, t * P:(t + 1) * P, :], P) for t in range(TT)] + [
            (r.o_y_s.rearrange("b t d -> (b t) d"), NS)]

        @block.sync
        def _(sp):
            for n, (dst, rows) in enumerate(tiles):
                sp.wait_ge(kept_a, n + 1)
                sp.wait_ge(kept_v, n + 1)
                sp.dma_start(dst, stage[0:rows, n % 2, :]).then_inc(stored[n % 2], 16)
            sp.wait_ge(stored[0], 16 * 5)
            sp.wait_ge(stored[1], 16 * 4)

        @block.tensor
        def _(pe):
            for n, (_, rows) in enumerate(tiles):
                if n >= 2:
                    pe.wait_ge(kept_a, n - 1)
                    pe.wait_ge(kept_v, n - 1)
                for half in range(2):
                    for k in range(4):
                        mm = pe.transpose(r.ps[0:rows, n % 2 * 2 + half, k * P:(k + 1) * P],
                                          r.X[:, 4 * half + k, n * P:n * P + rows], r.ident[:])
                    mm.then_inc(turned, 1)

        @block.scalar
        def _(act):
            for n, (_, rows) in enumerate(tiles):
                act.wait_ge(turned, 2 * n + 1)
                if n >= 2:
                    act.wait_ge(stored[n % 2], 16 * (n // 2))
                act.copy(stage[0:rows, n % 2, 0:512], r.ps[0:rows, n % 2 * 2, :]).then_inc(kept_a, 1)

        @block.vector
        def _(v):
            for n, (_, rows) in enumerate(tiles):
                v.wait_ge(turned, 2 * n + 2)
                if n >= 2:
                    v.wait_ge(stored[n % 2], 16 * (n // 2))
                v.tensor_copy(stage[0:rows, n % 2, 512:1024], r.ps[0:rows, n % 2 * 2 + 1, :]).then_inc(kept_v, 1)

def nsa_prompt_phase(nc, r):
    flat = r.H[:].rearrange("p k n -> p (k n)")
    UNITS = [(t, g) for t in range(TT) for g in range(2)]
    NU = len(UNITS)

    def blocks(t):
        lo = max(0, t - 4)
        return [("cmp", 0)] + [("sel", b) for b in range(t + 1)] + [("win", b) for b in range(lo, t + 1)]

    def groups(t):
        bl = blocks(t)
        return [bl[0:1]] + [bl[s:s + 4] for s in range(1, len(bl), 4)]

    first = [0]
    for t, g in UNITS:
        first.append(first[-1] + len(groups(t)))
    GT = first[-1]
    with phase(nc) as ctx:
        def sb(name, shape):
            return ctx.enter_context(nc.sbuf_tensor("np_" + name, shape, F32))

        causal, oldest = sb("causal", [P, P]), sb("oldest", [P, P])
        cmp_add, cmp_one = sb("cmp_add", [P, TT, 32]), sb("cmp_one", [P, TT, 32])
        kcb, vcbT, vcb = sb("kcb", [P, 32]), sb("vcbT", [P, 32]), sb("vcb", [32, P])
        QS = sb("q", [P, 2, P])
        gates = sb("gates", [P, 2, 2, 3])
        Psel, Pwin, Pcmp = sb("psel", [P, 2, T]), sb("pwin", [P, 2, 640]), sb("pcmp", [P, 2, 32])
        PT = sb("pt", [P, 14, P])
        top, ntop, den, coef = sb("top", [P, 2, 3]), sb("ntop", [P, 2, 3]), sb("den", [P, 2, 3]), sb("coef", [P, 2, 3])
        (tables_in, means_ready, vcb_turned, vcb_kept, q_ready, scored, masked, topped, negated, exped, inverted,
         weighed, scaled, turned, kept, o_ready, o_kept, spilled) = [
            nc.alloc_semaphore("np_" + s) for s in
            ("tables_in", "means_ready", "vcb_turned", "vcb_kept", "q_ready", "scored", "masked", "topped", "negated",
             "exped", "inverted", "weighed", "scaled", "turned", "kept", "o_ready", "o_kept",
             "spilled")]
        block = ctx.enter_context(nc.Block())
        s_sel = r.ps[:, 0:2, :].rearrange("p b n -> p (b n)")
        s_win = r.ps[:, 2:4, :].rearrange("p b n -> p (b n)")
        gate_view = r.tok[:, :, R_NSA:R_NSA + 24].rearrange("p t (g h b) -> p t g h b", g=2, h=4)

        @block.sync
        def _(sp):
            for dst, src in ((causal[:], r.c_causal), (oldest[:], r.c_oldest),
                             (cmp_add[:].rearrange("p t c -> p (t c)"), r.c_cmp_add),
                             (cmp_one[:].rearrange("p t c -> p (t c)"), r.c_cmp_one)):
                sp.dma_start(dst, src).then_inc(tables_in, 16)
            sp.dma_start(r.x_spilled, r.X[:]).then_inc(spilled, 16)
            sp.wait_ge(spilled, 16)

        @block.tensor
        def _(pe):
            pe.wait_ge(means_ready, 2)
            pe.transpose(r.ps[0:32, 6, 0:P], vcbT[:], r.ident[:]).then_inc(vcb_turned, 1)
            pe.wait_ge(vcb_kept, 1)

            def scores(i, j):
                t, g = UNITS[j]
                rows = slice(64 * g, 64 * g + 64)
                lo, hi = max(0, t - 4) * P, (t + 1) * P
                pe.wait_ge(q_ready, i * TT + (t + 1))
                pe.wait_ge(exped, i * NU + (j + 1))
                for s in range(0, hi, 512):
                    e = min(hi, s + 512)
                    pe.matmul(s_sel[:, s:e], QS[rows, t % 2, :], r.H[rows, K_SEL, s:e], start=True, stop=True)
                for s in range(0, hi - lo, 512):
                    e = min(hi - lo, s + 512)
                    pe.matmul(s_win[:, s:e], QS[rows, t % 2, :], r.H[rows, K_WIN, lo + s:lo + e], start=True,
                              stop=True)
                pe.matmul(s_win[:, 640:672], QS[rows, t % 2, :], kcb[rows, :], start=True,
                          stop=True).then_inc(scored, 1)

            def turn(i, j):
                t, g = UNITS[j]
                pe.wait_ge(scaled, i * NU + (j + 1))
                lo = max(0, t - 4)
                for n, grp in enumerate(groups(t)):
                    gg = first[j] + n
                    pe.wait_ge(kept, i * GT + (max(gg - 1, 0) + 1))
                    for q, (kind, b) in enumerate(grp):
                        if kind == "cmp":
                            mm = pe.transpose(r.ps[0:32, 4 + gg % 2, 0:P], Pcmp[:, j % 2, :], r.ident[:])
                        else:
                            src = Psel[:, j % 2, b * P:(b + 1) * P] if kind == "sel" else \
                                Pwin[:, j % 2, (b - lo) * P:(b - lo + 1) * P]
                            mm = pe.transpose(r.ps[:, 4 + gg % 2, q * P:(q + 1) * P], src, r.ident[:])
                    mm.then_inc(turned, 1)

            def values(i, j):
                t, g = UNITS[j]
                bl = blocks(t)
                pe.wait_ge(kept, i * GT + (first[j + 1] + 1))
                pe.wait_ge(o_kept, i * NU + (max(j - 1, 0) + 1))
                for n, (kind, b) in enumerate(bl):
                    if kind == "cmp":
                        lhs, rhs = vcb[:], PT[0:32, 0, :]
                    else:
                        lhs = r.rows[:, b, 384:512] if kind == "sel" else r.rows[:, b, 640:768]
                        rhs = PT[:, n, :]
                    mm = pe.matmul(r.ps[:, 6 + j % 2, 0:P], lhs, rhs, start=(n == 0), stop=(n == len(bl) - 1))
                mm.then_inc(o_ready, 1)

            pe.sem_inc(scored, 1)
            pe.sem_inc(turned, 1)
            pe.sem_inc(o_ready, 1)
            with pe.Fori(0, 4) as i:
                scores(i, 0)
                for j in range(NU):
                    if j + 1 < NU:
                        scores(i, j + 1)
                    turn(i, j)
                    values(i, j)

        @block.scalar
        def _(act):
            act.sem_inc(exped, 1)
            act.sem_inc(kept, 1)
            with act.Fori(0, 4) as i:
                for j, (t, g) in enumerate(UNITS):
                    s = j % 2
                    lo, hi = max(0, t - 4) * P, (t + 1) * P
                    act.wait_ge(turned, i * GT + ((first[j - 1] if j else 0) + 1))
                    act.wait_ge(negated, i * NU + (j + 1))
                    act.activation(Pcmp[:, s, :], s_win[:, 640:672], ACT.Exp, bias=ntop[:, s, 0:1], scale=0.125,
                                   accum_out=den[:, s, 0:1])
                    act.activation(Psel[:, s, 0:hi], s_sel[:, 0:hi], ACT.Exp, bias=ntop[:, s, 1:2], scale=0.125,
                                   accum_out=den[:, s, 1:2])
                    act.activation(Pwin[:, s, 0:hi - lo], s_win[:, 0:hi - lo], ACT.Exp, bias=ntop[:, s, 2:3],
                                   scale=0.125, accum_out=den[:, s, 2:3]).then_inc(exped, 1)
                    at = 0
                    for n, grp in enumerate(groups(t)):
                        gg = first[j] + n
                        if n == 0:
                            act.wait_ge(o_ready, i * NU + (j + 1))
                        act.wait_ge(turned, i * GT + (gg + 2))
                        if n == 0:
                            act.copy(PT[0:32, 0, :], r.ps[0:32, 4 + gg % 2, 0:P]).then_inc(kept, 1)
                        else:
                            act.copy(PT[:, at:at + len(grp), :].rearrange("p b n -> p (b n)"),
                                     r.ps[:, 4 + gg % 2, 0:len(grp) * P]).then_inc(kept, 1)
                        at += len(grp)

        @block.vector
        def _(v):
            v.tensor_reduce(kcb[:], r.H[:, K_CMP, 0:T].rearrange("p (c j) -> p c j", j=32), AX.X, ALU.add)
            v.tensor_reduce(vcbT[:], r.H[:, V_CMP, 0:T].rearrange("p (c j) -> p c j", j=32), AX.X,
                            ALU.add).then_inc(means_ready, 1)
            v.wait_ge(means_ready, 1)
            v.tensor_scalar(kcb[:], kcb[:], 1 / 32, None, ALU.mult)
            v.tensor_scalar(vcbT[:], vcbT[:], 1 / 32, None, ALU.mult).then_inc(means_ready, 1)
            v.wait_ge(vcb_turned, 1)
            v.tensor_copy(vcb[:], r.ps[0:32, 6, 0:P]).then_inc(vcb_kept, 1)
            v.wait_ge(tables_in, 64)
            v.sem_inc(o_kept, 1)

            def fetch(i, t):
                v.wait_ge(scored, i * NU + (max(2 * t - 2, 0) + 1))
                v.tensor_copy(gates[:, t % 2, :, :], gate_view[:, t, :, bass.ds(i, 1), :].squeeze(2))
                v.tensor_copy(QS[:, t % 2, :], flat[:, bass.ds(i * N + (Q_B * N + t * P), P)]).then_inc(q_ready, 1)

            def maxima(i, j):
                t, g = UNITS[j]
                s = j % 2
                hi = (t + 1) * P
                w = hi - max(0, t - 4) * P
                v.wait_ge(scored, i * NU + (j + 2))
                v.tensor_tensor(s_sel[:, hi - P:hi], s_sel[:, hi - P:hi], causal[:], ALU.add)
                v.tensor_tensor(s_win[:, w - P:w], s_win[:, w - P:w], causal[:], ALU.add)
                if t >= 4:
                    v.tensor_tensor(s_win[:, 0:P], s_win[:, 0:P], oldest[:], ALU.add)
                v.tensor_tensor(s_win[:, 640:672], s_win[:, 640:672], cmp_add[:, t, :], ALU.add).then_inc(masked, 1)
                v.wait_ge(masked, i * NU + (j + 1))
                v.tensor_reduce(top[:, s, 0:1], s_win[:, 640:672], AX.X, ALU.max)
                v.tensor_reduce(top[:, s, 1:2], s_sel[:, 0:hi], AX.X, ALU.max)
                v.tensor_reduce(top[:, s, 2:3], s_win[:, 0:w], AX.X, ALU.max).then_inc(topped, 1)
                v.wait_ge(topped, i * NU + (j + 1))
                v.tensor_scalar(ntop[:, s, :], top[:, s, :], -0.125, None, ALU.mult).then_inc(negated, 1)

            def weigh(i, j):
                t, g = UNITS[j]
                s = j % 2
                hi = (t + 1) * P
                w = hi - max(0, t - 4) * P
                v.wait_ge(exped, i * NU + (j + 2))
                v.reciprocal(coef[:, s, :], den[:, s, :]).then_inc(inverted, 1)
                v.wait_ge(inverted, i * NU + (j + 1))
                v.tensor_tensor(coef[:, s, :], coef[:, s, :], gates[:, t % 2, g, :], ALU.mult).then_inc(weighed, 1)
                v.wait_ge(weighed, i * NU + (j + 1))
                v.scalar_tensor_tensor(out=Pcmp[:, s, :], in0=Pcmp[:, s, :], scalar=coef[:, s, 0:1],
                                       in1=cmp_one[:, t, :], op0=ALU.mult, op1=ALU.mult)
                v.tensor_scalar(Psel[:, s, 0:hi], Psel[:, s, 0:hi], coef[:, s, 1:2], None, ALU.mult)
                v.tensor_scalar(Pwin[:, s, 0:w], Pwin[:, s, 0:w], coef[:, s, 2:3], None, ALU.mult).then_inc(scaled, 1)

            with v.Fori(0, 4) as i:
                fetch(i, 0)
                maxima(i, 0)
                for j, (t, g) in enumerate(UNITS):
                    weigh(i, j)
                    if g == 0 and t + 1 < TT:
                        fetch(i, t + 1)
                    if j + 1 < NU:
                        maxima(i, j + 1)
                    v.wait_ge(o_ready, i * NU + (j + 2))
                    v.tensor_scalar(flat[64 * g:64 * g + 64, bass.ds(i * N + (Q_B * N + t * P), P)],
                                    r.ps[64 * g:64 * g + 64, 6 + j % 2, 0:P], 1.0, None,
                                    ALU.mult).then_inc(o_kept, 1)


def conv_phase(nc, r):
    flat = r.H[:].rearrange("p k n -> p (k n)")
    buf = r.bufT[:].rearrange("p k (s j) -> p k s j", j=3)
    with phase(nc) as ctx:
        cw = ctx.enter_context(nc.sbuf_tensor("conv_w", [P, 48], F32))
        acc = ctx.enter_context(nc.sbuf_tensor("conv_acc", [P, 2, N], F32))
        w_in, tapped, acc_free = [nc.alloc_semaphore("conv_" + s) for s in ("w_in", "tapped", "acc_free")]
        block = ctx.enter_context(nc.Block())

        @block.sync
        def _(sp):
            sp.dma_start(cw[:], r.conv_w).then_inc(w_in, 16)

        @block.vector
        def _(v):
            v.wait_ge(w_in, 16)
            v.sem_inc(acc_free, 2)
            with v.Fori(0, 6) as i:
                for u in range(2):
                    v.wait_ge(acc_free, i * 2 + (u + 1))
                    v.tensor_scalar(acc[:, u, :], flat[:, bass.ds(i * (2 * N) + u * N, N)],
                                    cw[:, bass.ds(i * 2 + (36 + u), 1)], None, ALU.mult).then_inc(tapped, 1)
                    for j in (2, 1, 0):
                        w = cw[:, bass.ds(i * 2 + (12 * j + u), 1)]
                        back = 3 - j
                        v.wait_ge(tapped, i * 8 + (4 * u + back))
                        v.scalar_tensor_tensor(out=acc[:, u, T:N], in0=buf[:, bass.ds(i * 2 + u, 1), :, j].squeeze(1),
                                               scalar=w, in1=acc[:, u, T:N], op0=ALU.mult, op1=ALU.add)
                        v.scalar_tensor_tensor(out=acc[:, u, back:T],
                                               in0=flat[:, bass.ds(i * (2 * N) + u * N, T - back)],
                                               scalar=w, in1=acc[:, u, back:T], op0=ALU.mult,
                                               op1=ALU.add).then_inc(tapped, 1)

        @block.scalar
        def _(act):
            act.activation(r.H[:, GATE_A:GATE_A + 4, :], r.H[:, GATE_A:GATE_A + 4, :], ACT.Silu)
            with act.Fori(0, 6) as i:
                for u in range(2):
                    act.wait_ge(tapped, i * 8 + (4 * u + 4))
                    act.wait_ge(w_in, 16)
                    act.activation(flat[:, bass.ds(i * (2 * N) + u * N, N)], acc[:, u, :],
                                   ACT.Silu).then_inc(acc_free, 1)


class Sweep:

    def __init__(self, r, kp_last):
        x = r.X[:].rearrange("p k n -> p (k n)")
        size = PGRP * 384

        def pages(ap):
            return ap.rearrange("p (j n) -> p j n", j=PGRP)

        self.KP = [pages(x[:, 0:size]), pages(x[:, size:2 * size]),
                   pages(r.H[:, K_CMP:K_CMP + 2, :].rearrange("p k n -> p (k n)")[:, 0:size]), kp_last]
        at = 2 * size
        self.SC = x[0:NS * 8, at:at + PAGES * P + 1]
        at += PAGES * P + 4
        self.level = x[:, at:at + LEVELS * P].rearrange("p (l n) -> p l n", l=LEVELS)
        at += LEVELS * P
        self.pool = x[:, at:at + 4]
        self.KT = r.H[:, K_SEL, 0:1024].rearrange("p (u n) -> p u n", u=2)
        self.VCT = r.H[:, V_SEL, 0:1024].rearrange("p (s n) -> p s n", s=NS)
        self.KC = r.H[:, K_WIN, 0:1024].rearrange("p (s n) -> p s n", s=NS)
        self.Q = r.H[:, V_WIN, 0:NS * 64]
        self.Qs = self.Q.rearrange("p (s q) -> p s q", s=NS)
        self.pages = r.H[0:1, V_WIN, NS * 64:NS * 64 + NS * PAGES].bitcast(I32)


def delta_prompt_phase(nc, r):
    assert NG == TT and NS == 2 * (LEVELS - 3)
    cache = r.cache.rearrange("n e t c g d -> (n e) t (c g d)")
    n_pool = r.cache.shape[0]
    R = 64
    H4 = range(HEADS)
    with phase(nc) as ctx:
        def sb(name, shape):
            return ctx.enter_context(nc.sbuf_tensor("dp_" + name, shape, F32))

        sw = Sweep(r, sb("kp_last", [P, PGRP, 384])[:])
        level, upper, rowsel = sw.level, sb("upper", [P, P]), sb("rowsel", [NSMALL, 8, P])
        ng = sb("ng", [P, 1])
        SQ, RN = sb("sq", [P, 8, P]), sb("rn", [P, 8, P])
        QT, KT, VT, GB, DL, EG, QG, AT, QK = [sb(n, [P, 4, P]) for n in
                                              ("qt", "kt", "vt", "gb", "dl", "eg", "qg", "at", "qk")]
        AM = sb("am", [P, 2, 4, P])
        Dm, DT, PS, KBG, KD, VB, S, RO = [sb(n, [P, 4, P]) for n in ("d", "dt", "p", "kbg", "kd", "vb", "s", "ro")]
        U, WT = SQ[:, 0:4, :], SQ[:, 4:8, :]
        VN, OS = RN[:, 0:4, :], RN[:, 4:8, :]
        tk, e4, bg = sb("tk", [P, 12]), sb("e4", [P, 8]), sb("bg", [P, 4])
        names = ("tables_in", "chunk_done", "squared", "sums_ready", "logged", "rn_ready", "gb_ready", "v_copied",
                 "decay_in", "decay_ready", "qk_ready", "turned", "kk_ready", "lt_masked", "at_half", "at_ready",
                 "bg_ready", "kbg_ready", "kdv_ready", "am_ready", "p_ready", "p_kept", "d_ready", "updated",
                 "uw_ready", "wt_kept", "u_kept", "ws_ready", "vn_ready", "o_ready", "ds_ready", "o_squared",
                 "o_summed", "o_logged", "ro_ready", "o_scaled", "s_ready", "stored")
        (tables_in, chunk_done, squared, sums_ready, logged, rn_ready, gb_ready, v_copied, decay_in, decay_ready,
         qk_ready, turned, kk_ready, lt_masked, at_half, at_ready, bg_ready, kbg_ready, kdv_ready, am_ready, p_ready,
         p_kept, d_ready, updated, uw_ready, wt_kept, u_kept, ws_ready, vn_ready, o_ready, ds_ready, o_squared,
         o_summed, o_logged, ro_ready, o_scaled, s_ready, stored) = [
            nc.alloc_semaphore("dp_" + s) for s in names]
        pages_in, q_zero, q_ready, k_turned, kt_kept, kt_used, pooled, pool_kept, sc_kept = [
            nc.alloc_semaphore("dp_" + s) for s in
            ("pages_in", "q_zero", "q_ready", "k_turned", "kt_kept", "kt_used", "pooled", "pool_kept", "sc_kept")]
        kp_in = [nc.alloc_semaphore(f"dp_kp_in{u}") for u in range(4)]
        block = ctx.enter_context(nc.Block())

        def samples(lv):
            return range(2 * (lv - 2), 2 * (lv - 2) + 2) if 2 <= lv < LEVELS - 1 else ()

        def bank(b):
            return r.ps[:, b, :].rearrange("p (h n) -> p h n", h=4)

        @block.sync
        def _(sp):
            for dst, src in ((level.rearrange("p l n -> p (l n)"), r.c_level), (upper[:], r.c_upper),
                             (rowsel[:].rearrange("p l n -> p (l n)"), r.c_rowsel), (ng[:], r.delta_ng),
                             (sw.pool, r.c_pool)):
                sp.dma_start(dst, src).then_inc(tables_in, 16)
            sp.dma_start(sw.pages, r.page_table.rearrange("(a b) n -> a (b n)", a=1)).then_inc(pages_in, 16)
            sp.wait_ge(pages_in, 16)
            with sp.Fori(0, NG) as c:
                for s in range(NS):
                    sp.wait_ge(k_turned, c * NS + (s + 1))
                    for j in range(PGRP):
                        page = sp.value_load(sw.pages[0:1, bass.ds(c * PGRP + (s * PAGES + j), 1)], min_val=0,
                                             max_val=n_pool - 1)
                        sp.dma_start(sw.KP[s % 4][:, j, :],
                                     cache[bass.ds(page, 1), :, 0:384].squeeze(0)).then_inc(kp_in[s % 4], 16)
            sp.wait_ge(s_ready, TT + 1)
            sp.dma_start(r.o_dS_p[0, 0].rearrange("h d e -> d h e"), S[:]).then_inc(stored, 16)
            sp.wait_ge(stored, 16)

        @block.scalar
        def _(act):
            act.preload_act_table_set("natural_log_exp_and_others")
            act.sem_inc(kt_kept, 2)
            with act.Fori(0, TT) as c:
                cols = bass.ds(c * P, P)
                act.wait_ge(chunk_done, c + 1)
                act.wait_ge(tables_in, 80)
                act.activation(SQ[:], r.H[:, Q_A:Q_A + 8, cols], ACT.Square).then_inc(squared, 1)
                act.copy(VT[:], r.H[:, V_A:V_A + 4, cols]).then_inc(v_copied, 1)
                act.wait_ge(sums_ready, c + 1)
                act.activation(RN[:].rearrange("p k n -> p (k n)"), r.ps[:, 0:2, :].rearrange("p b n -> p (b n)"),
                               ACT.Ln, bias=r.bias[:, 1:2]).then_inc(logged, 1)
                act.wait_ge(logged, c + 1)
                act.activation(RN[:], RN[:], ACT.Exp, scale=-0.5).then_inc(rn_ready, 1)
                act.wait_ge(decay_in, c + 1)
                act.activation(DL[:], DL[:], ACT.Exp)
                act.activation(EG[:], GB[:], ACT.Exp)
                act.activation(e4[:], tk[:, 4:12], ACT.Exp).then_inc(decay_ready, 1)
                act.wait_ge(decay_ready, c + 1)
                act.wait_ge(turned, c + 1)
                for h in H4:
                    act.activation(KD[:, h, :], bank(4)[:, h, :], ACT.Copy, scale=e4[:, 4 + h:5 + h])
                for h in H4:
                    mm = act.activation(VB[:, h, :], bank(5)[:, h, :], ACT.Copy, scale=tk[:, h:h + 1])
                mm.then_inc(kdv_ready, 1)
                for lv in range(LEVELS):
                    act.wait_ge(p_ready, c * LEVELS + (lv + 1))
                    act.copy(PS[:], bank(6)).then_inc(p_kept, 1)
                    for s in samples(lv):
                        act.wait_ge(k_turned, c * NS + (s + 5))
                        act.wait_ge(kt_used, c * NS + (s + 1))
                        act.copy(sw.KT[:, s % 2, :], r.ps[:, s % 2, :]).then_inc(kt_kept, 1)
                act.wait_ge(uw_ready, c + 1)
                act.copy(WT, bank(1)).then_inc(wt_kept, 1)
                act.wait_ge(o_ready, c + 1)
                act.activation(OS, bank(5), ACT.Square).then_inc(o_squared, 1)
                act.wait_ge(o_summed, c + 1)
                act.activation(RO[:], bank(7), ACT.Ln, bias=r.bias[:, 1:2], scale=1 / 128).then_inc(o_logged, 1)
                act.wait_ge(o_logged, c + 1)
                act.activation(RO[:], RO[:], ACT.Exp, scale=-0.5).then_inc(ro_ready, 1)

        @block.tensor
        def _(pe):
            pe.wait_ge(tables_in, 80)
            pe.wait_ge(q_ready, 1)
            pe.sem_inc(k_turned, 4)
            pe.sem_inc(kt_used, 2)

            def turn(c, s):
                pe.wait_ge(kp_in[s % 4], c * 128 + (s // 4 + 1) * 64)
                pe.wait_ge(pool_kept, c * NS + (s + 1))
                for part in range(2):
                    for j in range(PGRP):
                        mm = pe.matmul(r.ps[:, 4 + s % 2, 16 * part + 4 * j:16 * part + 4 * j + 4],
                                       sw.KP[s % 4][:, j, part * P:(part + 1) * P], sw.pool, start=True, stop=True)
                mm.then_inc(pooled, 1)
                pe.wait_ge(kt_kept, c * NS + (s + 1))
                for j in range(PGRP):
                    mm = pe.transpose(r.ps[:, s % 2, j * P:(j + 1) * P], sw.KP[s % 4][:, j, 256:384], r.ident[:])
                mm.then_inc(k_turned, 1)

            def scores(c, s):
                pe.wait_ge(kt_kept, c * NS + (s + 3))
                pe.matmul(r.ps[0:R, 2, :], sw.Qs[:, s, :], sw.KT[:, s % 2, :], start=(s == 0),
                          stop=(s == NS - 1)).then_inc(kt_used, 1)

            def step(c, n):
                if 0 <= n < NS:
                    turn(c, n)
                if 1 <= n <= NS:
                    scores(c, n - 1)

            with pe.Fori(0, TT) as c:
                cols = bass.ds(c * P, P)
                pe.wait_ge(squared, c + 1)
                pe.matmul(r.ps[:, 0, :], r.ones[:], SQ[:, 0:4, :], start=True, stop=True)
                pe.matmul(r.ps[:, 1, :], r.ones[:], SQ[:, 4:8, :], start=True, stop=True)
                pe.wait_ge(sc_kept, c + 1)
                for j in range(8):
                    mm = pe.matmul(bank(2 + j // 4)[:, j % 4, :], rowsel[:, j, :], r.H[0:NSMALL, SMALL, cols],
                                   start=True, stop=True)
                mm.then_inc(sums_ready, 1)
                pe.wait_ge(v_copied, c + 1)
                for h in H4:
                    pe.transpose(bank(5)[:, h, :], VT[:, h, :], r.ident[:])
                pe.wait_ge(qk_ready, c + 1)
                for h in H4:
                    mm = pe.transpose(bank(4)[:, h, :], KT[:, h, :], r.ident[:])
                mm.then_inc(turned, 1)
                for h in H4:
                    pe.matmul(bank(0)[:, h, :], KT[:, h, :], KT[:, h, :], start=True, stop=True)
                for h in H4:
                    mm = pe.matmul(bank(1)[:, h, :], KT[:, h, :], QT[:, h, :], start=True, stop=True)
                mm.then_inc(kk_ready, 1)
                for lv in range(LEVELS):
                    pe.wait_ge(am_ready, c * LEVELS + (lv + 1))
                    pe.wait_ge(updated, c * (LEVELS + 1) + (lv + 1))
                    for h in H4:
                        mm = pe.matmul(bank(6)[:, h, :], AM[:, lv % 2, h, :], Dm[:, h, :], start=True, stop=True)
                    mm.then_inc(p_ready, 1)
                    step(c, 2 * (lv - 2))
                    pe.wait_ge(p_kept, c * LEVELS + (lv + 1))
                    if lv < LEVELS - 1:
                        for h in H4:
                            pe.matmul(bank(7)[:, h, :], DT[:, h, :], PS[:, h, :], start=True, stop=True)
                    for h in H4:
                        mm = pe.matmul(bank(3)[:, h, :], PS[:, h, :], DT[:, h, :], start=True, stop=True)
                    mm.then_inc(d_ready, 1)
                    step(c, 2 * (lv - 2) + 1)
                pe.wait_ge(pool_kept, c * NS + (NS + 2))
                pe.wait_ge(updated, c * (LEVELS + 1) + (LEVELS + 1))
                pe.wait_ge(kdv_ready, c + 1)
                pe.wait_ge(kbg_ready, c + 1)
                for h in H4:
                    pe.matmul(bank(0)[:, h, :], DT[:, h, :], VB[:, h, :], start=True, stop=True)
                for h in H4:
                    mm = pe.matmul(bank(1)[:, h, :], KBG[:, h, :], DT[:, h, :], start=True, stop=True)
                mm.then_inc(uw_ready, 1)
                pe.wait_ge(wt_kept, c + 1)
                pe.wait_ge(s_ready, c + 1)
                for h in H4:
                    mm = pe.matmul(bank(4)[:, h, :], WT[:, h, :], S[:, h, :], start=True, stop=True)
                mm.then_inc(ws_ready, 1)
                pe.wait_ge(vn_ready, c + 1)
                for h in H4:
                    pe.matmul(bank(5)[:, h, :], S[:, h, :], QG[:, h, :], start=True, stop=False)
                    mm = pe.matmul(bank(5)[:, h, :], VN[:, h, :], QK[:, h, :], start=False, stop=True)
                mm.then_inc(o_ready, 1)
                for h in H4:
                    mm = pe.matmul(bank(6)[:, h, :], KD[:, h, :], VN[:, h, :], start=True, stop=True)
                mm.then_inc(ds_ready, 1)
                pe.wait_ge(o_squared, c + 1)
                pe.matmul(r.ps[:, 7, :], r.ones[:], OS, start=True, stop=True).then_inc(o_summed, 1)

        def means(v, c, s):
            v.wait_ge(pooled, c * NS + (s + 1))
            v.tensor_copy(sw.KC[:, s, bass.ds(c * 16, 16)], r.ps[:, 4 + s % 2, 0:16])
            v.tensor_copy(sw.VCT[:, s, bass.ds(c * 16, 16)], r.ps[:, 4 + s % 2, 16:32]).then_inc(pool_kept, 1)

        def update(v, c, lv):
            v.wait_ge(d_ready, c * LEVELS + (lv + 1))
            if lv < LEVELS - 1:
                v.tensor_tensor(Dm[:], Dm[:], bank(7), ALU.subtract)
            v.tensor_tensor(DT[:], DT[:], bank(3), ALU.subtract).then_inc(updated, 1)

        @block.vector
        def _(v):
            v.wait_ge(tables_in, 80)
            v.memset(S[:], 0.0).then_inc(s_ready, 1)
            v.sem_inc(chunk_done, 1)
            v.sem_inc(pool_kept, 2)
            v.sem_inc(sc_kept, 1)
            v.memset(sw.Q, 0.0).then_inc(q_zero, 1)
            v.wait_ge(q_zero, 1)
            for i in range(4):
                for g in range(2):
                    h = i + 4 * g
                    mm = v.tensor_copy(sw.Q[64 * g:64 * g + 64, h:h + 72 * (NS - 1) + 1:72],
                                       r.H[64 * g:64 * g + 64, Q_B + i, T:N])
            mm.then_inc(q_ready, 1)
            ident4 = r.ident[:].unsqueeze(1).to_broadcast([P, 4, P])
            upper4 = upper[:].unsqueeze(1).to_broadcast([P, 4, P])
            with v.Fori(0, TT) as c:
                cols = bass.ds(c * P, P)
                v.wait_ge(chunk_done, c + 1)
                v.tensor_copy(tk[:, 0:4], r.tok[:, bass.ds(c, 1), R_BETA:R_BETA + 4].squeeze(1))
                v.tensor_copy(tk[:, 4:8], r.tok[:, bass.ds(c, 1), R_G:R_G + 4].squeeze(1))
                v.tensor_copy(Dm[:], ident4)
                v.tensor_copy(DT[:], ident4).then_inc(updated, 1)
                v.wait_ge(updated, c * (LEVELS + 1) + 1)
                v.wait_ge(sums_ready, c + 1)
                v.tensor_copy(GB[:], bank(3)).then_inc(gb_ready, 1)
                v.wait_ge(gb_ready, c + 1)
                for h in H4:
                    v.tensor_scalar(DL[:, h, :], GB[:, h, :], tk[:, 4 + h:5 + h], 0.0, ALU.subtract, ALU.min)
                v.tensor_tensor(tk[:, 8:12], GB[:, :, P - 1], tk[:, 4:8], ALU.subtract).then_inc(decay_in, 1)
                v.wait_ge(rn_ready, c + 1)
                v.scalar_tensor_tensor(out=QT[:], in0=r.H[:, Q_A:Q_A + 4, cols], scalar=128 ** -0.5, in1=RN[:, 0:4, :],
                                       op0=ALU.mult, op1=ALU.mult)
                v.tensor_tensor(KT[:], r.H[:, K_A:K_A + 4, cols], RN[:, 4:8, :], ALU.mult).then_inc(qk_ready, 1)
                v.wait_ge(decay_ready, c + 1)
                v.tensor_tensor(DL[:], DL[:], upper4, ALU.mult).then_inc(lt_masked, 1)
                v.tensor_tensor(bg[:], tk[:, 0:4], e4[:, 0:4], ALU.mult).then_inc(bg_ready, 1)
                v.wait_ge(lt_masked, c + 1)
                v.wait_ge(kk_ready, c + 1)
                v.tensor_tensor(AT[:], bank(0), DL[:], ALU.mult).then_inc(at_half, 1)
                v.wait_ge(at_half, c + 1)
                v.tensor_tensor(AT[:], AT[:], bank(2), ALU.mult).then_inc(at_ready, 1)
                v.wait_ge(at_ready, c + 1)
                for lv in range(LEVELS):
                    if lv >= 2:
                        v.wait_ge(p_ready, c * LEVELS + (lv - 1))
                    v.tensor_tensor(AM[:, lv % 2], AT[:], level[:, lv, :].unsqueeze(1).to_broadcast([P, 4, P]),
                                    ALU.mult).then_inc(am_ready, 1)
                    if lv == 0:
                        v.tensor_tensor(QK[:], bank(1), DL[:], ALU.mult)
                        v.wait_ge(qk_ready, c + 1)
                        v.tensor_tensor(QG[:], QT[:], EG[:], ALU.mult)
                    if lv == 1:
                        v.wait_ge(bg_ready, c + 1)
                        v.wait_ge(turned, c + 1)
                        v.wait_ge(kdv_ready, c + 1)
                        for h in H4:
                            mm = v.tensor_scalar(KBG[:, h, :], bank(4)[:, h, :], bg[:, h:h + 1], None, ALU.mult)
                        mm.then_inc(kbg_ready, 1)
                    if samples(lv - 2):
                        means(v, c, samples(lv - 2)[1])
                    if samples(lv - 1):
                        means(v, c, samples(lv - 1)[0])
                    if lv:
                        update(v, c, lv - 1)
                means(v, c, NS - 1)
                update(v, c, LEVELS - 1)
                v.wait_ge(uw_ready, c + 1)
                v.tensor_copy(U, bank(0)).then_inc(u_kept, 1)
                v.wait_ge(u_kept, c + 1)
                v.wait_ge(ws_ready, c + 1)
                v.tensor_tensor(VN, U, bank(4), ALU.subtract).then_inc(vn_ready, 1)
                v.wait_ge(kt_used, c * NS + (NS + 2))
                v.tensor_copy(sw.SC[:, bass.ds(c * (PGRP * P), PGRP * P)], r.ps[0:R, 2, :]).then_inc(sc_kept, 1)
                v.wait_ge(ds_ready, c + 1)
                for h in H4:
                    mm = v.scalar_tensor_tensor(out=S[:, h, :], in0=S[:, h, :], scalar=EG[:, h, P - 1:P],
                                                in1=bank(6)[:, h, :], op0=ALU.mult, op1=ALU.add)
                mm.then_inc(s_ready, 1)
                v.wait_ge(ro_ready, c + 1)
                v.scalar_tensor_tensor(out=RO[:], in0=bank(5), scalar=ng[:, 0:1], in1=RO[:], op0=ALU.mult,
                                       op1=ALU.mult).then_inc(o_scaled, 1)
                v.wait_ge(o_scaled, c + 1)
                v.tensor_tensor(r.H[:, GATE_A:GATE_A + 4, cols], RO[:], r.H[:, GATE_A:GATE_A + 4, cols],
                                ALU.mult).then_inc(chunk_done, 1)


def gla_gate_phase(nc, r):
    with phase(nc) as ctx:
        g2 = ctx.enter_context(nc.sbuf_tensor("gg_w", [16, 512], F32))
        b2 = ctx.enter_context(nc.sbuf_tensor("gg_b", [P, 4], F32))
        az = ctx.enter_context(nc.sbuf_tensor("gg_az", [P, 2, N], F32))
        w_in, product, biased, absed, exped, logged, lowered, done = [
            nc.alloc_semaphore("gg_" + s) for s in
            ("w_in", "product", "biased", "absed", "exped", "logged", "lowered", "done")]
        block = ctx.enter_context(nc.Block())

        @block.sync
        def _(sp):
            sp.dma_start(g2[:], r.w_g2).then_inc(w_in, 16)
            sp.dma_start(b2[:], r.b_g2).then_inc(w_in, 16)

        @block.tensor
        def _(pe):
            pe.wait_ge(w_in, 32)
            for m in range(4):
                if m >= 2:
                    pe.wait_ge(biased, m - 1)
                for c in range(NB):
                    mm = pe.matmul(r.ps[:, m % 2 * 3 + c, 0:CW], g2[:, m * P:(m + 1) * P],
                                   r.H[0:16, OG1, c * CW:(c + 1) * CW], start=True, stop=True)
                mm.then_inc(product, 1)

        @block.vector
        def _(v):
            def log_sigmoid(m):
                v.wait_ge(logged, m + 1)
                v.scalar_tensor_tensor(out=r.LA[:, m, :], in0=r.LA[:, m, :], scalar=0.0, in1=az[:, m % 2, :],
                                       op0=ALU.min, op1=ALU.subtract).then_inc(lowered, 1)
                v.wait_ge(lowered, m + 1)
                v.tensor_scalar(r.LA[:, m, :], r.LA[:, m, :], 1 / 16, None, ALU.mult).then_inc(done, 1)

            v.wait_ge(w_in, 32)
            for m in range(4):
                v.wait_ge(product, m + 1)
                for c in range(NB):
                    mm = v.tensor_scalar(r.LA[:, m, c * CW:(c + 1) * CW], r.ps[:, m % 2 * 3 + c, 0:CW], b2[:, m:m + 1],
                                         None, ALU.add)
                mm.then_inc(biased, 1)
                if m >= 2:
                    log_sigmoid(m - 2)
                v.wait_ge(biased, m + 1)
                v.scalar_tensor_tensor(out=az[:, m % 2, :], in0=r.LA[:, m, :], scalar=-1.0, in1=r.LA[:, m, :],
                                       op0=ALU.mult, op1=ALU.max).then_inc(absed, 1)
            log_sigmoid(2)
            log_sigmoid(3)

        @block.scalar
        def _(act):
            act.preload_act_table_set("natural_log_exp_and_others")
            for m in range(4):
                act.wait_ge(absed, m + 1)
                act.activation(az[:, m % 2, :], az[:, m % 2, :], ACT.Exp, scale=-1.0).then_inc(exped, 1)
                act.wait_ge(exped, m + 1)
                act.activation(az[:, m % 2, :], az[:, m % 2, :], ACT.Ln, bias=1.0).then_inc(logged, 1)
            act.activation(r.H[:, OR_:OR_ + 8, :], r.H[:, OR_:OR_ + 8, :], ACT.Silu)


def gla_prompt_phase(nc, r):
    H4 = range(HEADS)
    with phase(nc) as ctx:
        def sb(name, shape):
            return ctx.enter_context(nc.sbuf_tensor("gp_" + name, shape, F32))

        upper, keep16, one = sb("upper", [P, P]), sb("keep16", [P, P]), sb("one", [P, P])
        gn = sb("gn", [P, 2])
        VT, VK, OS = sb("vt", [P, 8, P]), sb("vk", [P, 8, P]), sb("os", [P, 8, P])
        B, BL, QL, QB, KD, KT, ATT, RO = [sb(n, [P, 4, P]) for n in ("b", "bl", "ql", "qb", "kd", "kt", "att", "ro")]
        BR = sb("br", [P, 4, 8])
        GL = sb("gl", [P, 4])
        EX = sb("ex", [P, 2, 8, P])
        S = sb("s", [P, 4, GV])
        names = ("tables_in", "chunk_done", "v_copied", "v_turned", "v_kept", "scanned", "ref_ready", "q_exped",
                 "kd_exped", "kd_ready", "kd_turned", "kd_kept", "q_ready", "ex_ready", "kx_ready", "att_ready",
                 "att_kept", "o_ready", "ds_ready", "s_ready", "o_squared", "o_summed", "o_logged", "ro_ready",
                 "o_scaled", "stored", "zeroed")
        (tables_in, chunk_done, v_copied, v_turned, v_kept, scanned, ref_ready, q_exped, kd_exped, kd_ready, kd_turned,
         kd_kept, q_ready, ex_ready, kx_ready, att_ready, att_kept, o_ready, ds_ready, s_ready, o_squared, o_summed,
         o_logged, ro_ready, o_scaled, stored, zeroed) = [nc.alloc_semaphore("gp_" + s) for s in names]
        block = ctx.enter_context(nc.Block())

        def bank(b):
            return r.ps[:, b, :].rearrange("p (h n) -> p h n", h=4)

        def pair(b):
            return r.ps[:, b:b + 2, :].rearrange("p b (h n) -> p (b h) n", h=4)

        @block.sync
        def _(sp):
            sp.dma_start(upper[:], r.c_upper).then_inc(tables_in, 16)
            sp.dma_start(gn[:], r.gla_ng).then_inc(tables_in, 16)
            sp.wait_ge(s_ready, TT + 1)
            sp.dma_start(r.o_gS_p[0, 0].rearrange("h d e -> d h e"), S[:]).then_inc(stored, 16)
            sp.wait_ge(stored, 16)

        @block.scalar
        def _(act):
            act.preload_act_table_set("natural_log_exp_and_others")
            act.wait_ge(zeroed, 1)
            with act.Fori(0, TT) as c:
                cols = bass.ds(c * P, P)
                act.wait_ge(chunk_done, c + 1)
                act.wait_ge(tables_in, 32)
                act.copy(VT[:], r.H[:, OV:OV + 8, cols]).then_inc(v_copied, 1)
                act.wait_ge(ref_ready, c + 1)
                act.activation(QL[:], BL[:], ACT.Exp)
                act.activation(QB[:], B[:], ACT.Exp).then_inc(q_exped, 1)
                act.activation(GL[:], B[:, :, P - 1], ACT.Exp)
                for h in H4:
                    mm = act.activation(KD[:, h, :], B[:, h, :], ACT.Exp, bias=B[:, h, P - 1:P], scale=-1.0)
                mm.then_inc(kd_exped, 1)
                act.wait_ge(v_turned, c + 1)
                act.copy(VK[:], pair(0)).then_inc(v_kept, 1)
                for h in H4:
                    if h >= 2:
                        act.wait_ge(att_ready, c * 4 + (h - 1))
                    for b in range(8):
                        mm = act.activation(EX[:, h % 2, b, 0:16 * (b + 1)], B[:, h, 0:16 * (b + 1)], ACT.Exp,
                                            bias=BR[:, h, b:b + 1], scale=-1.0)
                    mm.then_inc(ex_ready, 1)
                    if h == 1:
                        act.wait_ge(kd_turned, c + 1)
                        act.copy(KT[:], bank(2)).then_inc(kd_kept, 1)
                act.wait_ge(o_ready, c + 1)
                act.activation(OS[:], pair(4), ACT.Square).then_inc(o_squared, 1)
                act.wait_ge(o_summed, c + 1)
                act.activation(RO[:], bank(0), ACT.Ln, bias=r.bias[:, 1:2], scale=1 / GV).then_inc(o_logged, 1)
                act.wait_ge(o_logged, c + 1)
                act.activation(RO[:], RO[:], ACT.Exp, scale=-0.5).then_inc(ro_ready, 1)

        @block.tensor
        def _(pe):
            pe.wait_ge(tables_in, 32)
            with pe.Fori(0, TT) as c:
                pe.wait_ge(v_copied, c + 1)
                for j in range(8):
                    mm = pe.transpose(pair(0)[:, j, :], VT[:, j, :], r.ident[:])
                mm.then_inc(v_turned, 1)
                pe.wait_ge(kd_ready, c + 1)
                for h in H4:
                    mm = pe.transpose(bank(2)[:, h, :], KD[:, h, :], r.ident[:])
                mm.then_inc(kd_turned, 1)
                pe.wait_ge(q_ready, c + 1)
                for h in H4:
                    pe.wait_ge(kx_ready, c * 4 + (h + 1))
                    for b in range(8):
                        mm = pe.matmul(bank(3)[:, h, 16 * b:16 * b + 16], EX[:, h % 2, b, :],
                                       QL[:, h, 16 * b:16 * b + 16], start=True, stop=True)
                    mm.then_inc(att_ready, 1)
                pe.wait_ge(att_kept, c + 1)
                pe.wait_ge(s_ready, c + 1)
                pe.wait_ge(v_kept, c + 1)
                for h in H4:
                    for e in range(2):
                        pe.matmul(pair(4)[:, 2 * h + e, :], S[:, h, e * P:(e + 1) * P], QB[:, h, :], start=True,
                                  stop=False)
                        mm = pe.matmul(pair(4)[:, 2 * h + e, :], VK[:, 2 * h + e, :], ATT[:, h, :], start=False,
                                       stop=True)
                mm.then_inc(o_ready, 1)
                pe.wait_ge(kd_kept, c + 1)
                for h in H4:
                    mm = pe.matmul(pair(6)[:, 2 * h:2 * h + 2, :], KT[:, h, :], VK[:, 2 * h:2 * h + 2, :], start=True,
                                   stop=True)
                mm.then_inc(ds_ready, 1)
                pe.wait_ge(o_squared, c + 1)
                sq = OS[:].rearrange("p (h e) n -> p h e n", e=2)
                pe.matmul(r.ps[:, 0, :], r.ones[:], sq[:, :, 0, :], start=True, stop=False)
                pe.matmul(r.ps[:, 0, :], r.ones[:], sq[:, :, 1, :], start=False, stop=True).then_inc(o_summed, 1)

        @block.vector
        def _(v):
            v.memset(S[:], 0.0).then_inc(s_ready, 1)
            v.memset(EX[:], 0.0)
            v.memset(one[:], 1.0)
            v.memset(keep16[:], 1.0).then_inc(zeroed, 1)
            v.wait_ge(zeroed, 1)
            v.memset(keep16[:].rearrange("p (b t) -> p b t", t=16)[:, :, 0:1], 0.0).then_inc(zeroed, 1)
            v.wait_ge(zeroed, 2)
            v.wait_ge(tables_in, 32)
            v.sem_inc(chunk_done, 1)
            with v.Fori(0, TT) as c:
                cols = bass.ds(c * P, P)
                v.wait_ge(chunk_done, c + 1)
                for h in H4:
                    la = r.LA[:, h, cols]
                    v.tensor_tensor_scan(B[:, h, :], one[:], la, 0.0, ALU.mult, ALU.add)
                    mm = v.tensor_tensor_scan(BL[:, h, :], keep16[:], la, 0.0, ALU.mult, ALU.add)
                mm.then_inc(scanned, 1)
                v.wait_ge(scanned, c + 1)
                v.tensor_tensor(BR[:], B[:].rearrange("p h (b t) -> p h b t", t=16)[:, :, :, 0],
                                BL[:].rearrange("p h (b t) -> p h b t", t=16)[:, :, :, 0],
                                ALU.subtract).then_inc(ref_ready, 1)
                q, k = r.H[:, OQ:OQ + 4, cols], r.H[:, OK:OK + 4, cols]
                v.wait_ge(q_exped, c + 1)
                v.scalar_tensor_tensor(out=QL[:], in0=q, scalar=128 ** -0.5, in1=QL[:], op0=ALU.mult, op1=ALU.mult)
                v.scalar_tensor_tensor(out=QB[:], in0=q, scalar=128 ** -0.5, in1=QB[:], op0=ALU.mult,
                                       op1=ALU.mult).then_inc(q_ready, 1)
                v.wait_ge(kd_exped, c + 1)
                v.tensor_tensor(KD[:], k, KD[:], ALU.mult).then_inc(kd_ready, 1)
                for h in H4:
                    v.wait_ge(ex_ready, c * 4 + (h + 1))
                    v.tensor_tensor(EX[:, h % 2], EX[:, h % 2],
                                    r.H[:, OK + h, cols].unsqueeze(1).to_broadcast([P, 8, P]),
                                    ALU.mult).then_inc(kx_ready, 1)
                v.wait_ge(att_ready, c * 4 + 4)
                v.tensor_tensor(ATT[:], bank(3), upper[:].unsqueeze(1).to_broadcast([P, 4, P]),
                                ALU.mult).then_inc(att_kept, 1)
                v.wait_ge(ds_ready, c + 1)
                for h in H4:
                    mm = v.scalar_tensor_tensor(out=S[:, h, :], in0=S[:, h, :], scalar=GL[:, h:h + 1],
                                                in1=pair(6)[:, 2 * h:2 * h + 2, :].rearrange("p e n -> p (e n)"),
                                                op0=ALU.mult, op1=ALU.add)
                mm.then_inc(s_ready, 1)
                v.wait_ge(ro_ready, c + 1)
                out = OS[:].rearrange("p (h e) n -> p h e n", e=2)
                got = pair(4).rearrange("p (h e) n -> p h e n", e=2)
                for e in range(2):
                    mm = v.scalar_tensor_tensor(out=out[:, :, e, :], in0=got[:, :, e, :], scalar=gn[:, e:e + 1],
                                                in1=RO[:], op0=ALU.mult, op1=ALU.mult)
                mm.then_inc(o_scaled, 1)
                v.wait_ge(o_scaled, c + 1)
                v.tensor_tensor(r.H[:, OR_:OR_ + 8, cols], OS[:], r.H[:, OR_:OR_ + 8, cols],
                                ALU.mult).then_inc(chunk_done, 1)


def sample_state_phase(nc, r, delta):
    E = 1 if delta else 2
    tag = "ds_" if delta else "gs_"
    Qc, Kc, Vc, Oc = (Q_A, K_A, V_A, GATE_A) if delta else (OQ, OK, OV, OR_)
    state_in = r.state_delta_S[0] if delta else r.state_gla_S[0]
    state_out = r.o_dS_s[0] if delta else r.o_gS_s[0]
    q, k = r.H[:, Qc:Qc + 4, T:N], r.H[:, Kc:Kc + 4, T:N]
    val, gate = r.H[:, Vc:Vc + 4 * E, T:N], r.H[:, Oc:Oc + 4 * E, T:N]
    with phase(nc) as ctx:
        def sb(name, shape):
            return ctx.enter_context(nc.sbuf_tensor(tag + name, shape, F32))

        S = sb("s", [P, NS, 4, E * P])
        tmp = r.H[:, Kc:Kc + 2, 0:4 * E * P].rearrange("p u (h e) -> p u h e", h=4)
        pick, ng = sb("pick", [NS, NS, P]), sb("ng", [P, E])
        qn, kn, dec, kw, prod, qk = [sb(n, [P, 4, NS]) for n in ("qn", "kn", "dec", "kw", "prod", "qk")]
        sq, rn = sb("sq", [P, 8, NS]), sb("rn", [P, 8, NS])
        vn, o, os_ = sb("vn", [P, 4 * E, NS]), sb("o", [P, 4 * E, NS]), sb("os", [P, 4 * E, NS])
        vrow = r.H[0:NS, Kc + 2, 0:4 * E * P]
        ro = sb("ro", [P, 4, NS])
        rowsel = sb("rowsel", [NSMALL, 8, P]) if delta else None
        bb = sb("bb", [P, 8, NS])
        s_in = [nc.alloc_semaphore(tag + f"s_in{i}") for i in range(NS)]
        tables_in, act_step, dve_step, pe_step, spread, outer, moved, stored = [
            nc.alloc_semaphore(tag + s) for s in
            ("tables_in", "act_step", "dve_step", "pe_step", "spread", "outer", "moved", "stored")]
        block = ctx.enter_context(nc.Block())
        nt = 3 if delta else 2

        def small(b, n):
            return r.ps[:, b, 0:n * NS].rearrange("p (h s) -> p h s", s=NS)

        @block.sync
        def _(sp):
            sp.dma_start(pick[:].rearrange("p s n -> p (s n)"), r.c_pick).then_inc(tables_in, 16)
            sp.dma_start(ng[:], r.delta_ng if delta else r.gla_ng).then_inc(tables_in, 16)
            if delta:
                sp.dma_start(rowsel[:].rearrange("p l n -> p (l n)"), r.c_rowsel).then_inc(tables_in, 16)
            for s in range(NS):
                sp.dma_start(S[:, s], state_in[s].rearrange("h d e -> d h e")).then_inc(s_in[s], 16)
            for s in range(NS):
                sp.wait_ge(moved, s + 1)
                sp.dma_start(state_out[s].rearrange("h d e -> d h e"), S[:, s]).then_inc(stored, 16)
            sp.wait_ge(stored, 16 * NS)

        @block.scalar
        def _(act):
            act.preload_act_table_set("natural_log_exp_and_others")
            act.wait_ge(tables_in, 16 * nt)
            if delta:
                act.activation(sq[:], r.H[:, Qc:Qc + 8, T:N], ACT.Square).then_inc(act_step, 1)
                act.wait_ge(pe_step, 1)
                act.activation(rn[:], small(0, 8), ACT.Ln, bias=r.bias[:, 1:2]).then_inc(act_step, 1)
                act.wait_ge(act_step, 2)
                act.activation(rn[:], rn[:], ACT.Exp, scale=-0.5)
                act.activation(dec[:], small(1, 8)[:, 4:8, :], ACT.Exp)
                act.copy(bb[:], small(1, 8)).then_inc(act_step, 1)
            else:
                act.activation(dec[:], r.LA[:, :, T:N], ACT.Exp).then_inc(act_step, 1)
                act.sem_inc(act_step, 2)
            act.wait_ge(pe_step, 4)
            for j in range(E):
                mm = act.copy(vrow[:, j * 512:(j + 1) * 512], r.ps[0:NS, 4 + j, :])
            mm.then_inc(act_step, 1)
            for s in range(NS):
                act.wait_ge(spread, s + 1)
                if s >= 2:
                    act.wait_ge(moved, s - 1)
                for h in range(4):
                    src = r.ps[:, s % 2 * 2:s % 2 * 2 + E, :].rearrange("p b n -> p (b n)")[:, h * E * P:(h + 1) * E * P]
                    mm = act.activation(tmp[:, s % 2, h, :], src, ACT.Copy, scale=kn[:, h, s:s + 1])
                mm.then_inc(outer, 1)
            act.wait_ge(dve_step, 6)
            act.activation(os_[:], o[:], ACT.Square).then_inc(act_step, 1)
            act.wait_ge(pe_step, 5)
            act.activation(ro[:], small(7, 4), ACT.Ln, bias=r.bias[:, 1:2], scale=1 / (E * P)).then_inc(act_step, 1)
            act.wait_ge(act_step, 6)
            act.activation(ro[:], ro[:], ACT.Exp, scale=-0.5).then_inc(act_step, 1)

        @block.vector
        def _(v):
            v.wait_ge(tables_in, 16 * nt)
            v.wait_ge(act_step, 3)
            if delta:
                v.scalar_tensor_tensor(out=qn[:], in0=q, scalar=128 ** -0.5, in1=rn[:, 0:4, :], op0=ALU.mult,
                                       op1=ALU.mult)
                v.tensor_tensor(kn[:], k, rn[:, 4:8, :], ALU.mult).then_inc(dve_step, 1)
                v.wait_ge(dve_step, 1)
                v.tensor_tensor(prod[:], qn[:], kn[:], ALU.mult)
                v.tensor_tensor(kw[:], kn[:], dec[:], ALU.mult).then_inc(dve_step, 1)
                v.wait_ge(dve_step, 2)
                v.tensor_tensor(kw[:], kw[:], bb[:, 0:4, :], ALU.mult)
                v.tensor_tensor(qn[:], qn[:], dec[:], ALU.mult)
                v.tensor_tensor(vn[:], val, bb[:, 0:4, :], ALU.mult).then_inc(dve_step, 1)
            else:
                v.tensor_copy(kn[:], k)
                v.tensor_scalar(qn[:], q, 128 ** -0.5, None, ALU.mult).then_inc(dve_step, 1)
                v.wait_ge(dve_step, 1)
                v.tensor_tensor(prod[:], qn[:], k, ALU.mult).then_inc(dve_step, 1)
                v.wait_ge(dve_step, 2)
                v.tensor_tensor(qn[:], qn[:], dec[:], ALU.mult)
                v.tensor_copy(vn[:], val).then_inc(dve_step, 1)
            v.wait_ge(pe_step, 2)
            mm = v.tensor_copy(qk[:], small(6, 4))
            if delta:
                mm = v.tensor_tensor(vn[:], vn[:], small(2, 4), ALU.subtract)
            mm.then_inc(dve_step, 1)
            v.wait_ge(dve_step, 4)
            v.wait_ge(pe_step, 3)
            v.tensor_tensor(o[:].rearrange("p (h e) s -> p h e s", e=E), vn[:].rearrange("p (h e) s -> p h e s", e=E),
                            qk[:].unsqueeze(2).to_broadcast([P, 4, E, NS]), ALU.mult).then_inc(dve_step, 1)
            v.wait_ge(dve_step, 5)
            v.tensor_tensor(o[:], o[:], small(3, 4 * E), ALU.add).then_inc(dve_step, 1)
            for s in range(NS):
                v.wait_ge(outer, s + 1)
                for h in range(4):
                    mm = v.scalar_tensor_tensor(out=S[:, s, h, :], in0=S[:, s, h, :], scalar=dec[:, h, s:s + 1],
                                                in1=tmp[:, s % 2, h, :], op0=ALU.mult, op1=ALU.add)
                mm.then_inc(moved, 1)
            v.wait_ge(act_step, 7)
            ov = o[:].rearrange("p (h e) s -> p h e s", e=E)
            for e in range(E):
                mm = v.scalar_tensor_tensor(out=ov[:, :, e, :], in0=ov[:, :, e, :], scalar=ng[:, e:e + 1], in1=ro[:],
                                            op0=ALU.mult, op1=ALU.mult)
            mm.then_inc(dve_step, 1)
            v.wait_ge(dve_step, 7)
            v.tensor_tensor(gate, gate, o[:], ALU.mult)

        @block.tensor
        def _(pe):
            pe.wait_ge(tables_in, 16 * nt)
            if delta:
                pe.wait_ge(act_step, 1)
                pe.matmul(r.ps[:, 0, 0:8 * NS], r.ones[:], sq[:], start=True, stop=True)
                for j in range(8):
                    mm = pe.matmul(small(1, 8)[:, j, :], rowsel[:, j, :], r.H[0:NSMALL, SMALL, T:N], start=True,
                                   stop=True)
                mm.then_inc(pe_step, 1)
            else:
                pe.sem_inc(pe_step, 1)
            pe.wait_ge(dve_step, 3)
            pe.matmul(r.ps[:, 6, 0:4 * NS], r.ones[:], prod[:], start=True, stop=True)
            for s in range(NS):
                pe.wait_ge(s_in[s], 16)
                if delta:
                    for h in range(4):
                        pe.matmul(small(2, 4)[:, h, s:s + 1], S[:, s, h, :], kw[:, h, s:s + 1], start=True, stop=True)
            pe.matmul(r.ps[:, 7, 0:4 * NS], r.ones[:], prod[:], start=True, stop=True).then_inc(pe_step, 1)
            for s in range(NS):
                for h in range(4):
                    for e in range(E):
                        mm = pe.matmul(small(3, 4 * E)[:, h * E + e, s:s + 1], S[:, s, h, e * P:(e + 1) * P],
                                       qn[:, h, s:s + 1], start=True, stop=True)
            mm.then_inc(pe_step, 1)
            pe.wait_ge(dve_step, 4)
            for j in range(4 * E):
                mm = pe.transpose(r.ps[0:NS, 4 + j // 4, j % 4 * P:(j % 4 + 1) * P], vn[:, j, :], r.ident[:])
            mm.then_inc(pe_step, 1)
            pe.wait_ge(act_step, 4)
            pe.wait_ge(dve_step, 6)
            for s in range(NS):
                if s >= 2:
                    pe.wait_ge(outer, s - 1)
                for j in range(E):
                    mm = pe.matmul(r.ps[:, s % 2 * 2 + j, :], pick[:, s, :], vrow[:, j * 512:(j + 1) * 512],
                                   start=True, stop=True)
                mm.then_inc(spread, 1)
            pe.wait_ge(act_step, 5)
            if delta:
                pe.matmul(r.ps[:, 7, 0:4 * NS], r.ones[:], os_[:], start=True, stop=True).then_inc(pe_step, 1)
            else:
                ov = os_[:].rearrange("p (h e) s -> p h e s", e=2)
                pe.matmul(r.ps[:, 7, 0:4 * NS], r.ones[:], ov[:, :, 0, :], start=True, stop=False)
                pe.matmul(r.ps[:, 7, 0:4 * NS], r.ones[:], ov[:, :, 1, :], start=False,
                          stop=True).then_inc(pe_step, 1)


def nsa_sample_phase(nc, r):
    flat = r.H[:].rearrange("p k n -> p (k n)")
    R = 64
    cache = r.cache.rearrange("n e t c g d -> (n e) t (c g d)")
    n_pool = r.cache.shape[0]
    win = r.state_nsa_win[0].rearrange("b (j p) c g d -> b p j c (g d)", p=P)
    at = [0]

    def room(rows, n):
        at[0] += n
        assert at[0] <= 12 * N
        return flat[0:rows, at[0] - n:at[0]]

    PAST = PAGES * P
    SW = room(R, 513)
    PT = room(P, 37 * R).rearrange("p (n q) -> p n q", q=R)
    VC = room(P, NS * P).rearrange("p (s n) -> p s n", s=NS)
    with phase(nc) as ctx:
        def sb(name, shape, dt=F32):
            return ctx.enter_context(nc.sbuf_tensor("ns_" + name, shape, dt))

        sw = Sweep(r, sb("kp_last", [P, PGRP, 384])[:])
        KP, KT, KC, VCT, Qs, SC, pages = sw.KP, sw.KT, sw.KC, sw.VCT, sw.Qs, sw.SC, sw.pages
        VP = sb("vp", [P, NG + 1, PGRP, P])
        group, own, headrow = sb("group", [R, R]), sb("own", [NS, R]), sb("headrow", [R, 8])
        PC, G24, gates = sb("pc", [R, P]), sb("g24", [R, 8, 3]), sb("gates", [R, 3])
        pick, top8, mask = sb("pick", [R, 72]), sb("top8", [R, 8]), sb("mask", [R, 64])
        top, ntop, den, coef = sb("top", [R, 3]), sb("ntop", [R, 3]), sb("den", [R, 3]), sb("coef", [R, 3])
        pn, diag = sb("pn", [NS, 2, R]), sb("diag", [R, 2, R])
        O = sb("o", [P, R])
        tables_in, k_turned, kt_kept, kt_used, sc_kept = [
            nc.alloc_semaphore("ns_" + s) for s in ("tables_in", "k_turned", "kt_kept", "kt_used", "sc_kept")]
        kp_in = [nc.alloc_semaphore(f"ns_kp_in{u}") for u in range(4)]
        vp_in = [nc.alloc_semaphore(f"ns_vp_in{u}") for u in range(NG + 1)]
        vp_in2 = [nc.alloc_semaphore(f"ns_vp_in2_{u}") for u in range(NG)]
        pe_step, dve_step, act_step, pt_turned, pt_kept, vp_used, o_ready = [
            nc.alloc_semaphore("ns_" + s) for s in
            ("pe_step", "dve_step", "act_step", "pt_turned", "pt_kept", "vp_used", "o_ready")]
        block = ctx.enter_context(nc.Block())

        def fetch(eng, mine, vp_in):
            def page(index):
                return eng.value_load(pages[0:1, bass.ds(index, 1)], min_val=0, max_val=n_pool - 1)

            with eng.Fori(0, NS) as s:
                for g in range(NG):
                    eng.wait_ge(vp_used, s * (NG + 1) + (g + 1))
                    for j in mine:
                        eng.dma_start(VP[:, g, j, :],
                                      cache[bass.ds(page(s * PAGES + (g * PGRP + j)), 1), :, 384:512].squeeze(0)
                                      ).then_inc(vp_in[g], 16)
                if 0 in mine:
                    eng.wait_ge(vp_used, s * (NG + 1) + (NG + 1))
                    eng.dma_start(VP[:, NG, :, :], win[bass.ds(s, 1), :, :, 1, :].squeeze(0)).then_inc(vp_in[NG], 16)

        @block.sync
        def _(sp):
            for s in range(4):
                sp.dma_start(KP[s][:, :, 256:384], win[s, :, :, 0, :]).then_inc(kp_in[s], 16)
            for dst, src in ((group[:], r.c_group), (own[:], r.c_own), (headrow[:], r.c_headrow)):
                sp.dma_start(dst, src).then_inc(tables_in, 16)
            for s in range(4, NS):
                sp.wait_ge(k_turned, s - 3)
                sp.dma_start(KP[s % 4][:, :, 256:384], win[s, :, :, 0, :]).then_inc(kp_in[s % 4], 16)
            fetch(sp, (0, 1), vp_in)

        @block.gpsimd
        def _(pool_):
            fetch(pool_, (2, 3), vp_in2)

        @block.tensor
        def _(pe):
            pe.sem_inc(vp_used, NG + 1)

            def turn(s):
                pe.wait_ge(kp_in[s % 4], (s // 4 + 1) * 16)
                if s >= 2:
                    pe.wait_ge(kt_kept, s - 1)
                for j in range(PGRP):
                    mm = pe.transpose(r.ps[:, s % 2, j * P:(j + 1) * P], KP[s % 4][:, j, 256:384], r.ident[:])
                mm.then_inc(k_turned, 1)

            turn(0)
            for s in range(NS):
                if s + 1 < NS:
                    turn(s + 1)
                pe.wait_ge(kt_kept, s + 1)
                pe.matmul(r.ps[0:R, 2, :], Qs[:, s, :], KT[:, s % 2, :], start=(s == 0),
                          stop=(s == NS - 1)).then_inc(kt_used, 1)
            pe.wait_ge(tables_in, 48)
            for s in range(NS):
                pe.matmul(r.ps[0:R, 3, 0:1], Qs[:, s, :], r.H[:, K_SEL, T + s:T + s + 1], start=(s == 0),
                          stop=(s == NS - 1))
            for s in range(NS):
                pe.matmul(r.ps[0:R, 3, 1:2], Qs[:, s, :], r.H[:, K_WIN, T + s:T + s + 1], start=(s == 0),
                          stop=(s == NS - 1))
            for s in range(NS):
                pe.matmul(r.ps[0:R, 3, P:2 * P], Qs[:, s, :], KC[:, s, :], start=(s == 0), stop=(s == NS - 1))
            pe.matmul(r.ps[0:R, 3, 32:56], own[:], r.tok[0:NS, 8, R_NSA:R_NSA + 24], start=True,
                      stop=True).then_inc(pe_step, 1)
            for s in range(NS):
                mm = pe.transpose(r.ps[:, s // 4, s % 4 * P:(s % 4 + 1) * P], VCT[:, s, :], r.ident[:])
            mm.then_inc(pe_step, 1)
            pe.wait_ge(dve_step, 4)
            pe.matmul(r.ps[0:R, 4, 0:P], group[:], PC[:], start=True, stop=True).then_inc(pe_step, 1)
            pe.wait_ge(dve_step, 15)
            for j in range(2):
                mm = pe.matmul(r.ps[0:NS, 4, 256 + R * j:256 + R * (j + 1)], r.ones[0:R, 0:NS], diag[:, j, :],
                               start=True, stop=True)
            mm.then_inc(pe_step, 1)
            pe.wait_ge(act_step, 3)
            for b in range(5):
                if b >= 2:
                    pe.wait_ge(pt_kept, b - 1)
                for n in range(8 * b, min(8 * b + 8, 37)):
                    src = SC[:, n * P:(n + 1) * P] if n < 32 else SW[:, (n - 32) * P:(n - 31) * P] if n < 36 else PC[:]
                    mm = pe.transpose(r.ps[:, b % 2, n % 8 * R:(n % 8 + 1) * R], src, r.ident[0:R, 0:R])
                mm.then_inc(pt_turned, 1)
            pe.wait_ge(pt_kept, 5)
            for s in range(NS):
                pe.matmul(r.ps[:, 7, s * 8:s * 8 + 8], VC[:, s, :], PT[:, 36, s * 8:s * 8 + 8], start=True, stop=True)
            pe.wait_ge(dve_step, 16)
            pe.matmul(r.ps[:, 5, 0:R], r.srows[0:NS, 384:512], pn[:, 0, :], start=True, stop=False)
            pe.matmul(r.ps[:, 5, 0:R], r.srows[0:NS, 640:768], pn[:, 1, :], start=False, stop=True)
            with pe.Fori(0, NS) as s:
                for g in range(NG + 1):
                    pe.wait_ge(vp_in[g], s * 32 + 32 if g < NG else s * 16 + 16)
                    if g < NG:
                        pe.wait_ge(vp_in2[g], s * 32 + 32)
                    for j in range(PGRP):
                        mm = pe.matmul(r.ps[:, 6, bass.ds(s * 8, 8)], VP[:, g, j, :],
                                       PT[:, 4 * g + j, bass.ds(s * 8, 8)], start=(g == 0 and j == 0),
                                       stop=(g == NG and j == PGRP - 1))
                    mm.then_inc(vp_used, 1)

        @block.scalar
        def _(act):
            for s in range(NS):
                act.wait_ge(k_turned, s + 1)
                if s >= 2:
                    act.wait_ge(kt_used, s - 1)
                act.copy(KT[:, s % 2, :], r.ps[:, s % 2, :]).then_inc(kt_kept, 1)
            act.wait_ge(dve_step, 2)
            act.activation(PC[:], r.ps[0:R, 3, P:2 * P], ACT.Exp, bias=ntop[:, 0:1], scale=0.125,
                           accum_out=den[:, 0:1]).then_inc(act_step, 1)
            act.wait_ge(pe_step, 2)
            act.copy(VC[:, 0:4, :].rearrange("p s n -> p (s n)"), r.ps[:, 0, :])
            act.copy(VC[:, 4:8, :].rearrange("p s n -> p (s n)"), r.ps[:, 1, :]).then_inc(act_step, 1)
            act.wait_ge(dve_step, 12)
            act.activation(SC, SC, ACT.Exp, bias=ntop[:, 1:2], scale=0.125, accum_out=den[:, 1:2])
            act.activation(SW[:], SW[:], ACT.Exp, bias=ntop[:, 2:3], scale=0.125,
                           accum_out=den[:, 2:3]).then_inc(act_step, 1)
            for b in range(5):
                n = min(8, 37 - 8 * b)
                act.wait_ge(pt_turned, b + 1)
                act.copy(PT[:, 8 * b:8 * b + n, :].rearrange("p n q -> p (n q)"),
                         r.ps[:, b % 2, 0:n * R]).then_inc(pt_kept, 1)

        @block.vector
        def _(v):
            v.sem_inc(dve_step, 1)
            v.wait_ge(kt_used, NS)
            v.tensor_copy(SW[:, 0:512], r.ps[0:R, 2, :]).then_inc(sc_kept, 1)
            v.wait_ge(pe_step, 1)
            v.wait_ge(sc_kept, 1)
            v.memset(SW[:, 0:1], NEG)
            v.tensor_copy(SC[:, PAST:PAST + 1], r.ps[0:R, 3, 0:1])
            v.tensor_copy(SW[:, 512:513], r.ps[0:R, 3, 1:2])
            v.tensor_tensor(G24[:], r.ps[0:R, 3, 32:56].rearrange("p (h b) -> p h b", b=3),
                            headrow[:].unsqueeze(2).to_broadcast([R, 8, 3]), ALU.mult)
            v.tensor_reduce(top[:, 0:1], r.ps[0:R, 3, P:2 * P], AX.X, ALU.max).then_inc(sc_kept, 1)
            v.wait_ge(sc_kept, 2)
            v.tensor_reduce(gates[:], G24[:].rearrange("p h b -> p b h"), AX.X, ALU.add)
            v.tensor_reduce(top[:, 2:3], SW[:], AX.X, ALU.max)
            v.tensor_scalar(ntop[:, 0:1], top[:, 0:1], -0.125, None, ALU.mult).then_inc(dve_step, 1)
            v.wait_ge(act_step, 1)
            v.reciprocal(coef[:, 0:1], den[:, 0:1]).then_inc(dve_step, 1)
            v.wait_ge(dve_step, 3)
            v.tensor_scalar(PC[:], PC[:], coef[:, 0:1], None, ALU.mult).then_inc(dve_step, 1)
            v.memset(pick[:], NEG).then_inc(dve_step, 1)
            v.wait_ge(dve_step, 5)
            v.wait_ge(pe_step, 3)
            v.tensor_scalar(PC[:], PC[:], gates[:, 0:1], None, ALU.mult)
            v.tensor_reduce(pick[:, 0:64], r.ps[0:R, 4, 0:P].rearrange("p (b c) -> p b c", c=2), AX.X,
                            ALU.add).then_inc(dve_step, 1)
            v.wait_ge(dve_step, 6)
            v.memset(pick[:, 0:1], 1e9)
            v.memset(pick[:, 63:65], 1e9).then_inc(dve_step, 1)
            v.wait_ge(dve_step, 7)
            for n in range(2):
                v.max(top8[:], pick[:]).then_inc(dve_step, 1)
                v.wait_ge(dve_step, 8 + 2 * n)
                v.match_replace(pick[:], top8[:], pick[:], -3e38).then_inc(dve_step, 1)
                v.wait_ge(dve_step, 9 + 2 * n)
            v.tensor_scalar(mask[:], pick[:, 0:64], -2e38, NEG, ALU.is_gt, ALU.mult).then_inc(sc_kept, 1)
            v.wait_ge(sc_kept, 3)
            sv = SC[:, 0:PAST].rearrange("p (b n) -> p b n", n=64)
            v.tensor_tensor(sv, sv, mask[:].unsqueeze(2).to_broadcast([R, 64, 64]), ALU.add).then_inc(sc_kept, 1)
            v.wait_ge(sc_kept, 4)
            v.tensor_reduce(top[:, 1:2], SC, AX.X, ALU.max).then_inc(sc_kept, 1)
            v.wait_ge(sc_kept, 5)
            v.tensor_scalar(ntop[:, 1:3], top[:, 1:3], -0.125, None, ALU.mult).then_inc(dve_step, 1)
            v.wait_ge(act_step, 3)
            v.reciprocal(coef[:, 1:3], den[:, 1:3]).then_inc(dve_step, 1)
            v.wait_ge(dve_step, 13)
            v.tensor_tensor(coef[:, 1:3], coef[:, 1:3], gates[:, 1:3], ALU.mult).then_inc(dve_step, 1)
            v.wait_ge(dve_step, 14)
            v.tensor_scalar(SC, SC, coef[:, 1:2], None, ALU.mult)
            v.tensor_scalar(SW[:], SW[:], coef[:, 2:3], None, ALU.mult).then_inc(sc_kept, 1)
            v.wait_ge(sc_kept, 6)
            v.tensor_scalar(diag[:, 0, :], r.ident[0:R, 0:R], SC[:, PAST:PAST + 1], None, ALU.mult)
            v.tensor_scalar(diag[:, 1, :], r.ident[0:R, 0:R], SW[:, 512:513], None,
                            ALU.mult).then_inc(dve_step, 1)
            v.wait_ge(pe_step, 4)
            v.tensor_tensor(pn[:], r.ps[0:NS, 4, 256:256 + 2 * R].rearrange("p (j q) -> p j q", j=2),
                            own[:].unsqueeze(1).to_broadcast([NS, 2, R]), ALU.mult).then_inc(dve_step, 1)
            v.wait_ge(vp_used, (NG + 1) * (NS + 1))
            v.tensor_copy(O[:], r.ps[:, 6, 0:R]).then_inc(dve_step, 1)
            v.wait_ge(dve_step, 17)
            v.tensor_tensor(O[:], O[:], r.ps[:, 7, 0:R], ALU.add).then_inc(dve_step, 1)
            v.wait_ge(dve_step, 18)
            v.tensor_tensor(O[:], O[:], r.ps[:, 5, 0:R], ALU.add).then_inc(dve_step, 1)
            v.wait_ge(dve_step, 19)
            for g in range(2):
                v.tensor_copy(r.H[64 * g:64 * g + 64, Q_B:Q_B + 4, T:N],
                              O[64 * g:64 * g + 64, :].rearrange("p (s h) -> p h s", h=8)[:, 4 * g:4 * g + 4, :])



def build(nc, a, outs):
    r = Res()
    (r.o_y_p, r.o_y_s, r.o_rows_p, r.o_win_p, r.o_conv_p, r.o_dS_p, r.o_gS_p, r.o_rows_s, r.o_win_s, r.o_conv_s,
     r.o_dS_s, r.o_gS_s) = outs
    r.x_prompt, r.x_sample = a["x_prompt"], a["x_sample"]
    r.cache, r.state_nsa_win, r.state_delta_conv = a["cache_nsa_kv"], a["state_nsa_win"], a["state_delta_conv"]
    r.state_delta_S, r.state_gla_S, r.page_table = a["state_delta_S"], a["state_gla_S"], a["page_table"]
    r.dt_bias, r.A_log = a["delta_dt_bias"], a["delta_A_log"]
    r.conv_w, r.delta_ng = a["conv_w_delta"], a["delta_norm_g"]
    r.c_causal, r.c_oldest, r.c_cmp_add, r.c_cmp_one = a["c_causal"], a["c_oldest"], a["c_cmp_add"], a["c_cmp_one"]
    r.c_level, r.c_upper, r.c_rowsel = a["c_level"], a["c_upper"], a["c_rowsel"]
    r.c_pick, r.gla_ng, r.b_g2, r.w_g2 = a["c_pick"], a["gla_norm_g"], a["b_gla_gate2"], a["w_gla_gate2"][0]
    r.c_pool, r.c_group, r.c_own, r.c_headrow = a["c_pool"], a["c_group"], a["c_own"], a["c_headrow"]
    r.x_spilled = nc.dram_tensor("x_spilled", [P, KD, N], F32, kind="Internal").ap()
    r.w_ffn_gate, r.w_ffn_up = a["w_ffn_gate"], a["w_ffn_up"]
    with ExitStack() as ctx:
        def sb(name, shape, dt=F32):
            return ctx.enter_context(nc.sbuf_tensor(name, shape, dt))

        r.X, r.Xh = ctx.enter_context(twin(nc, "X", [P, KD, N]))
        r.ps = ctx.enter_context(nc.psum_tensor("ps", [P, 8, 512], F32))
        r.ident = sb("ident", [P, P])
        r.ones, r.ones_d = sb("ones", [P, P]), sb("ones_d", [P, P])
        r.bias = sb("bias", [P, 2])
        r.lng, r.lnb = sb("lng", [P, 4 * KD]), sb("lnb", [P, 4 * KD])
        r.const_loads = [(r.ident[:], a["c_ident"]),
                         (r.lng[:], a["ln_g"]),
                         (r.lnb[:], a["ln_b"])]
        def low(tag):
            return nc.sbuf_tensor("Xl_" + tag, [P, KD, N], F32R)

        def view(w):
            return w.rearrange("(k p) n -> p k n", p=P)

        def whole(w):
            half = w.shape[1] // 2
            return lambda m, u, shift: [
                ((slice(None), slice(s, s + half), slice(None)), w[:, s:s + half, bass.ds(m * P + shift, P)])
                for s in (0, half)]

        w_even = view(a["w_in_even"][0])

        def load_even(m, u, shift):
            if shift is None:
                c0 = 2056 + 64 * (m - 16)
                return [((slice(None), slice(None), slice(64 * g, 64 * g + 64)),
                         w_even[:, :, c0 + 256 * g:c0 + 256 * g + 64]) for g in range(2)]
            return whole(w_even)(m, u, shift)

        even_chunks = [(0, 12, 0), (12, 16, 8), (16, 20, None), (20, 26, 8)]
        every = slice(None)
        even_small = [((every, every, slice(R_BETA, R_BETA + 4)), w_even[:, :, 1536:1540]),
                      ((every, every, slice(R_G, R_G + 4)), w_even[:, :, 1540:1544]),
                      ((every, every, slice(R_NSA, R_NSA + 24)), w_even[:, :, 3336:3360])]
        with ExitStack() as even:
            r.H, r.Hlo = even.enter_context(twin(nc, "H0", [P, 27, N], (GATE_A, GATE_A + 8)))
            with low("in_even") as r.Xl:
                load_phase(nc, r)
                project_split_phase(nc, r, "in_even", even_chunks, load_even, r.H, even_small)
            r.tok = even.enter_context(nc.sbuf_tensor("tok", [P, 9, NSMALL], F32))
            r.bufT = even.enter_context(nc.sbuf_tensor("bufT", [P, 12, 24], F32))
            r.srows = even.enter_context(nc.sbuf_tensor("srows", [NS, 768], F32))
            with nc.sbuf_tensor("rows", [P, TT, 768], F32) as rows:
                r.rows = rows
                even_rows_phase(nc, r)
                gates_phase(nc, r)
                nsa_prompt_phase(nc, r)
            conv_phase(nc, r)
            delta_prompt_phase(nc, r)
            sample_state_phase(nc, r, True)
            nsa_sample_phase(nc, r)
            w_out = view(a["w_out_even"][0])

            def load_out_even(part, m):
                cols = bass.ds(m * P, P)
                tail = a["w_out_even"][0, 512:1024].rearrange("(g i p) n -> g p i n", g=2, p=64)
                return [((every, slice(0, 4), every), w_out[:, 0:4, cols]),
                        ((slice(0, 64), slice(4, 8), every), tail[0][:, :, cols]),
                        ((slice(64, 128), slice(4, 8), every), tail[1][:, :, cols])]

            residual_phase(nc, r, "out_even", r.H[:, GATE_A:GATE_A + 8, :], r.Hlo[:], 1,
                           load_out_even, reload=True)

        def ffn(layer):
            w_down = view(a["w_ffn_down"][layer])

            def load_down(part, m):
                half = KF // 2
                return [((every, every, every), w_down[:, part * half:part * half + half, bass.ds(m * P, P)])]

            with twin(nc, f"F{layer}", [P, KF, N]) as (r.F, r.Flo):
                with low(f"ffn{layer}") as r.Xl:
                    norm_phase(nc, r, layer, 0, True)
                    ffn_up_phase(nc, r, layer)
                residual_phase(nc, r, f"down{layer}", r.F[:], r.Flo[:], 2, load_down)

        ffn(0)
        w_odd = view(a["w_in_odd"][0])
        with twin(nc, "H1", [P, 25, N], (OR_, OR_ + 8)) as (r.H, r.Hlo):
            with low("in_odd") as r.Xl:
                norm_phase(nc, r, 0, 1, True)
                project_split_phase(nc, r, "in_odd", [(0, 16, 0), (16, 24, 16)], whole(w_odd), r.H,
                                    [((every, every, slice(0, 16)), w_odd[:, :, 2048:2064])])
            with nc.sbuf_tensor("LA", [P, 4, N], F32) as r.LA:
                gla_gate_phase(nc, r)
                gla_prompt_phase(nc, r)
                sample_state_phase(nc, r, False)
            residual_phase(nc, r, "out_odd", r.H[:, OR_:OR_ + 8, :], r.Hlo[:], 1,
                           lambda part, m: whole(view(a["w_out_odd"][0]))(m, 0, 0))
        ffn(1)
        norm_phase(nc, r, 1, 1, False)
        store_phase(nc, r)


_INS = ["x_prompt", "x_sample", "cache_nsa_kv", "state_nsa_win", "state_delta_conv", "state_delta_S", "state_gla_S",
        "page_table", "w_in_even", "conv_w_delta", "delta_A_log", "delta_dt_bias", "delta_norm_g", "w_out_even",
        "w_in_odd", "w_gla_gate2", "b_gla_gate2", "gla_norm_g", "w_out_odd", "w_ffn_gate", "w_ffn_up", "w_ffn_down",
        "ln_g", "ln_b"]
_OUTS = [(1, T, D), (NS, 1, D), (1, 1, T, 4, 2, 64), (1, 1, 512, 2, 2, 64), (1, 1, 3, 1536), (1, 1, 4, 128, 128),
         (1, 1, 4, 128, 256), (1, NS, 1, 4, 2, 64), (1, NS, 512, 2, 2, 64), (1, NS, 3, 1536), (1, NS, 4, 128, 128),
         (1, NS, 4, 128, 256)]


def per_partition(v):
    v = np.asarray(v)
    return v.reshape(-1, P).T


def kernel(**inputs):
    import concourse.bacc as bacc
    from concourse.bass_utils import run_bass_kernel_spmd

    nc = bacc.Bacc("TRN2", target_bir_lowering=False, num_devices=1)
    arrays, aps = {}, {}
    for name in ("ln_g", "ln_b", "conv_w_delta", "delta_norm_g", "gla_norm_g", "b_gla_gate2"):
        inputs[name] = per_partition(inputs[name])
    for name in ("delta_A_log", "delta_dt_bias"):
        inputs[name] = np.asarray(inputs[name]).T
    for name, arr in [(n, inputs[n]) for n in _INS] + list(constants().items()):
        arr = np.ascontiguousarray(arr)
        arrays["in_" + name] = arr
        aps[name] = nc.dram_tensor("in_" + name, arr.shape, mybir.dt.from_np(arr.dtype), kind="ExternalInput").ap()
    outs = [nc.dram_tensor(f"out_{i}", shape, F32, kind="ExternalOutput").ap() for i, shape in enumerate(_OUTS)]
    build(nc, aps, outs)
    result = run_bass_kernel_spmd(nc, [arrays], core_ids=[0])
    return tuple(result.results[0][f"out_{i}"] for i in range(len(_OUTS)))
```

```python
import math
from contextlib import ExitStack, contextmanager

import numpy as np

import concourse.bass as bass
from concourse import mybir
from concourse.alu_op_type import AluOpType as ALU

ACT = mybir.ActivationFunctionType
F32 = mybir.dt.float32
I32 = mybir.dt.int32
F32R = mybir.dt.float32r
AX = mybir.AxisListType

P = 128
D = 1024
KD = D // P
T = 1024
TT = T // P
NS = 8
N = T + NS
CW = N // 3
NB = 3
FF = 2816
KF = FF // P
ALPHA = 4.0 ** 0.25
NEG = -1e30
HEADS = 4
GV = 256
PAGES = 32
PGRP = 4
NG = PAGES // PGRP

Q_A, K_A, V_A, GATE_A, Q_B, K_CMP, V_CMP, K_SEL, V_SEL, K_WIN, V_WIN, SMALL = 0, 4, 8, 12, 16, 20, 21, 22, 23, 24, 25, 26
R_BETA, R_G, R_NSA = 0, 32, 64
NSMALL = 96
OQ, OK, OV, OR_, OG1 = 0, 4, 8, 16, 24
LEVELS = 7


def constants():
    i = np.arange(P)
    ident = np.eye(P, dtype=np.float32)
    level = np.zeros((P, LEVELS, P), np.float32)
    for lv in range(LEVELS):
        s = 1 << lv
        row, col = i[None, :], i[:, None]
        level[:, lv] = (row // (2 * s) == col // (2 * s)) & (row // s % 2 == 1) & (col // s % 2 == 0)
    upper = (i[:, None] <= i[None, :]).astype(np.float32)
    causal = np.where(i[None, :] <= i[:, None], 0, NEG).astype(np.float32)
    oldest = np.where(i[None, :] > i[:, None], 0, NEG).astype(np.float32)
    qpos = (np.arange(TT) * P)[None, :, None] + i[:, None, None]
    ok = (np.arange(32)[None, None, :] + 1) * 32 <= qpos + 1
    cmp_add = np.where(ok, 0, NEG).astype(np.float32).reshape(P, -1)
    cmp_one = ok.astype(np.float32).reshape(P, -1)
    pool = np.where(i[:, None] // 32 == np.arange(4)[None, :], 1 / 32, 0).astype(np.float32)
    rowsel = np.zeros((NSMALL, 8, P), np.float32)
    for h in range(HEADS):
        rowsel[R_BETA + h, h] = 1
        rowsel[R_G + h, 4 + h] = 1
    sh = np.arange(64)
    group = ((sh[:, None] // 8 == sh[None, :] // 8) & (sh[:, None] % 8 // 4 == sh[None, :] % 8 // 4)).astype(np.float32)
    own = (np.arange(8)[:, None] == sh[None, :] // 8).astype(np.float32)
    headrow = (np.arange(8)[None, :] == sh[:, None] % 8).astype(np.float32)
    pick = np.repeat(np.eye(8, dtype=np.float32), P, axis=1)
    return {
        "c_ident": ident, "c_level": level.reshape(P, -1), "c_upper": upper, "c_causal": causal, "c_oldest": oldest,
        "c_cmp_add": cmp_add, "c_cmp_one": cmp_one, "c_pool": pool, "c_rowsel": rowsel.reshape(NSMALL, -1),
        "c_group": group, "c_own": own, "c_headrow": headrow, "c_pick": pick,
    }


class Res:
    pass


@contextmanager
def phase(nc):
    with nc.cleanup_on_exit():
        with ExitStack() as ctx:
            yield ctx
    nc.all_engine_barrier()


@contextmanager
def twin(nc, name, shape, part=None):
    offset = -(-nc.sbuf_base // 32) * 32
    rounded = list(shape)
    if part:
        offset += part[0] * N * 4
        rounded[1] = part[1] - part[0]
    with nc.sbuf_tensor(name, shape, F32) as tile:
        yield tile, nc.alloc_sbuf_tensor_at(name + "_rounded", rounded, F32R, offset=offset)


class Ring:

    def __init__(self, nc, stack, name, kn, load):
        self.nc, self.name, self.load = nc, name, load
        self.raw, self.lo = stack.enter_context(twin(nc, name + "_w", [P, 2, kn, P]))
        self.hi = stack.enter_context(nc.sbuf_tensor(name + "_w_hi", [P, 2, kn, P], F32R))

    def semaphores(self):
        self.first_in = [self.nc.alloc_semaphore(self.name + f"_first_in{u}") for u in range(2)]
        self.first_hi = self.nc.alloc_semaphore(self.name + "_first_hi")

    def fetch_first(self, eng):
        for u in range(2):
            for dst, src in self.load(u):
                eng.dma_start(self.raw[:, u][dst], src).then_inc(self.first_in[u], 16)

    def split_first(self, pool):
        for u in range(2):
            pool.wait_ge(self.first_in[u], 16 * len(self.load(u)))
            pool.tensor_copy(self.hi[:, u], self.raw[:, u]).then_inc(self.first_hi, 1)
            pool.wait_ge(self.first_hi, u + 1)
            pool.tensor_tensor(self.lo[:, u], self.raw[:, u], self.hi[:, u].bitcast(F32), ALU.subtract)


def load_phase(nc, r, ring):
    with phase(nc) as ctx:
        stage = ctx.enter_context(nc.sbuf_tensor("x_stage", [P, 3, D], F32))
        const_in = nc.alloc_semaphore("const_in")
        x_in = [nc.alloc_semaphore(f"x_in{u}") for u in range(3)]
        x_turned = nc.alloc_semaphore("x_turned")
        x_rounded = nc.alloc_semaphore("x_rounded")
        x_kept = nc.alloc_semaphore("x_kept")
        ones_set = nc.alloc_semaphore("ones_set")
        ring.semaphores()
        block = ctx.enter_context(nc.Block())
        tiles = [(r.x_prompt[0, t * P:(t + 1) * P, :], P) for t in range(TT)] + [
            (r.x_sample.rearrange("b t d -> (b t) d"), NS)]
        n_const = len(r.const_loads)

        @block.sync
        def _(sp):
            for n, (src, rows) in enumerate(tiles):
                if n >= 3:
                    sp.wait_ge(x_turned, 2 * (n - 2))
                sp.dma_start(stage[0:rows, n % 3, :], src).then_inc(x_in[n % 3], 16)
                if n == 2:
                    ring.fetch_first(sp)

        @block.gpsimd
        def _(pool):
            ring.split_first(pool)

        @block.scalar
        def _(act):
            for dst, src in r.const_loads:
                act.dma_start(dst, src).then_inc(const_in, 16)
            act.wait_ge(const_in, 16 * n_const)
            for n, (_, rows) in enumerate(tiles):
                act.wait_ge(x_turned, 2 * n + 2)
                for half in range(2):
                    act.copy(r.Xh[:, 4 * half:4 * half + 4, n * P:n * P + rows],
                             r.ps[:, n % 2 * 2 + half, :].rearrange("p (k t) -> p k t", k=4)[:, :, 0:rows]
                             ).then_inc(x_rounded, 1)

        @block.vector
        def _(v):
            v.memset(r.ones_d[:], 1.0 / D)
            v.memset(r.ones[:], 1.0)
            v.memset(r.bias[:, 0:1], 1e-5)
            v.memset(r.bias[:, 1:2], 1e-6).then_inc(ones_set, 1)
            for n, (_, rows) in enumerate(tiles):
                for half in range(2):
                    v.wait_ge(x_rounded, 2 * n + 1 + half)
                    v.tensor_tensor(r.Xl[:, 4 * half:4 * half + 4, n * P:n * P + rows],
                                    r.ps[:, n % 2 * 2 + half, :].rearrange("p (k t) -> p k t", k=4)[:, :, 0:rows],
                                    r.Xh[:, 4 * half:4 * half + 4, n * P:n * P + rows].bitcast(F32),
                                    ALU.subtract).then_inc(x_kept, 1)

        @block.tensor
        def _(pe):
            pe.wait_ge(const_in, 16 * n_const)
            for n, (_, rows) in enumerate(tiles):
                pe.wait_ge(x_in[n % 3], 16 * (n // 3 + 1))
                if n >= 2:
                    pe.wait_ge(x_kept, 2 * (n - 1))
                for half in range(2):
                    for k in range(4):
                        mm = pe.transpose(r.ps[:, n % 2 * 2 + half, k * P:k * P + rows],
                                          stage[0:rows, n % 3, (4 * half + k) * P:(4 * half + k + 1) * P],
                                          r.ident[0:rows, 0:rows])
                    mm.then_inc(x_turned, 1)


def residual_phase(nc, r, name, moving, moving_lo, parts, load, reload=False):
    kn = moving.shape[1] // parts
    flat = r.X[:].rearrange("p k n -> p (k n)")
    with phase(nc) as ctx:
        raw, lo = ctx.enter_context(twin(nc, name + "_w", [P, 2, kn, P]))
        hi = ctx.enter_context(nc.sbuf_tensor(name + "_w_hi", [P, 2, kn, P], F32R))
        moving_hi = ctx.enter_context(nc.sbuf_tensor(name + "_m_hi", [P, kn, N], F32R))
        w_in = [nc.alloc_semaphore(name + f"_w_in{u}") for u in range(2)]
        w_split, m_rounded, m_split, product, bank_free, x_in = [nc.alloc_semaphore(name + s) for s in (
            "_w_split", "_m_rounded", "_m_split", "_product", "_bank_free", "_x_in")]
        block = ctx.enter_context(nc.Block())
        per = len(load(0, 0))
        all_banks = NB * KD

        @block.sync
        def _(sp):
            for u in range(2):
                for dst, src in load(0, u):
                    sp.dma_start(raw[:, u][dst], src).then_inc(w_in[u], 16)
            if reload:
                sp.dma_start(r.X[:], r.x_spilled).then_inc(x_in, 16)
            for part in range(parts):
                with sp.Fori(0 if part else 1, KD // 2) as i:
                    for u in range(2):
                        sp.wait_ge(product, i * 6 + (part * all_banks + 3 * u - 3))
                        for dst, src in load(part, i * 2 + u):
                            sp.dma_start(raw[:, u][dst], src).then_inc(w_in[u], 16)

        @block.gpsimd
        def _(pool):
            split_weights(pool, r, w_in, w_split, raw, hi, lo, KD * parts, per)

        @block.tensor
        def _(pe):
            def three(part, u, c, k):
                dst, cols = r.ps[:, 3 * u + c, 0:CW], slice(c * CW, (c + 1) * CW)
                pe.matmul(dst, hi[:, u, k, :], moving_hi[:, k, cols], start=(k == 0), stop=False)
                pe.matmul(dst, hi[:, u, k, :], moving_lo[:, part * kn + k, cols], start=False, stop=False)
                return pe.matmul(dst, lo[:, u, k, :], moving_hi[:, k, cols], start=False, stop=(k == kn - 1))

            def chunk(part, u, split, free):
                pe.wait_ge(w_split, split)
                for c in range(NB):
                    pe.wait_ge(bank_free, free + (c + 1))
                    for k in range(kn):
                        mm = three(part, u, c, k)
                    mm.then_inc(product, 1)

            for part in range(parts):
                pe.wait_ge(w_split, 2 * KD * part + 2)
                pe.wait_ge(bank_free, all_banks * part + 3)
                for k in range(kn):
                    pe.wait_ge(m_split, kn * part + k + 1)
                    for c in range(NB):
                        mm = three(part, 0, c, k)
                        if k == kn - 1:
                            mm.then_inc(product, 1)
                chunk(part, 1, 2 * KD * part + 4, all_banks * part + 3)
                with pe.Fori(1, KD // 2) as i:
                    for u in range(2):
                        chunk(part, u, i * 4 + (2 * KD * part + 2 * u + 2), i * 6 + (all_banks * part + 3 * u))

        @block.scalar
        def _(act):
            for part in range(parts):
                if part:
                    act.wait_ge(product, all_banks * part)
                for k in range(kn):
                    act.copy(moving_hi[:, k, :], moving[:, part * kn + k, :]).then_inc(m_rounded, 1)

        @block.vector
        def _(v):
            v.sem_inc(bank_free, 6)
            for part in range(parts):
                for k in range(kn):
                    v.wait_ge(m_rounded, part * kn + k + 1)
                    v.tensor_tensor(moving_lo[:, part * kn + k, :], moving[:, part * kn + k, :],
                                    moving_hi[:, k, :].bitcast(F32), ALU.subtract).then_inc(m_split, 1)
                if reload:
                    v.wait_ge(x_in, 16)
                with v.Fori(0, KD // 2) as i:
                    for u in range(2):
                        for c in range(NB):
                            v.wait_ge(product, i * 6 + (all_banks * part + 3 * u + c + 1))
                            dst = flat[:, bass.ds(i * (2 * N) + (u * N + c * CW), CW)]
                            v.scalar_tensor_tensor(out=dst, in0=dst, scalar=1.0 if part else ALPHA,
                                                   in1=r.ps[:, 3 * u + c, 0:CW], op0=ALU.mult,
                                                   op1=ALU.add).then_inc(bank_free, 1)


def split_weights(pool, r, w_in, w_split, raw, hi, lo, steps, per, first=0):
    if first:
        pool.sem_inc(w_split, 4)
    ones = r.ones[:].unsqueeze(1).to_broadcast([P, raw.shape[2], P])
    with pool.Fori(first, steps // 2) as i:
        for u in range(2):
            pool.wait_ge(w_in[u], i * (16 * per) + 16 * per * (1 - first))
            pool.tensor_tensor(hi[:, u], raw[:, u], ones, ALU.mult).then_inc(w_split, 1)
            pool.wait_ge(w_split, i * 4 + (2 * u + 1))
            pool.tensor_tensor(lo[:, u], raw[:, u], hi[:, u].bitcast(F32), ALU.subtract).then_inc(w_split, 1)


def project_split_phase(nc, r, name, chunks, load, out, small, ring):
    total = chunks[-1][1]
    flat = out[:].rearrange("p k n -> p (k n)")
    with phase(nc) as ctx:
        raw, hi, lo = ring.raw, ring.hi, ring.lo
        w_in = [nc.alloc_semaphore(name + f"_w_in{u}") for u in range(2)]
        w_split, w_clear, w_small, product, bank_free = [nc.alloc_semaphore(name + s) for s in (
            "_w_split", "_w_clear", "_w_small", "_product", "_bank_free")]
        block = ctx.enter_context(nc.Block())
        per = len(load(0, 0, 0))

        @block.sync
        def _(sp):
            for a, b, shift in chunks:
                a = max(a, 2)
                if shift is not None:
                    with sp.Fori(a // 2, b // 2) as i:
                        for u in range(2):
                            sp.wait_ge(product, i * 6 + (3 * u - 3))
                            for dst, src in load(i * 2 + u, u, shift):
                                sp.dma_start(raw[:, u][dst], src).then_inc(w_in[u], 16)
                else:
                    for m in range(a, b):
                        sp.wait_ge(product, 3 * m - 3)
                        for dst, src in load(m, m % 2, shift):
                            sp.dma_start(raw[:, m % 2][dst], src).then_inc(w_in[m % 2], 16)
            sp.wait_ge(w_clear, 1)
            for dst, src in small:
                sp.dma_start(raw[:, 0][dst], src).then_inc(w_small, 16)

        @block.gpsimd
        def _(pool):
            split_weights(pool, r, w_in, w_split, raw, hi, lo, total, per, first=1)
            pool.wait_ge(product, 3 * total - 3)
            pool.memset(raw[:, 0, :, :], 0.0).then_inc(w_clear, 1)
            pool.wait_ge(w_small, 16 * len(small))
            pool.tensor_copy(hi[:, 0], raw[:, 0]).then_inc(w_split, 1)
            pool.wait_ge(w_split, 2 * total + 1)
            pool.tensor_tensor(lo[:, 0], raw[:, 0], hi[:, 0].bitcast(F32), ALU.subtract).then_inc(w_split, 1)

        @block.tensor
        def _(pe):
            def products(u, rows, c):
                for k in range(KD):
                    cols = slice(c * CW, (c + 1) * CW)
                    dst = r.ps[0:rows, 3 * u + c, 0:CW]
                    pe.matmul(dst, hi[:, u, k, 0:rows], r.Xh[:, k, cols], start=(k == 0), stop=False)
                    pe.matmul(dst, hi[:, u, k, 0:rows], r.Xl[:, k, cols], start=False, stop=False)
                    mm = pe.matmul(dst, lo[:, u, k, 0:rows], r.Xh[:, k, cols], start=False, stop=(k == KD - 1))
                mm.then_inc(product, 1)

            with pe.Fori(0, total // 2) as i:
                for u in range(2):
                    pe.wait_ge(w_split, i * 4 + (2 * u + 2))
                    for c in range(NB):
                        pe.wait_ge(bank_free, i * 6 + (3 * u + c + 1))
                        products(u, P, c)
            pe.wait_ge(w_split, 2 * total + 2)
            for c in range(NB):
                pe.wait_ge(bank_free, 3 * total + c + 1)
                products(0, NSMALL, c)

        @block.vector
        def _(v):
            v.sem_inc(bank_free, 6)
            with v.Fori(0, total // 2) as i:
                for u in range(2):
                    for c in range(NB):
                        v.wait_ge(product, i * 6 + (3 * u + c + 1))
                        v.tensor_scalar(flat[:, bass.ds(i * (2 * N) + (u * N + c * CW), CW)],
                                        r.ps[:, 3 * u + c, 0:CW], 1.0, None, ALU.mult).then_inc(bank_free, 1)
            for c in range(NB):
                v.wait_ge(product, 3 * total + c + 1)
                v.tensor_copy(out[0:NSMALL, total, c * CW:(c + 1) * CW],
                              r.ps[0:NSMALL, c, 0:CW]).then_inc(bank_free, 1)
            v.tensor_tensor(r.X[:], r.Xh[:].bitcast(F32), r.Xl[:].bitcast(F32), ALU.add)


def norm_phase(nc, r, layer, which, scratch, ring=None):
    ln = layer * 2 + which
    split = ring is not None
    square = scratch.rearrange("p k n -> p (k n)")[:, 0:2 * KD * CW].rearrange("p (u k n) -> p u k n", u=2, k=KD)
    with phase(nc) as ctx:
        rstd = ctx.enter_context(nc.sbuf_tensor(f"ln{ln}_rstd", [P, NB, CW], F32))
        mean_ready, centred, squared, var_ready, rstd_ready, scaled, logged, whole, rounded, low_ready = [
            nc.alloc_semaphore(f"ln{ln}_" + s) for s in
            ("mean_ready", "centred", "squared", "var_ready", "rstd_ready", "scaled", "logged", "whole", "rounded",
             "low_ready")]
        if split:
            ring.semaphores()
        block = ctx.enter_context(nc.Block())

        if split:
            @block.sync
            def _(sp):
                ring.fetch_first(sp)

            @block.gpsimd
            def _(pool):
                ring.split_first(pool)

        def cols(c):
            return slice(c * CW, (c + 1) * CW)

        @block.vector
        def _(v):
            def centre(c):
                v.wait_ge(mean_ready, c + 1)
                v.tensor_tensor(r.X[:, :, cols(c)], r.X[:, :, cols(c)],
                                r.ps[:, c, 0:CW].unsqueeze(1).to_broadcast([P, KD, CW]),
                                ALU.subtract).then_inc(centred, 1)

            def scale(c):
                v.wait_ge(rstd_ready, c + 1)
                v.tensor_tensor(r.X[:, :, cols(c)], r.X[:, :, cols(c)],
                                rstd[:, c, :].unsqueeze(1).to_broadcast([P, KD, CW]), ALU.mult).then_inc(scaled, 1)

            def low(c):
                if split:
                    v.wait_ge(rounded, c + 1)
                    v.tensor_tensor(r.Xl[:, :, cols(c)], square[:, c % 2], r.Xh[:, :, cols(c)].bitcast(F32),
                                    ALU.subtract).then_inc(low_ready, 1)

            centre(0)
            centre(1)
            scale(0)
            centre(2)
            scale(1)
            low(0)
            scale(2)
            low(1)
            low(2)

        @block.tensor
        def _(pe):
            def mean(c):
                for k in range(KD):
                    mm = pe.matmul(r.ps[:, c, 0:CW], r.ones_d[:], r.X[:, k, cols(c)], start=(k == 0),
                                   stop=(k == KD - 1))
                mm.then_inc(mean_ready, 1)

            def variance(c):
                pe.wait_ge(squared, c + 1)
                for k in range(KD):
                    mm = pe.matmul(r.ps[:, 3 + c, 0:CW], r.ones_d[:], square[:, c % 2, k, :], start=(k == 0),
                                   stop=(k == KD - 1))
                mm.then_inc(var_ready, 1)

            mean(0)
            mean(1)
            variance(0)
            mean(2)
            variance(1)
            variance(2)

        @block.scalar
        def _(act):
            act.preload_act_table_set("natural_log_exp_and_others")

            def squares(c):
                act.wait_ge(centred, c + 1)
                if c >= 2:
                    act.wait_ge(var_ready, c - 1)
                    if split:
                        act.wait_ge(low_ready, c - 1)
                act.activation(square[:, c % 2], r.X[:, :, cols(c)], ACT.Square).then_inc(squared, 1)

            def inverse_root(c):
                act.wait_ge(var_ready, c + 1)
                act.activation(rstd[:, c, :], r.ps[:, 3 + c, 0:CW], ACT.Ln, bias=r.bias[:, 0:1]).then_inc(logged, 1)
                act.wait_ge(logged, c + 1)
                act.activation(rstd[:, c, :], rstd[:, c, :], ACT.Exp, scale=-0.5).then_inc(rstd_ready, 1)

            def finish(c):
                act.wait_ge(scaled, c + 1)
                for k in range(KD):
                    dst = square[:, c % 2, k, :] if split else r.X[:, k, cols(c)]
                    mm = act.activation(dst, r.X[:, k, cols(c)], ACT.Identity,
                                        bias=r.lnb[:, ln * KD + k:ln * KD + k + 1],
                                        scale=r.lng[:, ln * KD + k:ln * KD + k + 1])
                if split:
                    mm.then_inc(whole, 1)
                    act.wait_ge(whole, c + 1)
                    act.copy(r.Xh[:, :, cols(c)], square[:, c % 2]).then_inc(rounded, 1)

            squares(0)
            squares(1)
            inverse_root(0)
            finish(0)
            inverse_root(1)
            squares(2)
            finish(1)
            inverse_root(2)
            finish(2)


def up_weights(r, layer):
    wg = r.w_ffn_gate[layer].rearrange("(k p) n -> p k n", p=P)
    wu = r.w_ffn_up[layer].rearrange("(k p) n -> p k n", p=P)
    return lambda m: [((slice(None), slice(part * KD, part * KD + KD), slice(None)), w[:, :, bass.ds(m * P, P)])
                      for part, w in ((0, wg), (1, wu))]


def ffn_up_phase(nc, r, layer, ring):
    flat = r.F[:].rearrange("p k n -> p (k n)")
    load = up_weights(r, layer)
    raw, hi, lo = ring.raw, ring.hi, ring.lo
    with phase(nc) as ctx:
        w_split = nc.alloc_semaphore(f"up{layer}_w_split")
        lit = ctx.enter_context(nc.sbuf_tensor(f"up{layer}_silu", [P, 2, CW], F32))
        w_in = [nc.alloc_semaphore(f"up{layer}_w_in{u}") for u in range(2)]
        gated, upped, silu_ready, hidden = [nc.alloc_semaphore(f"up{layer}_" + s) for s in
                                            ("gated", "upped", "silu_ready", "hidden")]
        block = ctx.enter_context(nc.Block())

        @block.sync
        def _(sp):
            with sp.Fori(1, KF // 2) as i:
                for u in range(2):
                    sp.wait_ge(upped, i * 6 + (3 * u - 3))
                    for dst, src in load(i * 2 + u):
                        sp.dma_start(raw[:, u][dst], src).then_inc(w_in[u], 16)

        @block.gpsimd
        def _(pool):
            split_weights(pool, r, w_in, w_split, raw, hi, lo, KF, 2, first=1)

        @block.tensor
        def _(pe):
            with pe.Fori(0, KF // 2) as i:
                for u in range(2):
                    pe.wait_ge(w_split, i * 4 + (2 * u + 2))
                    for c in range(NB):
                        pe.wait_ge(hidden, i * 6 + (3 * u + c + 1))
                        pair = (3 * u + c) % 3
                        for part, done in ((0, gated), (1, upped)):
                            dst = r.ps[:, 2 * pair + part, 0:CW]
                            for k in range(KD):
                                xh, xl = r.Xh[:, k, c * CW:(c + 1) * CW], r.Xl[:, k, c * CW:(c + 1) * CW]
                                pe.matmul(dst, hi[:, u, part * KD + k, :], xh, start=(k == 0), stop=False)
                                pe.matmul(dst, hi[:, u, part * KD + k, :], xl, start=False, stop=False)
                                mm = pe.matmul(dst, lo[:, u, part * KD + k, :], xh, start=False, stop=(k == KD - 1))
                            mm.then_inc(done, 1)

        @block.scalar
        def _(act):
            with act.Fori(0, KF // 2) as i:
                for g in range(6):
                    act.wait_ge(hidden, i * 6 + (g + 2))
                    act.wait_ge(gated, i * 6 + (g + 1))
                    act.activation(lit[:, g % 2, :], r.ps[:, 2 * (g % 3), 0:CW], ACT.Silu).then_inc(silu_ready, 1)

        @block.vector
        def _(v):
            v.sem_inc(hidden, 3)
            with v.Fori(0, KF // 2) as i:
                for g in range(6):
                    v.wait_ge(silu_ready, i * 6 + (g + 1))
                    v.wait_ge(upped, i * 6 + (g + 1))
                    v.tensor_tensor(flat[:, bass.ds(i * (2 * N) + (g // 3 * N + g % 3 * CW), CW)],
                                    lit[:, g % 2, :], r.ps[:, 2 * (g % 3) + 1, 0:CW], ALU.mult).then_inc(hidden, 1)
            v.tensor_tensor(r.X[:], r.Xh[:].bitcast(F32), r.Xl[:].bitcast(F32), ALU.add)


def even_rows_phase(nc, r):
    with phase(nc) as ctx:
        buf = ctx.enter_context(nc.sbuf_tensor("conv_buf", [24, 12 * P], F32))
        tail = ctx.enter_context(nc.sbuf_tensor("conv_tail", [11, 12 * P], F32))
        buf_in, turned, kept_a, kept_v, stored = [nc.alloc_semaphore("rows_" + s) for s in
                                                  ("buf_in", "turned", "kept_a", "kept_v", "stored")]
        block = ctx.enter_context(nc.Block())
        units = []
        for t in range(TT):
            units.append(([r.H[:, K_CMP + j, t * P:(t + 1) * P] for j in range(6)], P, P, r.rows[:, t, :]))
        units.append(([r.H[:, K_CMP + j, T:N] for j in range(6)], NS, P, r.srows[:, :]))
        for g in range(2):
            units.append(([r.H[:, 6 * g + j, T - 3:N] for j in range(6)], 11, P, tail[:, g * 6 * P:(g + 1) * 6 * P]))
        for g in range(2):
            units.append(([buf[:, (6 * g + j) * P:(6 * g + j + 1) * P] for j in range(6)], P, 24,
                          r.bufT[:, 6 * g:6 * g + 6, :].rearrange("p k n -> p (k n)")))

        @block.sync
        def _(sp):
            conv = r.state_delta_conv[0]
            n = 0
            sp.dma_start(buf[:], conv.rearrange("b j c -> (b j) c")).then_inc(buf_in, 16)
            sp.dma_start(r.o_conv_s[0][:, 0:2, :], conv[:, 1:3, :]).then_inc(stored, 16)
            sp.dma_start(r.o_win_s[0].rearrange("b w c g d -> b w (c g d)")[:, 0:511, :],
                         r.state_nsa_win[0].rearrange("b w c g d -> b w (c g d)")[:, 1:512, :]).then_inc(stored, 16)
            n += 2
            for t in range(TT):
                sp.wait_ge(kept_a, t + 1)
                sp.wait_ge(kept_v, t + 1)
                sp.dma_start(r.o_rows_p[0, 0, t * P:(t + 1) * P].rearrange("t c g d -> t (c g d)"),
                             r.rows[:, t, 0:512]).then_inc(stored, 16)
                n += 1
                if t >= 4:
                    sp.dma_start(r.o_win_p[0, 0, (t - 4) * P:(t - 3) * P].rearrange("t c g d -> t (c g d)"),
                                 r.rows[:, t, 512:768]).then_inc(stored, 16)
                    n += 1
            sp.wait_ge(kept_a, 9)
            sp.wait_ge(kept_v, 9)
            sp.dma_start(r.o_rows_s[0, :, 0].rearrange("b c g d -> b (c g d)"), r.srows[:, 0:512]).then_inc(stored, 16)
            sp.dma_start(r.o_win_s[0, :, 511].rearrange("b c g d -> b (c g d)"),
                         r.srows[:, 512:768]).then_inc(stored, 16)
            sp.wait_ge(kept_a, 11)
            sp.wait_ge(kept_v, 11)
            sp.dma_start(r.o_conv_p[0, 0], tail[0:3, :]).then_inc(stored, 16)
            sp.dma_start(r.o_conv_s[0, :, 2], tail[3:11, :]).then_inc(stored, 16)
            n += 4
            sp.wait_ge(stored, 16 * n)

        @block.tensor
        def _(pe):
            for n, (srcs, rows, cols, _) in enumerate(units):
                b = n % 3 * 2
                if n >= 3:
                    pe.wait_ge(kept_a, n - 2)
                    pe.wait_ge(kept_v, n - 2)
                if n == 11:
                    pe.wait_ge(buf_in, 16)
                for j in range(6):
                    k = 24 if n >= 11 else P
                    mm = pe.transpose(r.ps[0:rows, b + j // 4, j % 4 * cols:j % 4 * cols + cols], srcs[j],
                                      r.ident[0:k, 0:k])
                    if j in (3, 5):
                        mm.then_inc(turned, 1)

        @block.scalar
        def _(act):
            for n, (_, rows, cols, dst) in enumerate(units):
                act.wait_ge(turned, 2 * n + 1)
                act.copy(dst[0:rows, 0:4 * cols], r.ps[0:rows, n % 3 * 2, 0:4 * cols]).then_inc(kept_a, 1)

        @block.vector
        def _(v):
            for n, (_, rows, cols, dst) in enumerate(units):
                v.wait_ge(turned, 2 * n + 2)
                v.tensor_copy(dst[0:rows, 4 * cols:6 * cols], r.ps[0:rows, n % 3 * 2 + 1, 0:2 * cols]).then_inc(kept_v, 1)


def gates_phase(nc, r):
    S = r.H[:, SMALL, :]
    B, G, C = slice(R_BETA, R_BETA + 4), slice(R_G, R_G + 4), slice(R_NSA, R_NSA + 24)
    with phase(nc) as ctx:
        par = ctx.enter_context(nc.sbuf_tensor("g_par", [P, 4], F32))
        z = ctx.enter_context(nc.sbuf_tensor("g_z", [P, N], F32))
        az = ctx.enter_context(nc.sbuf_tensor("g_az", [P, N], F32))
        keep = ctx.enter_context(nc.sbuf_tensor("g_keep", [P, T], F32))
        par_in, a, v_, turned, kept = [nc.alloc_semaphore("g_" + s) for s in
                                       ("par_in", "act_step", "dve_step", "turned", "kept")]
        block = ctx.enter_context(nc.Block())

        @block.sync
        def _(sp):
            sp.dma_start(par[G, 0:1], r.dt_bias).then_inc(par_in, 16)
            sp.dma_start(par[G, 1:2], r.A_log).then_inc(par_in, 16)

        @block.vector
        def _(v):
            v.memset(keep[:], 1.0).then_inc(v_, 1)
            v.wait_ge(v_, 1)
            v.memset(keep[:].rearrange("p (c t) -> p c t", t=P)[:, :, 0:1], 0.0)
            v.wait_ge(par_in, 32)
            v.tensor_scalar(z[G, :], S[G, :], par[G, 0:1], None, ALU.add).then_inc(v_, 1)
            v.wait_ge(v_, 2)
            v.scalar_tensor_tensor(out=az[G, :], in0=z[G, :], scalar=-1.0, in1=z[G, :], op0=ALU.mult,
                                   op1=ALU.max).then_inc(v_, 1)
            v.wait_ge(a, 2)
            v.tensor_scalar(z[B, :], z[B, :], 1.0, None, ALU.add)
            v.tensor_scalar(z[C, :], z[C, :], 1.0, None, ALU.add).then_inc(v_, 1)
            v.wait_ge(v_, 4)
            v.reciprocal(S[B, :], z[B, :])
            v.reciprocal(S[C, :], z[C, :])
            v.wait_ge(a, 5)
            v.scalar_tensor_tensor(out=z[G, :], in0=z[G, :], scalar=0.0, in1=az[G, :], op0=ALU.max,
                                   op1=ALU.add).then_inc(v_, 1)
            v.wait_ge(v_, 5)
            v.tensor_scalar(z[G, :], z[G, :], par[G, 2:3], -1.0, ALU.mult, ALU.mult).then_inc(v_, 1)
            v.wait_ge(v_, 6)
            v.tensor_tensor_scan(S[G, 0:T], keep[G, :], z[G, 0:T], 0.0, ALU.mult, ALU.add)
            v.tensor_copy(S[G, T:N], z[G, T:N]).then_inc(v_, 1)
            for n in range(9):
                rows = P if n < 8 else NS
                v.wait_ge(turned, n + 1)
                v.tensor_copy(r.tok[0:rows, n, :], r.ps[0:rows, n % 8, 0:NSMALL]).then_inc(kept, 1)

        @block.scalar
        def _(act):
            act.preload_act_table_set("natural_log_exp_and_others")
            act.activation(z[B, :], S[B, :], ACT.Exp, scale=-1.0).then_inc(a, 1)
            act.activation(z[C, :], S[C, :], ACT.Exp, scale=-1.0).then_inc(a, 1)
            act.wait_ge(par_in, 32)
            act.activation(par[G, 2:3], par[G, 1:2], ACT.Exp).then_inc(a, 1)
            act.wait_ge(v_, 3)
            act.activation(az[G, :], az[G, :], ACT.Exp, scale=-1.0).then_inc(a, 1)
            act.wait_ge(a, 4)
            act.activation(az[G, :], az[G, :], ACT.Ln, bias=1.0).then_inc(a, 1)

        @block.tensor
        def _(pe):
            pe.wait_ge(v_, 7)
            for n in range(9):
                rows = P if n < 8 else NS
                if n == 8:
                    pe.wait_ge(kept, 1)
                pe.transpose(r.ps[0:rows, n % 8, 0:NSMALL], S[0:NSMALL, n * P:n * P + rows],
                             r.ident[0:NSMALL, 0:NSMALL]).then_inc(turned, 1)


def store_phase(nc, r):
    with phase(nc) as ctx:
        stage = ctx.enter_context(nc.sbuf_tensor("y_stage", [P, 2, D], F32))
        turned, kept_a, kept_v = [nc.alloc_semaphore("y_" + s) for s in ("turned", "kept_a", "kept_v")]
        stored = [nc.alloc_semaphore(f"y_stored{u}") for u in range(2)]
        block = ctx.enter_context(nc.Block())
        tiles = [(r.o_y_p[0, t * P:(t + 1) * P, :], P) for t in range(TT)] + [
            (r.o_y_s.rearrange("b t d -> (b t) d"), NS)]

        @block.sync
        def _(sp):
            for n, (dst, rows) in enumerate(tiles):
                sp.wait_ge(kept_a, n + 1)
                sp.wait_ge(kept_v, n + 1)
                sp.dma_start(dst, stage[0:rows, n % 2, :]).then_inc(stored[n % 2], 16)
            sp.wait_ge(stored[0], 16 * 5)
            sp.wait_ge(stored[1], 16 * 4)

        @block.tensor
        def _(pe):
            for n, (_, rows) in enumerate(tiles):
                if n >= 2:
                    pe.wait_ge(kept_a, n - 1)
                    pe.wait_ge(kept_v, n - 1)
                for half in range(2):
                    for k in range(4):
                        mm = pe.transpose(r.ps[0:rows, n % 2 * 2 + half, k * P:(k + 1) * P],
                                          r.X[:, 4 * half + k, n * P:n * P + rows], r.ident[:])
                    mm.then_inc(turned, 1)

        @block.scalar
        def _(act):
            for n, (_, rows) in enumerate(tiles):
                act.wait_ge(turned, 2 * n + 1)
                if n >= 2:
                    act.wait_ge(stored[n % 2], 16 * (n // 2))
                act.copy(stage[0:rows, n % 2, 0:512], r.ps[0:rows, n % 2 * 2, :]).then_inc(kept_a, 1)

        @block.vector
        def _(v):
            for n, (_, rows) in enumerate(tiles):
                v.wait_ge(turned, 2 * n + 2)
                if n >= 2:
                    v.wait_ge(stored[n % 2], 16 * (n // 2))
                v.tensor_copy(stage[0:rows, n % 2, 512:1024], r.ps[0:rows, n % 2 * 2 + 1, :]).then_inc(kept_v, 1)

def nsa_prompt_phase(nc, r):
    flat = r.H[:].rearrange("p k n -> p (k n)")
    UNITS = [(t, g) for t in range(TT) for g in range(2)]
    NU = len(UNITS)

    def blocks(t):
        lo = max(0, t - 4)
        return [("cmp", 0)] + [("sel", b) for b in range(t + 1)] + [("win", b) for b in range(lo, t + 1)]

    def groups(t):
        bl = blocks(t)
        return [bl[0:1]] + [bl[s:s + 4] for s in range(1, len(bl), 4)]

    first = [0]
    for t, g in UNITS:
        first.append(first[-1] + len(groups(t)))
    GT = first[-1]
    with phase(nc) as ctx:
        def sb(name, shape):
            return ctx.enter_context(nc.sbuf_tensor("np_" + name, shape, F32))

        causal, oldest = sb("causal", [P, P]), sb("oldest", [P, P])
        cmp_add, cmp_one = sb("cmp_add", [P, TT, 32]), sb("cmp_one", [P, TT, 32])
        kcb, vcbT, vcb = sb("kcb", [P, 32]), sb("vcbT", [P, 32]), sb("vcb", [32, P])
        QS = sb("q", [P, 2, P])
        gates = sb("gates", [P, 2, 2, 3])
        Psel, Pwin, Pcmp = sb("psel", [P, 2, T]), sb("pwin", [P, 2, 640]), sb("pcmp", [P, 2, 32])
        PT = sb("pt", [P, 14, P])
        top, ntop, den, coef = sb("top", [P, 2, 3]), sb("ntop", [P, 2, 3]), sb("den", [P, 2, 3]), sb("coef", [P, 2, 3])
        (tables_in, means_ready, vcb_turned, vcb_kept, q_ready, scored, masked, topped, negated, exped, inverted,
         weighed, scaled, turned, kept, o_ready, o_kept, spilled) = [
            nc.alloc_semaphore("np_" + s) for s in
            ("tables_in", "means_ready", "vcb_turned", "vcb_kept", "q_ready", "scored", "masked", "topped", "negated",
             "exped", "inverted", "weighed", "scaled", "turned", "kept", "o_ready", "o_kept",
             "spilled")]
        cw, acc, tap = sb("conv_w", [P, 48]), sb("conv_acc", [P, N]), sb("conv_tap", [P, N])
        conv_w_in, conv_step = nc.alloc_semaphore("np_conv_w_in"), nc.alloc_semaphore("np_conv_step")
        block = ctx.enter_context(nc.Block())
        s_sel = r.ps[:, 0:2, :].rearrange("p b n -> p (b n)")
        s_win = r.ps[:, 2:4, :].rearrange("p b n -> p (b n)")
        gate_view = r.tok[:, :, R_NSA:R_NSA + 24].rearrange("p t (g h b) -> p t g h b", g=2, h=4)

        @block.sync
        def _(sp):
            for dst, src in ((causal[:], r.c_causal), (oldest[:], r.c_oldest),
                             (cmp_add[:].rearrange("p t c -> p (t c)"), r.c_cmp_add),
                             (cmp_one[:].rearrange("p t c -> p (t c)"), r.c_cmp_one)):
                sp.dma_start(dst, src).then_inc(tables_in, 16)
            sp.dma_start(cw[:], r.conv_w).then_inc(conv_w_in, 16)
            sp.dma_start(r.x_spilled, r.X[:]).then_inc(spilled, 16)
            sp.wait_ge(spilled, 16)

        @block.gpsimd
        def _(pool):
            buf = r.bufT[:].rearrange("p k (s j) -> p k s j", j=3)
            pool.wait_ge(conv_w_in, 16)
            for m in range(12):
                if m:
                    pool.wait_ge(conv_step, 8 * m)
                pool.tensor_scalar(acc[:], r.H[:, m, :], cw[:, 36 + m:37 + m], None, ALU.mult).then_inc(conv_step, 1)
                for n, j in enumerate((2, 1, 0)):
                    w, back = cw[:, 12 * j + m:12 * j + m + 1], 3 - j
                    pool.wait_ge(conv_step, 8 * m + 2 * n + 1)
                    pool.tensor_scalar(tap[:, T:N], buf[:, m, :, j], w, None, ALU.mult)
                    pool.tensor_scalar(tap[:, back:T], r.H[:, m, 0:T - back], w, None, ALU.mult).then_inc(conv_step, 1)
                    pool.wait_ge(conv_step, 8 * m + 2 * n + 2)
                    pool.tensor_tensor(acc[:, back:N], acc[:, back:N], tap[:, back:N], ALU.add).then_inc(conv_step, 1)
                pool.wait_ge(conv_step, 8 * m + 7)
                pool.tensor_copy(r.H[:, m, :], acc[:]).then_inc(conv_step, 1)

        @block.tensor
        def _(pe):
            pe.wait_ge(means_ready, 2)
            pe.transpose(r.ps[0:32, 6, 0:P], vcbT[:], r.ident[:]).then_inc(vcb_turned, 1)
            pe.wait_ge(vcb_kept, 1)

            def scores(i, j):
                t, g = UNITS[j]
                rows = slice(64 * g, 64 * g + 64)
                lo, hi = max(0, t - 4) * P, (t + 1) * P
                pe.wait_ge(q_ready, i * TT + (t + 1))
                pe.wait_ge(exped, i * NU + (j + 1))
                for s in range(0, hi, 512):
                    e = min(hi, s + 512)
                    pe.matmul(s_sel[:, s:e], QS[rows, t % 2, :], r.H[rows, K_SEL, s:e], start=True, stop=True)
                for s in range(0, hi - lo, 512):
                    e = min(hi - lo, s + 512)
                    pe.matmul(s_win[:, s:e], QS[rows, t % 2, :], r.H[rows, K_WIN, lo + s:lo + e], start=True,
                              stop=True)
                pe.matmul(s_win[:, 640:672], QS[rows, t % 2, :], kcb[rows, :], start=True,
                          stop=True).then_inc(scored, 1)

            def turn(i, j):
                t, g = UNITS[j]
                pe.wait_ge(scaled, i * NU + (j + 1))
                lo = max(0, t - 4)
                for n, grp in enumerate(groups(t)):
                    gg = first[j] + n
                    pe.wait_ge(kept, i * GT + (max(gg - 1, 0) + 1))
                    for q, (kind, b) in enumerate(grp):
                        if kind == "cmp":
                            mm = pe.transpose(r.ps[0:32, 4 + gg % 2, 0:P], Pcmp[:, j % 2, :], r.ident[:])
                        else:
                            src = Psel[:, j % 2, b * P:(b + 1) * P] if kind == "sel" else \
                                Pwin[:, j % 2, (b - lo) * P:(b - lo + 1) * P]
                            mm = pe.transpose(r.ps[:, 4 + gg % 2, q * P:(q + 1) * P], src, r.ident[:])
                    mm.then_inc(turned, 1)

            def values(i, j):
                t, g = UNITS[j]
                bl = blocks(t)
                pe.wait_ge(kept, i * GT + (first[j + 1] + 1))
                pe.wait_ge(o_kept, i * NU + (max(j - 1, 0) + 1))
                for n, (kind, b) in enumerate(bl):
                    if kind == "cmp":
                        lhs, rhs = vcb[:], PT[0:32, 0, :]
                    else:
                        lhs = r.rows[:, b, 384:512] if kind == "sel" else r.rows[:, b, 640:768]
                        rhs = PT[:, n, :]
                    mm = pe.matmul(r.ps[:, 6 + j % 2, 0:P], lhs, rhs, start=(n == 0), stop=(n == len(bl) - 1))
                mm.then_inc(o_ready, 1)

            pe.sem_inc(scored, 1)
            pe.sem_inc(turned, 1)
            pe.sem_inc(o_ready, 1)
            with pe.Fori(0, 4) as i:
                scores(i, 0)
                for j in range(NU):
                    if j + 1 < NU:
                        scores(i, j + 1)
                    turn(i, j)
                    values(i, j)

        @block.scalar
        def _(act):
            act.sem_inc(exped, 1)
            act.sem_inc(kept, 1)
            with act.Fori(0, 4) as i:
                for j, (t, g) in enumerate(UNITS):
                    s = j % 2
                    lo, hi = max(0, t - 4) * P, (t + 1) * P
                    act.wait_ge(turned, i * GT + ((first[j - 1] if j else 0) + 1))
                    act.wait_ge(negated, i * NU + (j + 1))
                    act.activation(Pcmp[:, s, :], s_win[:, 640:672], ACT.Exp, bias=ntop[:, s, 0:1], scale=0.125,
                                   accum_out=den[:, s, 0:1])
                    act.activation(Psel[:, s, 0:hi], s_sel[:, 0:hi], ACT.Exp, bias=ntop[:, s, 1:2], scale=0.125,
                                   accum_out=den[:, s, 1:2])
                    act.activation(Pwin[:, s, 0:hi - lo], s_win[:, 0:hi - lo], ACT.Exp, bias=ntop[:, s, 2:3],
                                   scale=0.125, accum_out=den[:, s, 2:3]).then_inc(exped, 1)
                    at = 0
                    for n, grp in enumerate(groups(t)):
                        gg = first[j] + n
                        if n == 0:
                            act.wait_ge(o_ready, i * NU + (j + 1))
                        act.wait_ge(turned, i * GT + (gg + 2))
                        if n == 0:
                            act.copy(PT[0:32, 0, :], r.ps[0:32, 4 + gg % 2, 0:P]).then_inc(kept, 1)
                        else:
                            act.copy(PT[:, at:at + len(grp), :].rearrange("p b n -> p (b n)"),
                                     r.ps[:, 4 + gg % 2, 0:len(grp) * P]).then_inc(kept, 1)
                        at += len(grp)

        @block.vector
        def _(v):
            v.tensor_reduce(kcb[:], r.H[:, K_CMP, 0:T].rearrange("p (c j) -> p c j", j=32), AX.X, ALU.add)
            v.tensor_reduce(vcbT[:], r.H[:, V_CMP, 0:T].rearrange("p (c j) -> p c j", j=32), AX.X,
                            ALU.add).then_inc(means_ready, 1)
            v.wait_ge(means_ready, 1)
            v.tensor_scalar(kcb[:], kcb[:], 1 / 32, None, ALU.mult)
            v.tensor_scalar(vcbT[:], vcbT[:], 1 / 32, None, ALU.mult).then_inc(means_ready, 1)
            v.wait_ge(vcb_turned, 1)
            v.tensor_copy(vcb[:], r.ps[0:32, 6, 0:P]).then_inc(vcb_kept, 1)
            v.wait_ge(tables_in, 64)
            v.sem_inc(o_kept, 1)

            def fetch(i, t):
                v.wait_ge(scored, i * NU + (max(2 * t - 2, 0) + 1))
                v.tensor_copy(gates[:, t % 2, :, :], gate_view[:, t, :, bass.ds(i, 1), :].squeeze(2))
                v.tensor_copy(QS[:, t % 2, :], flat[:, bass.ds(i * N + (Q_B * N + t * P), P)]).then_inc(q_ready, 1)

            def maxima(i, j):
                t, g = UNITS[j]
                s = j % 2
                hi = (t + 1) * P
                w = hi - max(0, t - 4) * P
                v.wait_ge(scored, i * NU + (j + 2))
                v.tensor_tensor(s_sel[:, hi - P:hi], s_sel[:, hi - P:hi], causal[:], ALU.add)
                v.tensor_tensor(s_win[:, w - P:w], s_win[:, w - P:w], causal[:], ALU.add)
                if t >= 4:
                    v.tensor_tensor(s_win[:, 0:P], s_win[:, 0:P], oldest[:], ALU.add)
                v.tensor_tensor(s_win[:, 640:672], s_win[:, 640:672], cmp_add[:, t, :], ALU.add).then_inc(masked, 1)
                v.wait_ge(masked, i * NU + (j + 1))
                v.tensor_reduce(top[:, s, 0:1], s_win[:, 640:672], AX.X, ALU.max)
                v.tensor_reduce(top[:, s, 1:2], s_sel[:, 0:hi], AX.X, ALU.max)
                v.tensor_reduce(top[:, s, 2:3], s_win[:, 0:w], AX.X, ALU.max).then_inc(topped, 1)
                v.wait_ge(topped, i * NU + (j + 1))
                v.tensor_scalar(ntop[:, s, :], top[:, s, :], -0.125, None, ALU.mult).then_inc(negated, 1)

            def weigh(i, j):
                t, g = UNITS[j]
                s = j % 2
                hi = (t + 1) * P
                w = hi - max(0, t - 4) * P
                v.wait_ge(exped, i * NU + (j + 2))
                v.reciprocal(coef[:, s, :], den[:, s, :]).then_inc(inverted, 1)
                v.wait_ge(inverted, i * NU + (j + 1))
                v.tensor_tensor(coef[:, s, :], coef[:, s, :], gates[:, t % 2, g, :], ALU.mult).then_inc(weighed, 1)
                v.wait_ge(weighed, i * NU + (j + 1))
                v.scalar_tensor_tensor(out=Pcmp[:, s, :], in0=Pcmp[:, s, :], scalar=coef[:, s, 0:1],
                                       in1=cmp_one[:, t, :], op0=ALU.mult, op1=ALU.mult)
                v.tensor_scalar(Psel[:, s, 0:hi], Psel[:, s, 0:hi], coef[:, s, 1:2], None, ALU.mult)
                v.tensor_scalar(Pwin[:, s, 0:w], Pwin[:, s, 0:w], coef[:, s, 2:3], None, ALU.mult).then_inc(scaled, 1)

            with v.Fori(0, 4) as i:
                fetch(i, 0)
                maxima(i, 0)
                for j, (t, g) in enumerate(UNITS):
                    weigh(i, j)
                    if g == 0 and t + 1 < TT:
                        fetch(i, t + 1)
                    if j + 1 < NU:
                        maxima(i, j + 1)
                    v.wait_ge(o_ready, i * NU + (j + 2))
                    v.tensor_scalar(flat[64 * g:64 * g + 64, bass.ds(i * N + (Q_B * N + t * P), P)],
                                    r.ps[64 * g:64 * g + 64, 6 + j % 2, 0:P], 1.0, None,
                                    ALU.mult).then_inc(o_kept, 1)


def silu_phase(nc, r):
    with phase(nc) as ctx:
        block = ctx.enter_context(nc.Block())

        @block.scalar
        def _(act):
            for m in range(0, GATE_A + 4, 4):
                act.activation(r.H[:, m:m + 4, :], r.H[:, m:m + 4, :], ACT.Silu)


class Sweep:

    def __init__(self, r, kp_last):
        x = r.X[:].rearrange("p k n -> p (k n)")
        size = PGRP * 384

        def pages(ap):
            return ap.rearrange("p (j n) -> p j n", j=PGRP)

        self.KP = [pages(x[:, 0:size]), pages(x[:, size:2 * size]),
                   pages(r.H[:, K_CMP:K_CMP + 2, :].rearrange("p k n -> p (k n)")[:, 0:size]), kp_last]
        at = 2 * size
        self.SC = x[0:NS * 8, at:at + PAGES * P + 1]
        at += PAGES * P + 4
        self.level = x[:, at:at + LEVELS * P].rearrange("p (l n) -> p l n", l=LEVELS)
        at += LEVELS * P
        self.pool = x[:, at:at + 4]
        self.KT = r.H[:, K_SEL, 0:1024].rearrange("p (u n) -> p u n", u=2)
        self.VCT = r.H[:, V_SEL, 0:1024].rearrange("p (s n) -> p s n", s=NS)
        self.KC = r.H[:, K_WIN, 0:1024].rearrange("p (s n) -> p s n", s=NS)
        self.Q = r.H[:, V_WIN, 0:NS * 64]
        self.Qs = self.Q.rearrange("p (s q) -> p s q", s=NS)
        self.pages = r.H[0:1, V_WIN, NS * 64:NS * 64 + NS * PAGES].bitcast(I32)


def delta_prompt_phase(nc, r):
    assert NG == TT and NS == 2 * (LEVELS - 3)
    cache = r.cache.rearrange("n e t c g d -> (n e) t (c g d)")
    n_pool = r.cache.shape[0]
    R = 64
    H4 = range(HEADS)
    with phase(nc) as ctx:
        def sb(name, shape):
            return ctx.enter_context(nc.sbuf_tensor("dp_" + name, shape, F32))

        sw = Sweep(r, sb("kp_last", [P, PGRP, 384])[:])
        level, upper, rowsel = sw.level, sb("upper", [P, P]), sb("rowsel", [NSMALL, 8, P])
        ng = sb("ng", [P, 1])
        SQ, RN = sb("sq", [P, 8, P]), sb("rn", [P, 8, P])
        QT, KT, VT, GB, DL, EG, QG, AT, QK = [sb(n, [P, 4, P]) for n in
                                              ("qt", "kt", "vt", "gb", "dl", "eg", "qg", "at", "qk")]
        AM = sb("am", [P, 2, 4, P])
        Dm, DT, PS, KBG, KD, VB, S, RO = [sb(n, [P, 4, P]) for n in ("d", "dt", "p", "kbg", "kd", "vb", "s", "ro")]
        U, WT = SQ[:, 0:4, :], SQ[:, 4:8, :]
        VN, OS = RN[:, 0:4, :], RN[:, 4:8, :]
        tk, e4, bg = sb("tk", [P, 12]), sb("e4", [P, 8]), sb("bg", [P, 4])
        names = ("tables_in", "chunk_done", "squared", "sums_ready", "logged", "rn_ready", "gb_ready", "v_copied",
                 "decay_in", "decay_ready", "qk_ready", "turned", "kk_ready", "lt_masked", "at_half", "at_ready",
                 "bg_ready", "kbg_ready", "kdv_ready", "am_ready", "p_ready", "p_kept", "d_ready", "dt_ready",
                 "d_updated", "dt_updated",
                 "uw_ready", "wt_kept", "u_kept", "ws_ready", "vn_ready", "o_ready", "ds_ready", "o_squared",
                 "o_summed", "o_logged", "ro_ready", "o_scaled", "s_ready", "stored")
        (tables_in, chunk_done, squared, sums_ready, logged, rn_ready, gb_ready, v_copied, decay_in, decay_ready,
         qk_ready, turned, kk_ready, lt_masked, at_half, at_ready, bg_ready, kbg_ready, kdv_ready, am_ready, p_ready,
         p_kept, d_ready, dt_ready, d_updated, dt_updated, uw_ready, wt_kept, u_kept, ws_ready, vn_ready, o_ready, ds_ready, o_squared,
         o_summed, o_logged, ro_ready, o_scaled, s_ready, stored) = [
            nc.alloc_semaphore("dp_" + s) for s in names]
        pages_in, q_zero, q_ready, k_turned, kt_kept, kt_used, pooled, pool_kept, sc_kept = [
            nc.alloc_semaphore("dp_" + s) for s in
            ("pages_in", "q_zero", "q_ready", "k_turned", "kt_kept", "kt_used", "pooled", "pool_kept", "sc_kept")]
        kp_in = [nc.alloc_semaphore(f"dp_kp_in{u}") for u in range(4)]
        block = ctx.enter_context(nc.Block())

        def samples(lv):
            return range(2 * (lv - 2), 2 * (lv - 2) + 2) if 2 <= lv < LEVELS - 1 else ()

        def bank(b):
            return r.ps[:, b, :].rearrange("p (h n) -> p h n", h=4)

        @block.sync
        def _(sp):
            for dst, src in ((level.rearrange("p l n -> p (l n)"), r.c_level), (upper[:], r.c_upper),
                             (rowsel[:].rearrange("p l n -> p (l n)"), r.c_rowsel), (ng[:], r.delta_ng),
                             (sw.pool, r.c_pool)):
                sp.dma_start(dst, src).then_inc(tables_in, 16)
            sp.dma_start(sw.pages, r.page_table.rearrange("(a b) n -> a (b n)", a=1)).then_inc(pages_in, 16)
            sp.wait_ge(pages_in, 16)
            with sp.Fori(0, NG) as c:
                for s in range(NS):
                    sp.wait_ge(k_turned, c * NS + (s + 1))
                    for j in range(PGRP):
                        page = sp.value_load(sw.pages[0:1, bass.ds(c * PGRP + (s * PAGES + j), 1)], min_val=0,
                                             max_val=n_pool - 1)
                        sp.dma_start(sw.KP[s % 4][:, j, :],
                                     cache[bass.ds(page, 1), :, 0:384].squeeze(0)).then_inc(kp_in[s % 4], 16)
            sp.wait_ge(s_ready, TT + 1)
            sp.dma_start(r.o_dS_p[0, 0].rearrange("h d e -> d h e"), S[:]).then_inc(stored, 16)
            sp.wait_ge(stored, 16)

        @block.scalar
        def _(act):
            act.preload_act_table_set("natural_log_exp_and_others")
            act.sem_inc(kt_kept, 2)
            with act.Fori(0, TT) as c:
                cols = bass.ds(c * P, P)
                act.wait_ge(chunk_done, c + 1)
                act.wait_ge(tables_in, 80)
                act.activation(SQ[:], r.H[:, Q_A:Q_A + 8, cols], ACT.Square).then_inc(squared, 1)
                act.copy(VT[:], r.H[:, V_A:V_A + 4, cols]).then_inc(v_copied, 1)
                act.wait_ge(sums_ready, c + 1)
                act.activation(RN[:].rearrange("p k n -> p (k n)"), r.ps[:, 0:2, :].rearrange("p b n -> p (b n)"),
                               ACT.Ln, bias=r.bias[:, 1:2]).then_inc(logged, 1)
                act.wait_ge(logged, c + 1)
                act.activation(RN[:], RN[:], ACT.Exp, scale=-0.5).then_inc(rn_ready, 1)
                act.wait_ge(decay_in, c + 1)
                act.activation(DL[:], DL[:], ACT.Exp)
                act.activation(EG[:], GB[:], ACT.Exp)
                act.activation(e4[:], tk[:, 4:12], ACT.Exp).then_inc(decay_ready, 1)
                act.wait_ge(decay_ready, c + 1)
                act.wait_ge(turned, c + 1)
                for h in H4:
                    act.activation(KD[:, h, :], bank(4)[:, h, :], ACT.Copy, scale=e4[:, 4 + h:5 + h])
                for h in H4:
                    mm = act.activation(VB[:, h, :], bank(5)[:, h, :], ACT.Copy, scale=tk[:, h:h + 1])
                mm.then_inc(kdv_ready, 1)
                for lv in range(1, LEVELS):
                    act.wait_ge(p_ready, c * LEVELS + (lv + 1))
                    act.copy(PS[:], bank(6)).then_inc(p_kept, 1)
                    for s in samples(lv):
                        act.wait_ge(k_turned, c * NS + (s + 5))
                        act.wait_ge(kt_used, c * NS + (s + 1))
                        act.copy(sw.KT[:, s % 2, :], r.ps[:, s % 2, :]).then_inc(kt_kept, 1)
                act.wait_ge(uw_ready, c + 1)
                act.copy(WT, bank(1)).then_inc(wt_kept, 1)
                act.wait_ge(o_ready, c + 1)
                act.activation(OS, bank(5), ACT.Square).then_inc(o_squared, 1)
                act.wait_ge(o_summed, c + 1)
                act.activation(RO[:], bank(7), ACT.Ln, bias=r.bias[:, 1:2], scale=1 / 128).then_inc(o_logged, 1)
                act.wait_ge(o_logged, c + 1)
                act.activation(RO[:], RO[:], ACT.Exp, scale=-0.5).then_inc(ro_ready, 1)

        @block.tensor
        def _(pe):
            pe.wait_ge(tables_in, 80)
            pe.wait_ge(q_ready, 1)
            pe.sem_inc(k_turned, 4)
            pe.sem_inc(kt_used, 2)

            def turn(c, s):
                pe.wait_ge(kp_in[s % 4], c * 128 + (s // 4 + 1) * 64)
                pe.wait_ge(pool_kept, c * NS + (s + 1))
                for part in range(2):
                    for j in range(PGRP):
                        mm = pe.matmul(r.ps[:, 4 + s % 2, 16 * part + 4 * j:16 * part + 4 * j + 4],
                                       sw.KP[s % 4][:, j, part * P:(part + 1) * P], sw.pool, start=True, stop=True)
                mm.then_inc(pooled, 1)
                pe.wait_ge(kt_kept, c * NS + (s + 1))
                for j in range(PGRP):
                    mm = pe.transpose(r.ps[:, s % 2, j * P:(j + 1) * P], sw.KP[s % 4][:, j, 256:384], r.ident[:])
                mm.then_inc(k_turned, 1)

            def scores(c, s):
                pe.wait_ge(kt_kept, c * NS + (s + 3))
                pe.matmul(r.ps[0:R, 2, :], sw.Qs[:, s, :], sw.KT[:, s % 2, :], start=(s == 0),
                          stop=(s == NS - 1)).then_inc(kt_used, 1)

            def step(c, n):
                if 0 <= n < NS:
                    turn(c, n)
                if 1 <= n <= NS:
                    scores(c, n - 1)

            with pe.Fori(0, TT) as c:
                cols = bass.ds(c * P, P)
                pe.wait_ge(squared, c + 1)
                pe.matmul(r.ps[:, 0, :], r.ones[:], SQ[:, 0:4, :], start=True, stop=True)
                pe.matmul(r.ps[:, 1, :], r.ones[:], SQ[:, 4:8, :], start=True, stop=True)
                pe.wait_ge(sc_kept, c + 1)
                for j in range(8):
                    mm = pe.matmul(bank(2 + j // 4)[:, j % 4, :], rowsel[:, j, :], r.H[0:NSMALL, SMALL, cols],
                                   start=True, stop=True)
                mm.then_inc(sums_ready, 1)
                pe.wait_ge(v_copied, c + 1)
                for h in H4:
                    pe.transpose(bank(5)[:, h, :], VT[:, h, :], r.ident[:])
                pe.wait_ge(qk_ready, c + 1)
                for h in H4:
                    mm = pe.transpose(bank(4)[:, h, :], KT[:, h, :], r.ident[:])
                mm.then_inc(turned, 1)
                for h in H4:
                    pe.matmul(bank(0)[:, h, :], KT[:, h, :], KT[:, h, :], start=True, stop=True)
                for h in H4:
                    mm = pe.matmul(bank(1)[:, h, :], KT[:, h, :], QT[:, h, :], start=True, stop=True)
                mm.then_inc(kk_ready, 1)
                pe.wait_ge(am_ready, c * LEVELS + 1)
                for h in H4:
                    mm = pe.transpose(bank(6)[:, h, :], AM[:, 0, h, :], r.ident[:])
                mm.then_inc(p_ready, 1)
                for lv in range(1, LEVELS):
                    pe.wait_ge(am_ready, c * LEVELS + (lv + 1))
                    pe.wait_ge(d_updated, c * (LEVELS - 1) + lv)
                    for h in H4:
                        mm = pe.matmul(bank(6)[:, h, :], AM[:, lv % 2, h, :], Dm[:, h, :], start=True, stop=True)
                    mm.then_inc(p_ready, 1)
                    step(c, 2 * (lv - 2))
                    pe.wait_ge(p_kept, c * (LEVELS - 1) + lv)
                    pe.wait_ge(dt_updated, c * LEVELS + lv)
                    if lv < LEVELS - 1:
                        for h in H4:
                            mm = pe.matmul(bank(7)[:, h, :], DT[:, h, :], PS[:, h, :], start=True, stop=True)
                        mm.then_inc(d_ready, 1)
                    for h in H4:
                        mm = pe.matmul(bank(3)[:, h, :], PS[:, h, :], DT[:, h, :], start=True, stop=True)
                    mm.then_inc(dt_ready, 1)
                    step(c, 2 * (lv - 2) + 1)
                pe.wait_ge(pool_kept, c * NS + (NS + 2))
                pe.wait_ge(dt_updated, c * LEVELS + LEVELS)
                pe.wait_ge(kdv_ready, c + 1)
                pe.wait_ge(kbg_ready, c + 1)
                for h in H4:
                    pe.matmul(bank(0)[:, h, :], DT[:, h, :], VB[:, h, :], start=True, stop=True)
                for h in H4:
                    mm = pe.matmul(bank(1)[:, h, :], KBG[:, h, :], DT[:, h, :], start=True, stop=True)
                mm.then_inc(uw_ready, 1)
                pe.wait_ge(wt_kept, c + 1)
                pe.wait_ge(s_ready, c + 1)
                for h in H4:
                    mm = pe.matmul(bank(4)[:, h, :], WT[:, h, :], S[:, h, :], start=True, stop=True)
                mm.then_inc(ws_ready, 1)
                pe.wait_ge(vn_ready, c + 1)
                for h in H4:
                    pe.matmul(bank(5)[:, h, :], S[:, h, :], QG[:, h, :], start=True, stop=False)
                    mm = pe.matmul(bank(5)[:, h, :], VN[:, h, :], QK[:, h, :], start=False, stop=True)
                mm.then_inc(o_ready, 1)
                for h in H4:
                    mm = pe.matmul(bank(6)[:, h, :], KD[:, h, :], VN[:, h, :], start=True, stop=True)
                mm.then_inc(ds_ready, 1)
                pe.wait_ge(o_squared, c + 1)
                pe.matmul(r.ps[:, 7, :], r.ones[:], OS, start=True, stop=True).then_inc(o_summed, 1)

        def means(v, c, s):
            v.wait_ge(pooled, c * NS + (s + 1))
            v.tensor_copy(sw.KC[:, s, bass.ds(c * 16, 16)], r.ps[:, 4 + s % 2, 0:16])
            v.tensor_copy(sw.VCT[:, s, bass.ds(c * 16, 16)], r.ps[:, 4 + s % 2, 16:32]).then_inc(pool_kept, 1)

        ident4 = r.ident[:].unsqueeze(1).to_broadcast([P, 4, P])

        def update(v, c, lv):
            if lv == 0:
                v.wait_ge(p_ready, c * LEVELS + 1)
                v.tensor_tensor(Dm[:], ident4, bank(6), ALU.subtract).then_inc(d_updated, 1)
                v.tensor_tensor(DT[:], ident4, AM[:, 0], ALU.subtract).then_inc(dt_updated, 1)
                return
            if lv < LEVELS - 1:
                v.wait_ge(d_ready, c * (LEVELS - 2) + lv)
                v.tensor_tensor(Dm[:], Dm[:], bank(7), ALU.subtract).then_inc(d_updated, 1)
            v.wait_ge(dt_ready, c * (LEVELS - 1) + lv)
            v.tensor_tensor(DT[:], DT[:], bank(3), ALU.subtract).then_inc(dt_updated, 1)

        @block.vector
        def _(v):
            v.wait_ge(tables_in, 80)
            v.memset(S[:], 0.0).then_inc(s_ready, 1)
            v.sem_inc(chunk_done, 1)
            v.sem_inc(pool_kept, 2)
            v.sem_inc(sc_kept, 1)
            v.memset(sw.Q, 0.0).then_inc(q_zero, 1)
            v.wait_ge(q_zero, 1)
            for i in range(4):
                for g in range(2):
                    h = i + 4 * g
                    mm = v.tensor_copy(sw.Q[64 * g:64 * g + 64, h:h + 72 * (NS - 1) + 1:72],
                                       r.H[64 * g:64 * g + 64, Q_B + i, T:N])
            mm.then_inc(q_ready, 1)
            upper4 = upper[:].unsqueeze(1).to_broadcast([P, 4, P])
            with v.Fori(0, TT) as c:
                cols = bass.ds(c * P, P)
                v.wait_ge(chunk_done, c + 1)
                v.tensor_copy(tk[:, 0:4], r.tok[:, bass.ds(c, 1), R_BETA:R_BETA + 4].squeeze(1))
                v.tensor_copy(tk[:, 4:8], r.tok[:, bass.ds(c, 1), R_G:R_G + 4].squeeze(1))
                v.wait_ge(sums_ready, c + 1)
                v.tensor_copy(GB[:], bank(3)).then_inc(gb_ready, 1)
                v.wait_ge(gb_ready, c + 1)
                for h in H4:
                    v.tensor_scalar(DL[:, h, :], GB[:, h, :], tk[:, 4 + h:5 + h], 0.0, ALU.subtract, ALU.min)
                v.tensor_tensor(tk[:, 8:12], GB[:, :, P - 1], tk[:, 4:8], ALU.subtract).then_inc(decay_in, 1)
                v.wait_ge(rn_ready, c + 1)
                v.scalar_tensor_tensor(out=QT[:], in0=r.H[:, Q_A:Q_A + 4, cols], scalar=128 ** -0.5, in1=RN[:, 0:4, :],
                                       op0=ALU.mult, op1=ALU.mult)
                v.tensor_tensor(KT[:], r.H[:, K_A:K_A + 4, cols], RN[:, 4:8, :], ALU.mult).then_inc(qk_ready, 1)
                v.wait_ge(decay_ready, c + 1)
                v.tensor_tensor(DL[:], DL[:], upper4, ALU.mult).then_inc(lt_masked, 1)
                v.tensor_tensor(bg[:], tk[:, 0:4], e4[:, 0:4], ALU.mult).then_inc(bg_ready, 1)
                v.wait_ge(lt_masked, c + 1)
                v.wait_ge(kk_ready, c + 1)
                v.tensor_tensor(AT[:], bank(0), DL[:], ALU.mult).then_inc(at_half, 1)
                v.wait_ge(at_half, c + 1)
                v.tensor_tensor(AT[:], AT[:], bank(2), ALU.mult).then_inc(at_ready, 1)
                v.wait_ge(at_ready, c + 1)
                for lv in range(LEVELS):
                    if lv >= 2:
                        v.wait_ge(p_ready, c * LEVELS + (lv - 1))
                    if lv == 2:
                        v.wait_ge(dt_updated, c * LEVELS + 1)
                    v.tensor_tensor(AM[:, lv % 2], AT[:], level[:, lv, :].unsqueeze(1).to_broadcast([P, 4, P]),
                                    ALU.mult).then_inc(am_ready, 1)
                    if lv == 0:
                        v.tensor_tensor(QK[:], bank(1), DL[:], ALU.mult)
                        v.wait_ge(qk_ready, c + 1)
                        v.tensor_tensor(QG[:], QT[:], EG[:], ALU.mult)
                    if lv == 1:
                        v.wait_ge(bg_ready, c + 1)
                        v.wait_ge(turned, c + 1)
                        v.wait_ge(kdv_ready, c + 1)
                        for h in H4:
                            mm = v.tensor_scalar(KBG[:, h, :], bank(4)[:, h, :], bg[:, h:h + 1], None, ALU.mult)
                        mm.then_inc(kbg_ready, 1)
                    if samples(lv - 2):
                        means(v, c, samples(lv - 2)[1])
                    if samples(lv - 1):
                        means(v, c, samples(lv - 1)[0])
                    if lv:
                        update(v, c, lv - 1)
                means(v, c, NS - 1)
                update(v, c, LEVELS - 1)
                v.wait_ge(uw_ready, c + 1)
                v.tensor_copy(U, bank(0)).then_inc(u_kept, 1)
                v.wait_ge(u_kept, c + 1)
                v.wait_ge(ws_ready, c + 1)
                v.tensor_tensor(VN, U, bank(4), ALU.subtract).then_inc(vn_ready, 1)
                v.wait_ge(kt_used, c * NS + (NS + 2))
                v.tensor_copy(sw.SC[:, bass.ds(c * (PGRP * P), PGRP * P)], r.ps[0:R, 2, :]).then_inc(sc_kept, 1)
                v.wait_ge(ds_ready, c + 1)
                for h in H4:
                    mm = v.scalar_tensor_tensor(out=S[:, h, :], in0=S[:, h, :], scalar=EG[:, h, P - 1:P],
                                                in1=bank(6)[:, h, :], op0=ALU.mult, op1=ALU.add)
                mm.then_inc(s_ready, 1)
                v.wait_ge(ro_ready, c + 1)
                v.scalar_tensor_tensor(out=RO[:], in0=bank(5), scalar=ng[:, 0:1], in1=RO[:], op0=ALU.mult,
                                       op1=ALU.mult).then_inc(o_scaled, 1)
                v.wait_ge(o_scaled, c + 1)
                v.tensor_tensor(r.H[:, GATE_A:GATE_A + 4, cols], RO[:], r.H[:, GATE_A:GATE_A + 4, cols],
                                ALU.mult).then_inc(chunk_done, 1)


def gla_gate_phase(nc, r):
    with phase(nc) as ctx:
        g2 = ctx.enter_context(nc.sbuf_tensor("gg_w", [16, 512], F32))
        b2 = ctx.enter_context(nc.sbuf_tensor("gg_b", [P, 4], F32))
        az = ctx.enter_context(nc.sbuf_tensor("gg_az", [P, 2, N], F32))
        w_in, product, biased, absed, exped, logged, lowered, done = [
            nc.alloc_semaphore("gg_" + s) for s in
            ("w_in", "product", "biased", "absed", "exped", "logged", "lowered", "done")]
        block = ctx.enter_context(nc.Block())

        @block.sync
        def _(sp):
            sp.dma_start(g2[:], r.w_g2).then_inc(w_in, 16)
            sp.dma_start(b2[:], r.b_g2).then_inc(w_in, 16)

        @block.tensor
        def _(pe):
            pe.wait_ge(w_in, 32)
            for m in range(4):
                if m >= 2:
                    pe.wait_ge(biased, m - 1)
                for c in range(NB):
                    mm = pe.matmul(r.ps[:, m % 2 * 3 + c, 0:CW], g2[:, m * P:(m + 1) * P],
                                   r.H[0:16, OG1, c * CW:(c + 1) * CW], start=True, stop=True)
                mm.then_inc(product, 1)

        @block.vector
        def _(v):
            def log_sigmoid(m):
                v.wait_ge(logged, m + 1)
                v.scalar_tensor_tensor(out=r.LA[:, m, :], in0=r.LA[:, m, :], scalar=0.0, in1=az[:, m % 2, :],
                                       op0=ALU.min, op1=ALU.subtract).then_inc(lowered, 1)
                v.wait_ge(lowered, m + 1)
                v.tensor_scalar(r.LA[:, m, :], r.LA[:, m, :], 1 / 16, None, ALU.mult).then_inc(done, 1)

            v.wait_ge(w_in, 32)
            for m in range(4):
                v.wait_ge(product, m + 1)
                for c in range(NB):
                    mm = v.tensor_scalar(r.LA[:, m, c * CW:(c + 1) * CW], r.ps[:, m % 2 * 3 + c, 0:CW], b2[:, m:m + 1],
                                         None, ALU.add)
                mm.then_inc(biased, 1)
                if m >= 2:
                    log_sigmoid(m - 2)
                v.wait_ge(biased, m + 1)
                v.scalar_tensor_tensor(out=az[:, m % 2, :], in0=r.LA[:, m, :], scalar=-1.0, in1=r.LA[:, m, :],
                                       op0=ALU.mult, op1=ALU.max).then_inc(absed, 1)
            log_sigmoid(2)
            log_sigmoid(3)

        @block.scalar
        def _(act):
            act.preload_act_table_set("natural_log_exp_and_others")
            for m in range(4):
                act.wait_ge(absed, m + 1)
                act.activation(az[:, m % 2, :], az[:, m % 2, :], ACT.Exp, scale=-1.0).then_inc(exped, 1)
                act.wait_ge(exped, m + 1)
                act.activation(az[:, m % 2, :], az[:, m % 2, :], ACT.Ln, bias=1.0).then_inc(logged, 1)
            act.activation(r.H[:, OR_:OR_ + 8, :], r.H[:, OR_:OR_ + 8, :], ACT.Silu)


def gla_prompt_phase(nc, r):
    H4 = range(HEADS)
    with phase(nc) as ctx:
        def sb(name, shape):
            return ctx.enter_context(nc.sbuf_tensor("gp_" + name, shape, F32))

        upper, keep16, one = sb("upper", [P, P]), sb("keep16", [P, P]), sb("one", [P, P])
        gn = sb("gn", [P, 2])
        VT, VK2, OS = sb("vt", [P, 8, P]), sb("vk", [P, 2, 8, P]), sb("os", [P, 8, P])
        B, BL, QL, KD, RO = [sb(n, [P, 4, P]) for n in ("b", "bl", "ql", "kd", "ro")]
        QB2, KT2, ATT2 = [sb(n, [P, 2, 4, P]) for n in ("qb", "kt", "att")]
        BR = sb("br", [P, 4, 8])
        GL2 = sb("gl", [P, 2, 4])
        EX = sb("ex", [P, 2, 8, P])
        S = sb("s", [P, 4, GV])
        names = ("tables_in", "chunk_done", "v_copied", "v_turned", "v_kept", "scanned", "ref_ready", "q_exped",
                 "kd_exped", "kd_ready", "kd_turned", "kd_kept", "q_ready", "ex_ready", "kx_ready", "att_ready",
                 "att_kept", "o_ready", "ds_ready", "s_ready", "o_squared", "o_summed", "o_logged", "ro_ready",
                 "o_scaled", "stored", "zeroed")
        (tables_in, chunk_done, v_copied, v_turned, v_kept, scanned, ref_ready, q_exped, kd_exped, kd_ready, kd_turned,
         kd_kept, q_ready, ex_ready, kx_ready, att_ready, att_kept, o_ready, ds_ready, s_ready, o_squared, o_summed,
         o_logged, ro_ready, o_scaled, stored, zeroed) = [nc.alloc_semaphore("gp_" + s) for s in names]
        block = ctx.enter_context(nc.Block())

        def bank(b):
            return r.ps[:, b, :].rearrange("p (h n) -> p h n", h=4)

        def pair(b):
            return r.ps[:, b:b + 2, :].rearrange("p b (h n) -> p (b h) n", h=4)

        def run(eng, body, front, back):
            front(0, 0)
            with eng.Fori(0, (TT - 2) // 2) as i:
                for u in range(2):
                    body(i * 2 + u, u, True)
            body(TT - 2, 0, False)
            back(TT - 1, 1)

        @block.sync
        def _(sp):
            sp.dma_start(upper[:], r.c_upper).then_inc(tables_in, 16)
            sp.dma_start(gn[:], r.gla_ng).then_inc(tables_in, 16)
            sp.wait_ge(s_ready, TT + 1)
            sp.dma_start(r.o_gS_p[0, 0].rearrange("h d e -> d h e"), S[:]).then_inc(stored, 16)
            sp.wait_ge(stored, 16)

        @block.scalar
        def _(act):
            act.preload_act_table_set("natural_log_exp_and_others")
            act.wait_ge(zeroed, 1)

            def copies(n):
                act.copy(VT[:], r.H[:, OV:OV + 8, bass.ds(n * P, P)]).then_inc(v_copied, 1)

            def decays(n, slot, first=False):
                if not first:
                    act.wait_ge(att_ready, n * 4)
                act.wait_ge(ref_ready, n + 1)
                act.activation(QL[:], BL[:], ACT.Exp)
                act.activation(QB2[:, slot], B[:], ACT.Exp).then_inc(q_exped, 1)
                act.activation(GL2[:, slot], B[:, :, P - 1], ACT.Exp)
                for h in H4:
                    mm = act.activation(KD[:, h, :], B[:, h, :], ACT.Exp, bias=B[:, h, P - 1:P], scale=-1.0)
                mm.then_inc(kd_exped, 1)

            def values(n, slot):
                act.wait_ge(v_turned, n + 1)
                act.copy(VK2[:, slot], pair(0)).then_inc(v_kept, 1)

            def factors(n, slot, heads):
                for h in heads:
                    if h >= 2:
                        act.wait_ge(att_ready, n * 4 + (h - 1))
                    for b in range(8):
                        mm = act.activation(EX[:, h % 2, b, 0:16 * (b + 1)], B[:, h, 0:16 * (b + 1)], ACT.Exp,
                                            bias=BR[:, h, b:b + 1], scale=-1.0)
                    mm.then_inc(ex_ready, 1)
                    if h == 1:
                        act.wait_ge(kd_turned, n + 1)
                        act.copy(KT2[:, slot], bank(2)).then_inc(kd_kept, 1)

            def squares(c):
                act.wait_ge(chunk_done, c + 1)
                act.wait_ge(o_ready, c + 1)
                act.activation(OS[:], pair(4), ACT.Square).then_inc(o_squared, 1)

            def norms(c):
                act.wait_ge(o_summed, c + 1)
                act.activation(RO[:], bank(6), ACT.Ln, bias=r.bias[:, 1:2], scale=1 / GV).then_inc(o_logged, 1)
                act.wait_ge(o_logged, c + 1)
                act.activation(RO[:], RO[:], ACT.Exp, scale=-0.5).then_inc(ro_ready, 1)

            def front(n, slot):
                copies(n)
                decays(n, slot, first=True)
                values(n, slot)
                factors(n, slot, H4)

            def body(c, slot, more):
                copies(c + 1)
                decays(c + 1, 1 - slot)
                values(c + 1, 1 - slot)
                factors(c + 1, 1 - slot, (0,))
                squares(c)
                factors(c + 1, 1 - slot, (1,))
                norms(c)
                factors(c + 1, 1 - slot, (2, 3))

            def back(c, slot):
                squares(c)
                norms(c)

            run(act, body, front, back)

        @block.tensor
        def _(pe):
            pe.wait_ge(tables_in, 32)

            def turn_values(n, first=False):
                pe.wait_ge(v_copied, n + 1)
                if not first:
                    pe.wait_ge(v_kept, n)
                for j in range(8):
                    mm = pe.transpose(pair(0)[:, j, :], VT[:, j, :], r.ident[:])
                mm.then_inc(v_turned, 1)

            def turn_keys(n):
                pe.wait_ge(kd_ready, n + 1)
                for h in H4:
                    mm = pe.transpose(bank(2)[:, h, :], KD[:, h, :], r.ident[:])
                mm.then_inc(kd_turned, 1)

            def scores(n, heads):
                pe.wait_ge(q_ready, n + 1)
                for h in heads:
                    pe.wait_ge(kx_ready, n * 4 + (h + 1))
                    for b in range(8):
                        mm = pe.matmul(bank(3)[:, h, 16 * b:16 * b + 16], EX[:, h % 2, b, :],
                                       QL[:, h, 16 * b:16 * b + 16], start=True, stop=True)
                    mm.then_inc(att_ready, 1)

            def outputs(c, slot):
                pe.wait_ge(att_kept, c + 1)
                pe.wait_ge(s_ready, c + 1)
                pe.wait_ge(v_kept, c + 1)
                pe.wait_ge(chunk_done, c + 1)
                for h in H4:
                    for e in range(2):
                        pe.matmul(pair(4)[:, 2 * h + e, :], S[:, h, e * P:(e + 1) * P], QB2[:, slot, h, :], start=True,
                                  stop=False)
                        mm = pe.matmul(pair(4)[:, 2 * h + e, :], VK2[:, slot, 2 * h + e, :], ATT2[:, slot, h, :],
                                       start=False, stop=True)
                mm.then_inc(o_ready, 1)
                pe.wait_ge(kd_kept, c + 1)
                for h in H4:
                    mm = pe.matmul(pair(6)[:, 2 * h:2 * h + 2, :], KT2[:, slot, h, :], VK2[:, slot, 2 * h:2 * h + 2, :],
                                   start=True, stop=True)
                mm.then_inc(ds_ready, 1)

            def sums(c):
                pe.wait_ge(o_squared, c + 1)
                pe.wait_ge(s_ready, c + 2)
                sq = OS[:].rearrange("p (h e) n -> p h e n", e=2)
                pe.matmul(r.ps[:, 6, :], r.ones[:], sq[:, :, 0, :], start=True, stop=False)
                pe.matmul(r.ps[:, 6, :], r.ones[:], sq[:, :, 1, :], start=False, stop=True).then_inc(o_summed, 1)

            def front(n, slot):
                turn_values(n, first=True)
                turn_keys(n)
                scores(n, H4)

            def body(c, slot, more):
                turn_values(c + 1)
                outputs(c, slot)
                turn_keys(c + 1)
                scores(c + 1, (0, 1))
                sums(c)
                scores(c + 1, (2, 3))

            def back(c, slot):
                outputs(c, slot)
                sums(c)

            run(pe, body, front, back)

        @block.vector
        def _(v):
            v.memset(S[:], 0.0).then_inc(s_ready, 1)
            v.memset(EX[:], 0.0)
            v.memset(one[:], 1.0)
            v.memset(keep16[:], 1.0).then_inc(zeroed, 1)
            v.wait_ge(zeroed, 1)
            v.memset(keep16[:].rearrange("p (b t) -> p b t", t=16)[:, :, 0:1], 0.0).then_inc(zeroed, 1)
            v.wait_ge(zeroed, 2)
            v.wait_ge(tables_in, 32)
            v.sem_inc(chunk_done, 1)

            def sums(n):
                for h in H4:
                    la = r.LA[:, h, bass.ds(n * P, P)]
                    v.tensor_tensor_scan(B[:, h, :], one[:], la, 0.0, ALU.mult, ALU.add)
                    mm = v.tensor_tensor_scan(BL[:, h, :], keep16[:], la, 0.0, ALU.mult, ALU.add)
                mm.then_inc(scanned, 1)
                v.wait_ge(scanned, n + 1)
                v.tensor_tensor(BR[:], B[:].rearrange("p h (b t) -> p h b t", t=16)[:, :, :, 0],
                                BL[:].rearrange("p h (b t) -> p h b t", t=16)[:, :, :, 0],
                                ALU.subtract).then_inc(ref_ready, 1)

            def queries(n, slot):
                q = r.H[:, OQ:OQ + 4, bass.ds(n * P, P)]
                v.wait_ge(q_exped, n + 1)
                v.scalar_tensor_tensor(out=QL[:], in0=q, scalar=128 ** -0.5, in1=QL[:], op0=ALU.mult, op1=ALU.mult)
                v.scalar_tensor_tensor(out=QB2[:, slot], in0=q, scalar=128 ** -0.5, in1=QB2[:, slot], op0=ALU.mult,
                                       op1=ALU.mult).then_inc(q_ready, 1)

            def keys(n):
                v.wait_ge(kd_exped, n + 1)
                v.tensor_tensor(KD[:], r.H[:, OK:OK + 4, bass.ds(n * P, P)], KD[:], ALU.mult).then_inc(kd_ready, 1)

            def factors(n, heads):
                for h in heads:
                    v.wait_ge(ex_ready, n * 4 + (h + 1))
                    v.tensor_tensor(EX[:, h % 2], EX[:, h % 2],
                                    r.H[:, OK + h, bass.ds(n * P, P)].unsqueeze(1).to_broadcast([P, 8, P]),
                                    ALU.mult).then_inc(kx_ready, 1)

            def attention(n, slot):
                v.wait_ge(att_ready, n * 4 + 4)
                v.tensor_tensor(ATT2[:, slot], bank(3), upper[:].unsqueeze(1).to_broadcast([P, 4, P]),
                                ALU.mult).then_inc(att_kept, 1)

            def state(c, slot):
                v.wait_ge(ds_ready, c + 1)
                for h in H4:
                    mm = v.scalar_tensor_tensor(out=S[:, h, :], in0=S[:, h, :], scalar=GL2[:, slot, h:h + 1],
                                                in1=pair(6)[:, 2 * h:2 * h + 2, :].rearrange("p e n -> p (e n)"),
                                                op0=ALU.mult, op1=ALU.add)
                mm.then_inc(s_ready, 1)

            def output(c):
                v.wait_ge(ro_ready, c + 1)
                out = OS[:].rearrange("p (h e) n -> p h e n", e=2)
                got = pair(4).rearrange("p (h e) n -> p h e n", e=2)
                for e in range(2):
                    mm = v.scalar_tensor_tensor(out=out[:, :, e, :], in0=got[:, :, e, :], scalar=gn[:, e:e + 1],
                                                in1=RO[:], op0=ALU.mult, op1=ALU.mult)
                mm.then_inc(o_scaled, 1)
                v.wait_ge(o_scaled, c + 1)
                gate = r.H[:, OR_:OR_ + 8, bass.ds(c * P, P)]
                v.tensor_tensor(gate, OS[:], gate, ALU.mult).then_inc(chunk_done, 1)

            def front(n, slot):
                sums(n)
                queries(n, slot)
                keys(n)
                factors(n, H4)
                sums(n + 1)
                attention(n, slot)

            def body(c, slot, more):
                queries(c + 1, 1 - slot)
                keys(c + 1)
                factors(c + 1, (0,))
                state(c, slot)
                factors(c + 1, (1,))
                output(c)
                factors(c + 1, (2, 3))
                if more:
                    sums(c + 2)
                attention(c + 1, 1 - slot)

            def back(c, slot):
                state(c, slot)
                output(c)

            run(v, body, front, back)


def sample_state_phase(nc, r, delta):
    E = 1 if delta else 2
    tag = "ds_" if delta else "gs_"
    Qc, Kc, Vc, Oc = (Q_A, K_A, V_A, GATE_A) if delta else (OQ, OK, OV, OR_)
    state_in = r.state_delta_S[0] if delta else r.state_gla_S[0]
    state_out = r.o_dS_s[0] if delta else r.o_gS_s[0]
    q, k = r.H[:, Qc:Qc + 4, T:N], r.H[:, Kc:Kc + 4, T:N]
    val, gate = r.H[:, Vc:Vc + 4 * E, T:N], r.H[:, Oc:Oc + 4 * E, T:N]
    with phase(nc) as ctx:
        def sb(name, shape):
            return ctx.enter_context(nc.sbuf_tensor(tag + name, shape, F32))

        S = sb("s", [P, NS, 4, E * P])
        tmp = r.H[:, Kc:Kc + 2, 0:4 * E * P].rearrange("p u (h e) -> p u h e", h=4)
        pick, ng = sb("pick", [NS, NS, P]), sb("ng", [P, E])
        qn, kn, dec, kw, prod, qk = [sb(n, [P, 4, NS]) for n in ("qn", "kn", "dec", "kw", "prod", "qk")]
        sq, rn = sb("sq", [P, 8, NS]), sb("rn", [P, 8, NS])
        vn, o, os_ = sb("vn", [P, 4 * E, NS]), sb("o", [P, 4 * E, NS]), sb("os", [P, 4 * E, NS])
        vrow = r.H[0:NS, Kc + 2, 0:4 * E * P]
        ro = sb("ro", [P, 4, NS])
        rowsel = sb("rowsel", [NSMALL, 8, P]) if delta else None
        bb = sb("bb", [P, 8, NS])
        s_in = [nc.alloc_semaphore(tag + f"s_in{i}") for i in range(NS)]
        tables_in, act_step, dve_step, pe_step, spread, outer, moved, stored = [
            nc.alloc_semaphore(tag + s) for s in
            ("tables_in", "act_step", "dve_step", "pe_step", "spread", "outer", "moved", "stored")]
        block = ctx.enter_context(nc.Block())
        nt = 3 if delta else 2

        def small(b, n):
            return r.ps[:, b, 0:n * NS].rearrange("p (h s) -> p h s", s=NS)

        @block.sync
        def _(sp):
            sp.dma_start(pick[:].rearrange("p s n -> p (s n)"), r.c_pick).then_inc(tables_in, 16)
            sp.dma_start(ng[:], r.delta_ng if delta else r.gla_ng).then_inc(tables_in, 16)
            if delta:
                sp.dma_start(rowsel[:].rearrange("p l n -> p (l n)"), r.c_rowsel).then_inc(tables_in, 16)
            for s in range(NS):
                sp.dma_start(S[:, s], state_in[s].rearrange("h d e -> d h e")).then_inc(s_in[s], 16)
            for s in range(NS):
                sp.wait_ge(moved, s + 1)
                sp.dma_start(state_out[s].rearrange("h d e -> d h e"), S[:, s]).then_inc(stored, 16)
            sp.wait_ge(stored, 16 * NS)

        @block.scalar
        def _(act):
            act.preload_act_table_set("natural_log_exp_and_others")
            act.wait_ge(tables_in, 16 * nt)
            if delta:
                act.activation(sq[:], r.H[:, Qc:Qc + 8, T:N], ACT.Square).then_inc(act_step, 1)
                act.wait_ge(pe_step, 1)
                act.activation(rn[:], small(0, 8), ACT.Ln, bias=r.bias[:, 1:2]).then_inc(act_step, 1)
                act.wait_ge(act_step, 2)
                act.activation(rn[:], rn[:], ACT.Exp, scale=-0.5)
                act.activation(dec[:], small(1, 8)[:, 4:8, :], ACT.Exp)
                act.copy(bb[:], small(1, 8)).then_inc(act_step, 1)
            else:
                act.activation(dec[:], r.LA[:, :, T:N], ACT.Exp).then_inc(act_step, 1)
                act.sem_inc(act_step, 2)
            act.wait_ge(pe_step, 4)
            for j in range(E):
                mm = act.copy(vrow[:, j * 512:(j + 1) * 512], r.ps[0:NS, 4 + j, :])
            mm.then_inc(act_step, 1)
            for s in range(NS):
                act.wait_ge(spread, s + 1)
                if s >= 2:
                    act.wait_ge(moved, s - 1)
                for h in range(4):
                    src = r.ps[:, s % 2 * 2:s % 2 * 2 + E, :].rearrange("p b n -> p (b n)")[:, h * E * P:(h + 1) * E * P]
                    mm = act.activation(tmp[:, s % 2, h, :], src, ACT.Copy, scale=kn[:, h, s:s + 1])
                mm.then_inc(outer, 1)
            act.wait_ge(dve_step, 6)
            act.activation(os_[:], o[:], ACT.Square).then_inc(act_step, 1)
            act.wait_ge(pe_step, 5)
            act.activation(ro[:], small(7, 4), ACT.Ln, bias=r.bias[:, 1:2], scale=1 / (E * P)).then_inc(act_step, 1)
            act.wait_ge(act_step, 6)
            act.activation(ro[:], ro[:], ACT.Exp, scale=-0.5).then_inc(act_step, 1)

        @block.vector
        def _(v):
            v.wait_ge(tables_in, 16 * nt)
            v.wait_ge(act_step, 3)
            if delta:
                v.scalar_tensor_tensor(out=qn[:], in0=q, scalar=128 ** -0.5, in1=rn[:, 0:4, :], op0=ALU.mult,
                                       op1=ALU.mult)
                v.tensor_tensor(kn[:], k, rn[:, 4:8, :], ALU.mult).then_inc(dve_step, 1)
                v.wait_ge(dve_step, 1)
                v.tensor_tensor(prod[:], qn[:], kn[:], ALU.mult)
                v.tensor_tensor(kw[:], kn[:], dec[:], ALU.mult).then_inc(dve_step, 1)
                v.wait_ge(dve_step, 2)
                v.tensor_tensor(kw[:], kw[:], bb[:, 0:4, :], ALU.mult)
                v.tensor_tensor(qn[:], qn[:], dec[:], ALU.mult)
                v.tensor_tensor(vn[:], val, bb[:, 0:4, :], ALU.mult).then_inc(dve_step, 1)
            else:
                v.tensor_copy(kn[:], k)
                v.tensor_scalar(qn[:], q, 128 ** -0.5, None, ALU.mult).then_inc(dve_step, 1)
                v.wait_ge(dve_step, 1)
                v.tensor_tensor(prod[:], qn[:], k, ALU.mult).then_inc(dve_step, 1)
                v.wait_ge(dve_step, 2)
                v.tensor_tensor(qn[:], qn[:], dec[:], ALU.mult)
                v.tensor_copy(vn[:], val).then_inc(dve_step, 1)
            v.wait_ge(pe_step, 2)
            mm = v.tensor_copy(qk[:], small(6, 4))
            if delta:
                mm = v.tensor_tensor(vn[:], vn[:], small(2, 4), ALU.subtract)
            mm.then_inc(dve_step, 1)
            v.wait_ge(dve_step, 4)
            v.wait_ge(pe_step, 3)
            v.tensor_tensor(o[:].rearrange("p (h e) s -> p h e s", e=E), vn[:].rearrange("p (h e) s -> p h e s", e=E),
                            qk[:].unsqueeze(2).to_broadcast([P, 4, E, NS]), ALU.mult).then_inc(dve_step, 1)
            v.wait_ge(dve_step, 5)
            v.tensor_tensor(o[:], o[:], small(3, 4 * E), ALU.add).then_inc(dve_step, 1)
            for s in range(NS):
                v.wait_ge(outer, s + 1)
                for h in range(4):
                    mm = v.scalar_tensor_tensor(out=S[:, s, h, :], in0=S[:, s, h, :], scalar=dec[:, h, s:s + 1],
                                                in1=tmp[:, s % 2, h, :], op0=ALU.mult, op1=ALU.add)
                mm.then_inc(moved, 1)
            v.wait_ge(act_step, 7)
            ov = o[:].rearrange("p (h e) s -> p h e s", e=E)
            for e in range(E):
                mm = v.scalar_tensor_tensor(out=ov[:, :, e, :], in0=ov[:, :, e, :], scalar=ng[:, e:e + 1], in1=ro[:],
                                            op0=ALU.mult, op1=ALU.mult)
            mm.then_inc(dve_step, 1)
            v.wait_ge(dve_step, 7)
            v.tensor_tensor(gate, gate, o[:], ALU.mult)

        @block.tensor
        def _(pe):
            pe.wait_ge(tables_in, 16 * nt)
            if delta:
                pe.wait_ge(act_step, 1)
                pe.matmul(r.ps[:, 0, 0:8 * NS], r.ones[:], sq[:], start=True, stop=True)
                for j in range(8):
                    mm = pe.matmul(small(1, 8)[:, j, :], rowsel[:, j, :], r.H[0:NSMALL, SMALL, T:N], start=True,
                                   stop=True)
                mm.then_inc(pe_step, 1)
            else:
                pe.sem_inc(pe_step, 1)
            pe.wait_ge(dve_step, 3)
            pe.matmul(r.ps[:, 6, 0:4 * NS], r.ones[:], prod[:], start=True, stop=True)
            for s in range(NS):
                pe.wait_ge(s_in[s], 16)
                if delta:
                    for h in range(4):
                        pe.matmul(small(2, 4)[:, h, s:s + 1], S[:, s, h, :], kw[:, h, s:s + 1], start=True, stop=True)
            pe.matmul(r.ps[:, 7, 0:4 * NS], r.ones[:], prod[:], start=True, stop=True).then_inc(pe_step, 1)
            for s in range(NS):
                for h in range(4):
                    for e in range(E):
                        mm = pe.matmul(small(3, 4 * E)[:, h * E + e, s:s + 1], S[:, s, h, e * P:(e + 1) * P],
                                       qn[:, h, s:s + 1], start=True, stop=True)
            mm.then_inc(pe_step, 1)
            pe.wait_ge(dve_step, 4)
            for j in range(4 * E):
                mm = pe.transpose(r.ps[0:NS, 4 + j // 4, j % 4 * P:(j % 4 + 1) * P], vn[:, j, :], r.ident[:])
            mm.then_inc(pe_step, 1)
            pe.wait_ge(act_step, 4)
            pe.wait_ge(dve_step, 6)
            for s in range(NS):
                if s >= 2:
                    pe.wait_ge(outer, s - 1)
                for j in range(E):
                    mm = pe.matmul(r.ps[:, s % 2 * 2 + j, :], pick[:, s, :], vrow[:, j * 512:(j + 1) * 512],
                                   start=True, stop=True)
                mm.then_inc(spread, 1)
            pe.wait_ge(act_step, 5)
            if delta:
                pe.matmul(r.ps[:, 7, 0:4 * NS], r.ones[:], os_[:], start=True, stop=True).then_inc(pe_step, 1)
            else:
                ov = os_[:].rearrange("p (h e) s -> p h e s", e=2)
                pe.matmul(r.ps[:, 7, 0:4 * NS], r.ones[:], ov[:, :, 0, :], start=True, stop=False)
                pe.matmul(r.ps[:, 7, 0:4 * NS], r.ones[:], ov[:, :, 1, :], start=False,
                          stop=True).then_inc(pe_step, 1)


def nsa_sample_phase(nc, r):
    flat = r.H[:].rearrange("p k n -> p (k n)")
    R = 64
    cache = r.cache.rearrange("n e t c g d -> (n e) t (c g d)")
    n_pool = r.cache.shape[0]
    win = r.state_nsa_win[0].rearrange("b (j p) c g d -> b p j c (g d)", p=P)
    at = [0]

    def room(rows, n):
        at[0] += n
        assert at[0] <= 12 * N
        return flat[0:rows, at[0] - n:at[0]]

    PAST = PAGES * P
    SW = room(R, 513)
    PT = room(P, 37 * R).rearrange("p (n q) -> p n q", q=R)
    VC = room(P, NS * P).rearrange("p (s n) -> p s n", s=NS)
    with phase(nc) as ctx:
        def sb(name, shape, dt=F32):
            return ctx.enter_context(nc.sbuf_tensor("ns_" + name, shape, dt))

        sw = Sweep(r, sb("kp_last", [P, PGRP, 384])[:])
        KP, KT, KC, VCT, Qs, SC, pages = sw.KP, sw.KT, sw.KC, sw.VCT, sw.Qs, sw.SC, sw.pages
        VP = sb("vp", [P, NG + 1, PGRP, P])
        group, own, headrow = sb("group", [R, R]), sb("own", [NS, R]), sb("headrow", [R, 8])
        PC, G24, gates = sb("pc", [R, P]), sb("g24", [R, 8, 3]), sb("gates", [R, 3])
        pick, top8, mask = sb("pick", [R, 72]), sb("top8", [R, 8]), sb("mask", [R, 64])
        top, ntop, den, coef = sb("top", [R, 3]), sb("ntop", [R, 3]), sb("den", [R, 3]), sb("coef", [R, 3])
        pn, diag = sb("pn", [NS, 2, R]), sb("diag", [R, 2, R])
        O = sb("o", [P, R])
        tables_in, k_turned, kt_kept, kt_used, sc_kept = [
            nc.alloc_semaphore("ns_" + s) for s in ("tables_in", "k_turned", "kt_kept", "kt_used", "sc_kept")]
        kp_in = [nc.alloc_semaphore(f"ns_kp_in{u}") for u in range(4)]
        vp_in = [nc.alloc_semaphore(f"ns_vp_in{u}") for u in range(NG + 1)]
        vp_in2 = [nc.alloc_semaphore(f"ns_vp_in2_{u}") for u in range(NG)]
        vp_in3 = [nc.alloc_semaphore(f"ns_vp_in3_{u}") for u in range(NG)]
        pe_step, dve_step, act_step, pt_turned, pt_kept, vp_used, o_ready = [
            nc.alloc_semaphore("ns_" + s) for s in
            ("pe_step", "dve_step", "act_step", "pt_turned", "pt_kept", "vp_used", "o_ready")]
        block = ctx.enter_context(nc.Block())

        def mine(which, g):
            return (which, 3) if g % 3 == which else (which,)

        def fetch(eng, first, end, which, vp_in):
            def page(index):
                return eng.value_load(pages[0:1, bass.ds(index, 1)], min_val=0, max_val=n_pool - 1)

            with eng.Fori(first, end) as s:
                for g in range(NG):
                    eng.wait_ge(vp_used, s * (NG + 1) + (g + 1))
                    for j in mine(which, g):
                        eng.dma_start(VP[:, g, j, :],
                                      cache[bass.ds(page(s * PAGES + (g * PGRP + j)), 1), :, 384:512].squeeze(0)
                                      ).then_inc(vp_in[g], 16)
                if which == 0:
                    eng.wait_ge(vp_used, s * (NG + 1) + (NG + 1))
                    eng.dma_start(VP[:, NG, :, :], win[bass.ds(s, 1), :, :, 1, :].squeeze(0)).then_inc(vp_in[NG], 16)

        @block.sync
        def _(sp):
            for s in range(4):
                sp.dma_start(KP[s][:, :, 256:384], win[s, :, :, 0, :]).then_inc(kp_in[s], 16)
            for dst, src in ((group[:], r.c_group), (own[:], r.c_own), (headrow[:], r.c_headrow)):
                sp.dma_start(dst, src).then_inc(tables_in, 16)
            for s in range(4, NS):
                sp.wait_ge(k_turned, s - 3)
                sp.dma_start(KP[s % 4][:, :, 256:384], win[s, :, :, 0, :]).then_inc(kp_in[s % 4], 16)
            fetch(sp, 0, NS, 0, vp_in)

        @block.gpsimd
        def _(pool_):
            fetch(pool_, 0, NS, 2, vp_in2)

        @block.tensor
        def _(pe):
            pe.sem_inc(vp_used, NG + 1)

            def turn(s):
                pe.wait_ge(kp_in[s % 4], (s // 4 + 1) * 16)
                if s >= 2:
                    pe.wait_ge(kt_kept, s - 1)
                for j in range(PGRP):
                    mm = pe.transpose(r.ps[:, s % 2, j * P:(j + 1) * P], KP[s % 4][:, j, 256:384], r.ident[:])
                mm.then_inc(k_turned, 1)

            turn(0)
            for s in range(NS):
                if s + 1 < NS:
                    turn(s + 1)
                pe.wait_ge(kt_kept, s + 1)
                pe.matmul(r.ps[0:R, 2, :], Qs[:, s, :], KT[:, s % 2, :], start=(s == 0),
                          stop=(s == NS - 1)).then_inc(kt_used, 1)
            pe.wait_ge(tables_in, 48)
            for s in range(NS):
                pe.matmul(r.ps[0:R, 3, 0:1], Qs[:, s, :], r.H[:, K_SEL, T + s:T + s + 1], start=(s == 0),
                          stop=(s == NS - 1))
            for s in range(NS):
                pe.matmul(r.ps[0:R, 3, 1:2], Qs[:, s, :], r.H[:, K_WIN, T + s:T + s + 1], start=(s == 0),
                          stop=(s == NS - 1))
            for s in range(NS):
                pe.matmul(r.ps[0:R, 3, P:2 * P], Qs[:, s, :], KC[:, s, :], start=(s == 0), stop=(s == NS - 1))
            pe.matmul(r.ps[0:R, 3, 32:56], own[:], r.tok[0:NS, 8, R_NSA:R_NSA + 24], start=True,
                      stop=True).then_inc(pe_step, 1)
            for s in range(NS):
                mm = pe.transpose(r.ps[:, s // 4, s % 4 * P:(s % 4 + 1) * P], VCT[:, s, :], r.ident[:])
            mm.then_inc(pe_step, 1)
            pe.wait_ge(dve_step, 4)
            pe.matmul(r.ps[0:R, 4, 0:P], group[:], PC[:], start=True, stop=True).then_inc(pe_step, 1)
            pe.wait_ge(dve_step, 15)
            for j in range(2):
                mm = pe.matmul(r.ps[0:NS, 4, 256 + R * j:256 + R * (j + 1)], r.ones[0:R, 0:NS], diag[:, j, :],
                               start=True, stop=True)
            mm.then_inc(pe_step, 1)
            pe.wait_ge(act_step, 3)
            for b in range(5):
                if b >= 2:
                    pe.wait_ge(pt_kept, b - 1)
                for n in range(8 * b, min(8 * b + 8, 37)):
                    src = SC[:, n * P:(n + 1) * P] if n < 32 else SW[:, (n - 32) * P:(n - 31) * P] if n < 36 else PC[:]
                    mm = pe.transpose(r.ps[:, b % 2, n % 8 * R:(n % 8 + 1) * R], src, r.ident[0:R, 0:R])
                mm.then_inc(pt_turned, 1)
            pe.wait_ge(pt_kept, 5)
            for s in range(NS):
                pe.matmul(r.ps[:, 7, s * 8:s * 8 + 8], VC[:, s, :], PT[:, 36, s * 8:s * 8 + 8], start=True, stop=True)
            pe.wait_ge(dve_step, 16)
            pe.matmul(r.ps[:, 5, 0:R], r.srows[0:NS, 384:512], pn[:, 0, :], start=True, stop=False)
            pe.matmul(r.ps[:, 5, 0:R], r.srows[0:NS, 640:768], pn[:, 1, :], start=False, stop=True)
            with pe.Fori(0, NS) as s:
                for g in range(NG + 1):
                    if g == NG:
                        pe.wait_ge(vp_in[g], s * 16 + 16)
                    else:
                        for which, pages_of in enumerate((vp_in, vp_in3, vp_in2)):
                            n = 16 * len(mine(which, g))
                            pe.wait_ge(pages_of[g], s * n + n)
                    for j in range(PGRP):
                        mm = pe.matmul(r.ps[:, 6, bass.ds(s * 8, 8)], VP[:, g, j, :],
                                       PT[:, 4 * g + j, bass.ds(s * 8, 8)], start=(g == 0 and j == 0),
                                       stop=(g == NG and j == PGRP - 1))
                    mm.then_inc(vp_used, 1)

        @block.scalar
        def _(act):
            fetch(act, 0, 1, 1, vp_in3)
            for s in range(NS):
                act.wait_ge(k_turned, s + 1)
                if s >= 2:
                    act.wait_ge(kt_used, s - 1)
                act.copy(KT[:, s % 2, :], r.ps[:, s % 2, :]).then_inc(kt_kept, 1)
            act.wait_ge(dve_step, 2)
            act.activation(PC[:], r.ps[0:R, 3, P:2 * P], ACT.Exp, bias=ntop[:, 0:1], scale=0.125,
                           accum_out=den[:, 0:1]).then_inc(act_step, 1)
            act.wait_ge(pe_step, 2)
            act.copy(VC[:, 0:4, :].rearrange("p s n -> p (s n)"), r.ps[:, 0, :])
            act.copy(VC[:, 4:8, :].rearrange("p s n -> p (s n)"), r.ps[:, 1, :]).then_inc(act_step, 1)
            act.wait_ge(dve_step, 12)
            act.activation(SC, SC, ACT.Exp, bias=ntop[:, 1:2], scale=0.125, accum_out=den[:, 1:2])
            act.activation(SW[:], SW[:], ACT.Exp, bias=ntop[:, 2:3], scale=0.125,
                           accum_out=den[:, 2:3]).then_inc(act_step, 1)
            for b in range(5):
                n = min(8, 37 - 8 * b)
                act.wait_ge(pt_turned, b + 1)
                act.copy(PT[:, 8 * b:8 * b + n, :].rearrange("p n q -> p (n q)"),
                         r.ps[:, b % 2, 0:n * R]).then_inc(pt_kept, 1)
            fetch(act, 1, NS, 1, vp_in3)

        @block.vector
        def _(v):
            v.sem_inc(dve_step, 1)
            v.wait_ge(kt_used, NS)
            v.tensor_copy(SW[:, 0:512], r.ps[0:R, 2, :]).then_inc(sc_kept, 1)
            v.wait_ge(pe_step, 1)
            v.wait_ge(sc_kept, 1)
            v.memset(SW[:, 0:1], NEG)
            v.tensor_copy(SC[:, PAST:PAST + 1], r.ps[0:R, 3, 0:1])
            v.tensor_copy(SW[:, 512:513], r.ps[0:R, 3, 1:2])
            v.tensor_tensor(G24[:], r.ps[0:R, 3, 32:56].rearrange("p (h b) -> p h b", b=3),
                            headrow[:].unsqueeze(2).to_broadcast([R, 8, 3]), ALU.mult)
            v.tensor_reduce(top[:, 0:1], r.ps[0:R, 3, P:2 * P], AX.X, ALU.max).then_inc(sc_kept, 1)
            v.wait_ge(sc_kept, 2)
            v.tensor_reduce(gates[:], G24[:].rearrange("p h b -> p b h"), AX.X, ALU.add)
            v.tensor_reduce(top[:, 2:3], SW[:], AX.X, ALU.max)
            v.tensor_scalar(ntop[:, 0:1], top[:, 0:1], -0.125, None, ALU.mult).then_inc(dve_step, 1)
            v.wait_ge(act_step, 1)
            v.reciprocal(coef[:, 0:1], den[:, 0:1]).then_inc(dve_step, 1)
            v.wait_ge(dve_step, 3)
            v.tensor_scalar(PC[:], PC[:], coef[:, 0:1], None, ALU.mult).then_inc(dve_step, 1)
            v.memset(pick[:], NEG).then_inc(dve_step, 1)
            v.wait_ge(dve_step, 5)
            v.wait_ge(pe_step, 3)
            v.tensor_scalar(PC[:], PC[:], gates[:, 0:1], None, ALU.mult)
            v.tensor_reduce(pick[:, 0:64], r.ps[0:R, 4, 0:P].rearrange("p (b c) -> p b c", c=2), AX.X,
                            ALU.add).then_inc(dve_step, 1)
            v.wait_ge(dve_step, 6)
            v.memset(pick[:, 0:1], 1e9)
            v.memset(pick[:, 63:65], 1e9).then_inc(dve_step, 1)
            v.wait_ge(dve_step, 7)
            for n in range(2):
                v.max(top8[:], pick[:]).then_inc(dve_step, 1)
                v.wait_ge(dve_step, 8 + 2 * n)
                v.match_replace(pick[:], top8[:], pick[:], -3e38).then_inc(dve_step, 1)
                v.wait_ge(dve_step, 9 + 2 * n)
            v.tensor_scalar(mask[:], pick[:, 0:64], -2e38, NEG, ALU.is_gt, ALU.mult).then_inc(sc_kept, 1)
            v.wait_ge(sc_kept, 3)
            sv = SC[:, 0:PAST].rearrange("p (b n) -> p b n", n=64)
            v.tensor_tensor(sv, sv, mask[:].unsqueeze(2).to_broadcast([R, 64, 64]), ALU.add).then_inc(sc_kept, 1)
            v.wait_ge(sc_kept, 4)
            v.tensor_reduce(top[:, 1:2], SC, AX.X, ALU.max).then_inc(sc_kept, 1)
            v.wait_ge(sc_kept, 5)
            v.tensor_scalar(ntop[:, 1:3], top[:, 1:3], -0.125, None, ALU.mult).then_inc(dve_step, 1)
            v.wait_ge(act_step, 3)
            v.reciprocal(coef[:, 1:3], den[:, 1:3]).then_inc(dve_step, 1)
            v.wait_ge(dve_step, 13)
            v.tensor_tensor(coef[:, 1:3], coef[:, 1:3], gates[:, 1:3], ALU.mult).then_inc(dve_step, 1)
            v.wait_ge(dve_step, 14)
            v.tensor_scalar(SC, SC, coef[:, 1:2], None, ALU.mult)
            v.tensor_scalar(SW[:], SW[:], coef[:, 2:3], None, ALU.mult).then_inc(sc_kept, 1)
            v.wait_ge(sc_kept, 6)
            v.tensor_scalar(diag[:, 0, :], r.ident[0:R, 0:R], SC[:, PAST:PAST + 1], None, ALU.mult)
            v.tensor_scalar(diag[:, 1, :], r.ident[0:R, 0:R], SW[:, 512:513], None,
                            ALU.mult).then_inc(dve_step, 1)
            v.wait_ge(pe_step, 4)
            v.tensor_tensor(pn[:], r.ps[0:NS, 4, 256:256 + 2 * R].rearrange("p (j q) -> p j q", j=2),
                            own[:].unsqueeze(1).to_broadcast([NS, 2, R]), ALU.mult).then_inc(dve_step, 1)
            v.wait_ge(vp_used, (NG + 1) * (NS + 1))
            v.tensor_copy(O[:], r.ps[:, 6, 0:R]).then_inc(dve_step, 1)
            v.wait_ge(dve_step, 17)
            v.tensor_tensor(O[:], O[:], r.ps[:, 7, 0:R], ALU.add).then_inc(dve_step, 1)
            v.wait_ge(dve_step, 18)
            v.tensor_tensor(O[:], O[:], r.ps[:, 5, 0:R], ALU.add).then_inc(dve_step, 1)
            v.wait_ge(dve_step, 19)
            for g in range(2):
                v.tensor_copy(r.H[64 * g:64 * g + 64, Q_B:Q_B + 4, T:N],
                              O[64 * g:64 * g + 64, :].rearrange("p (s h) -> p h s", h=8)[:, 4 * g:4 * g + 4, :])



def build(nc, a, outs):
    r = Res()
    (r.o_y_p, r.o_y_s, r.o_rows_p, r.o_win_p, r.o_conv_p, r.o_dS_p, r.o_gS_p, r.o_rows_s, r.o_win_s, r.o_conv_s,
     r.o_dS_s, r.o_gS_s) = outs
    r.x_prompt, r.x_sample = a["x_prompt"], a["x_sample"]
    r.cache, r.state_nsa_win, r.state_delta_conv = a["cache_nsa_kv"], a["state_nsa_win"], a["state_delta_conv"]
    r.state_delta_S, r.state_gla_S, r.page_table = a["state_delta_S"], a["state_gla_S"], a["page_table"]
    r.dt_bias, r.A_log = a["delta_dt_bias"], a["delta_A_log"]
    r.conv_w, r.delta_ng = a["conv_w_delta"], a["delta_norm_g"]
    r.c_causal, r.c_oldest, r.c_cmp_add, r.c_cmp_one = a["c_causal"], a["c_oldest"], a["c_cmp_add"], a["c_cmp_one"]
    r.c_level, r.c_upper, r.c_rowsel = a["c_level"], a["c_upper"], a["c_rowsel"]
    r.c_pick, r.gla_ng, r.b_g2, r.w_g2 = a["c_pick"], a["gla_norm_g"], a["b_gla_gate2"], a["w_gla_gate2"][0]
    r.c_pool, r.c_group, r.c_own, r.c_headrow = a["c_pool"], a["c_group"], a["c_own"], a["c_headrow"]
    r.x_spilled = nc.dram_tensor("x_spilled", [P, KD, N], F32, kind="Internal").ap()
    r.w_ffn_gate, r.w_ffn_up = a["w_ffn_gate"], a["w_ffn_up"]
    with ExitStack() as ctx:
        def sb(name, shape, dt=F32):
            return ctx.enter_context(nc.sbuf_tensor(name, shape, dt))

        r.X, r.Xh = ctx.enter_context(twin(nc, "X", [P, KD, N]))
        r.ps = ctx.enter_context(nc.psum_tensor("ps", [P, 8, 512], F32))
        r.ident = sb("ident", [P, P])
        r.ones, r.ones_d = sb("ones", [P, P]), sb("ones_d", [P, P])
        r.bias = sb("bias", [P, 2])
        r.lng, r.lnb = sb("lng", [P, 4 * KD]), sb("lnb", [P, 4 * KD])
        r.const_loads = [(r.ident[:], a["c_ident"]),
                         (r.lng[:], a["ln_g"]),
                         (r.lnb[:], a["ln_b"])]
        def low(tag):
            return nc.sbuf_tensor("Xl_" + tag, [P, KD, N], F32R)

        def view(w):
            return w.rearrange("(k p) n -> p k n", p=P)

        def whole(w):
            half = w.shape[1] // 2
            return lambda m, u, shift: [
                ((slice(None), slice(s, s + half), slice(None)), w[:, s:s + half, bass.ds(m * P + shift, P)])
                for s in (0, half)]

        w_even = view(a["w_in_even"][0])

        def load_even(m, u, shift):
            if shift is None:
                c0 = 2056 + 64 * (m - 16)
                return [((slice(None), slice(None), slice(64 * g, 64 * g + 64)),
                         w_even[:, :, c0 + 256 * g:c0 + 256 * g + 64]) for g in range(2)]
            return whole(w_even)(m, u, shift)

        even_chunks = [(0, 12, 0), (12, 16, 8), (16, 20, None), (20, 26, 8)]
        every = slice(None)
        even_small = [((every, every, slice(R_BETA, R_BETA + 4)), w_even[:, :, 1536:1540]),
                      ((every, every, slice(R_G, R_G + 4)), w_even[:, :, 1540:1544]),
                      ((every, every, slice(R_NSA, R_NSA + 24)), w_even[:, :, 3336:3360])]
        with ExitStack() as even:
            r.H, r.Hlo = even.enter_context(twin(nc, "H0", [P, 27, N], (GATE_A, GATE_A + 8)))
            with low("in_even") as r.Xl, ExitStack() as stack:
                ring = Ring(nc, stack, "in_even", KD, lambda u: load_even(u, u, 0))
                load_phase(nc, r, ring)
                project_split_phase(nc, r, "in_even", even_chunks, load_even, r.H, even_small, ring)
            r.tok = even.enter_context(nc.sbuf_tensor("tok", [P, 9, NSMALL], F32))
            r.bufT = even.enter_context(nc.sbuf_tensor("bufT", [P, 12, 24], F32))
            r.srows = even.enter_context(nc.sbuf_tensor("srows", [NS, 768], F32))
            with nc.sbuf_tensor("rows", [P, TT, 768], F32) as rows:
                r.rows = rows
                even_rows_phase(nc, r)
                gates_phase(nc, r)
                nsa_prompt_phase(nc, r)
            silu_phase(nc, r)
            delta_prompt_phase(nc, r)
            sample_state_phase(nc, r, True)
            nsa_sample_phase(nc, r)
            w_out = view(a["w_out_even"][0])

            def load_out_even(part, m):
                cols = bass.ds(m * P, P)
                tail = a["w_out_even"][0, 512:1024].rearrange("(g i p) n -> g p i n", g=2, p=64)
                return [((every, slice(0, 4), every), w_out[:, 0:4, cols]),
                        ((slice(0, 64), slice(4, 8), every), tail[0][:, :, cols]),
                        ((slice(64, 128), slice(4, 8), every), tail[1][:, :, cols])]

            residual_phase(nc, r, "out_even", r.H[:, GATE_A:GATE_A + 8, :], r.Hlo[:], 1,
                           load_out_even, reload=True)

        def ffn(layer):
            w_down = view(a["w_ffn_down"][layer])

            def load_down(part, m):
                half = KF // 2
                return [((every, every, every), w_down[:, part * half:part * half + half, bass.ds(m * P, P)])]

            with twin(nc, f"F{layer}", [P, KF, N]) as (r.F, r.Flo):
                with low(f"ffn{layer}") as r.Xl, ExitStack() as stack:
                    ring = Ring(nc, stack, f"up{layer}", 2 * KD, up_weights(r, layer))
                    norm_phase(nc, r, layer, 0, r.F[:], ring)
                    ffn_up_phase(nc, r, layer, ring)
                residual_phase(nc, r, f"down{layer}", r.F[:], r.Flo[:], 2, load_down)

        ffn(0)
        w_odd = view(a["w_in_odd"][0])
        with twin(nc, "H1", [P, 25, N], (OR_, OR_ + 8)) as (r.H, r.Hlo):
            with low("in_odd") as r.Xl, ExitStack() as stack:
                load_odd = whole(w_odd)
                ring = Ring(nc, stack, "in_odd", KD, lambda u: load_odd(u, u, 0))
                norm_phase(nc, r, 0, 1, r.H[:], ring)
                project_split_phase(nc, r, "in_odd", [(0, 16, 0), (16, 24, 16)], load_odd, r.H,
                                    [((every, every, slice(0, 16)), w_odd[:, :, 2048:2064])], ring)
            with nc.sbuf_tensor("LA", [P, 4, N], F32) as r.LA:
                gla_gate_phase(nc, r)
                gla_prompt_phase(nc, r)
                sample_state_phase(nc, r, False)
            residual_phase(nc, r, "out_odd", r.H[:, OR_:OR_ + 8, :], r.Hlo[:], 1,
                           lambda part, m: whole(view(a["w_out_odd"][0]))(m, 0, 0))
        ffn(1)
        with nc.sbuf_tensor("squares", [P, 6, N], F32) as squares:
            norm_phase(nc, r, 1, 1, squares[:])
        store_phase(nc, r)


_INS = ["x_prompt", "x_sample", "cache_nsa_kv", "state_nsa_win", "state_delta_conv", "state_delta_S", "state_gla_S",
        "page_table", "w_in_even", "conv_w_delta", "delta_A_log", "delta_dt_bias", "delta_norm_g", "w_out_even",
        "w_in_odd", "w_gla_gate2", "b_gla_gate2", "gla_norm_g", "w_out_odd", "w_ffn_gate", "w_ffn_up", "w_ffn_down",
        "ln_g", "ln_b"]
_OUTS = [(1, T, D), (NS, 1, D), (1, 1, T, 4, 2, 64), (1, 1, 512, 2, 2, 64), (1, 1, 3, 1536), (1, 1, 4, 128, 128),
         (1, 1, 4, 128, 256), (1, NS, 1, 4, 2, 64), (1, NS, 512, 2, 2, 64), (1, NS, 3, 1536), (1, NS, 4, 128, 128),
         (1, NS, 4, 128, 256)]


def per_partition(v):
    v = np.asarray(v)
    return v.reshape(-1, P).T


def kernel(**inputs):
    import concourse.bacc as bacc
    from concourse.bass_utils import run_bass_kernel_spmd

    nc = bacc.Bacc("TRN2", target_bir_lowering=False, num_devices=1)
    arrays, aps = {}, {}
    for name in ("ln_g", "ln_b", "conv_w_delta", "delta_norm_g", "gla_norm_g", "b_gla_gate2"):
        inputs[name] = per_partition(inputs[name])
    for name in ("delta_A_log", "delta_dt_bias"):
        inputs[name] = np.asarray(inputs[name]).T
    for name, arr in [(n, inputs[n]) for n in _INS] + list(constants().items()):
        arr = np.ascontiguousarray(arr)
        arrays["in_" + name] = arr
        aps[name] = nc.dram_tensor("in_" + name, arr.shape, mybir.dt.from_np(arr.dtype), kind="ExternalInput").ap()
    outs = [nc.dram_tensor(f"out_{i}", shape, F32, kind="ExternalOutput").ap() for i, shape in enumerate(_OUTS)]
    build(nc, aps, outs)
    result = run_bass_kernel_spmd(nc, [arrays], core_ids=[0])
    return tuple(result.results[0][f"out_{i}"] for i in range(len(_OUTS)))
```
